# Optimizing a Trainium2 kernel written in Bass

```python
import jax, jax.numpy as jnp
from jax import lax
import numpy as np

D_MODEL = 1024
BATCH = 1
SEQ = 512
DEPTH = 2
DEC_BATCH = 1
DEC_SEQ = 1024
PAST_LEN = 128

GRID_W = 64
BLOCK = 128
HEAD_DIM = 64
CONV_DIM = D_MODEL // 2
CONV_WIDTH = 31
WIN_HEADS = (D_MODEL // 2) // HEAD_DIM
WIN_KV_HEADS = 2
WINDOW = 128
ROT_DIM_B = HEAD_DIM // 4
ROPE_THETA_B = 500000.0
AX_HEADS = D_MODEL // HEAD_DIM
AX_KV_HEADS = 4
ROPE_THETA_C = 10000.0
N_EXPERTS = 16
D_EXPERT = D_MODEL
CAPACITY_FACTOR = 2
ALPHA = (2 * DEPTH) ** 0.25
BETA = (8 * DEPTH) ** -0.25
N_EVEN = (DEPTH + 1) // 2
N_ODD = DEPTH // 2
AB_Q = WIN_HEADS * HEAD_DIM
AB_KV = WIN_KV_HEADS * HEAD_DIM
AB_IN = 2 * CONV_DIM + AB_Q + 2 * AB_KV
C_Q = AX_HEADS * HEAD_DIM
C_KV = AX_KV_HEADS * HEAD_DIM
C_IN = C_Q + 2 * C_KV
LN_EPS = 1e-5
RMS_EPS = 1e-6

kernel_name = 'hybrid_conv_window_axial_ec_encoder'

def layer_norm(x, g, b):
    xf = x.astype(jnp.float32)
    mu = jnp.mean(xf, -1, keepdims=True)
    var = jnp.mean(jnp.square(xf - mu), -1, keepdims=True)
    return ((xf - mu) * lax.rsqrt(var + LN_EPS)).astype(x.dtype) * g + b

def rms_norm(x, g):
    xf = x.astype(jnp.float32)
    return (xf * lax.rsqrt(jnp.mean(xf * xf, -1, keepdims=True) + RMS_EPS)).astype(x.dtype) * g

def rope_angles(pos, dim, theta):
    inv = theta ** (-jnp.arange(0, dim, 2, dtype=jnp.float32) / dim)
    return pos[:, None] * inv[None, :]

def apply_rope(x, ang):
    half = x.shape[-1] // 2
    cos = jnp.cos(ang)[None, :, None, :].astype(x.dtype)
    sin = jnp.sin(ang)[None, :, None, :].astype(x.dtype)
    x1, x2 = x[..., :half], x[..., half:]
    return jnp.concatenate([x1 * cos - x2 * sin, x2 * cos + x1 * sin], axis=-1)

def conv_branch(u, gate, w, b, g, beta):
    h = u * jax.nn.sigmoid(gate)
    pad = CONV_WIDTH // 2
    h = lax.conv_general_dilated(h, w[:, None, :].astype(h.dtype), window_strides=(1,),
                                 padding=[(pad, pad)], dimension_numbers=('NWC', 'WIO', 'NWC'),
                                 feature_group_count=CONV_DIM) + b
    return jax.nn.silu(layer_norm(h, g, beta))

def window_attention(q, k, v, sink):
    B, S, H, Dh = q.shape
    KV = k.shape[2]
    G = H // KV
    nb = S // BLOCK
    qb = q.reshape(B, nb, BLOCK, KV, G, Dh)

    def band(t):
        tp = jnp.pad(t, ((0, 0), (BLOCK, BLOCK), (0, 0), (0, 0))).reshape(B, nb + 2, BLOCK, KV, Dh)
        return jnp.concatenate([tp[:, :-2], tp[:, 1:-1], tp[:, 2:]], axis=2)

    kb, vb = band(k), band(v)
    s = jnp.einsum('bnqkgd,bnskd->bnkgqs', qb, kb).astype(jnp.float32) * (Dh ** -0.5)
    blk = jnp.arange(nb)[:, None, None] * BLOCK
    qpos = blk + jnp.arange(BLOCK)[None, :, None]
    kpos = blk - BLOCK + jnp.arange(3 * BLOCK)[None, None, :]
    mask = (jnp.abs(kpos - qpos) <= WINDOW) & (kpos >= 0) & (kpos < S)
    s = jnp.where(mask[None, :, None, None], s, -jnp.inf)
    sk = sink.astype(jnp.float32).reshape(KV, G)[None, None, :, :, None, None]
    m = jnp.maximum(jnp.max(s, -1, keepdims=True), sk)
    p = jnp.exp(s - m)
    p = (p / (jnp.sum(p, -1, keepdims=True) + jnp.exp(sk - m))).astype(v.dtype)
    o = jnp.einsum('bnkgqs,bnskd->bnqkgd', p, vb)
    return o.reshape(B, S, H * Dh)

def blocked_attention(q, k, v):
    B, S, H, Dh = q.shape
    KV = k.shape[2]
    G = H // KV
    nb = S // BLOCK
    qb = jnp.moveaxis(q.reshape(B, nb, BLOCK, KV, G, Dh), 1, 0)
    scale = Dh ** -0.5

    def attend(qi):
        s = jnp.einsum('bqkgd,bskd->bkgqs', qi, k).astype(jnp.float32) * scale
        p = jax.nn.softmax(s, axis=-1).astype(v.dtype)
        return jnp.einsum('bkgqs,bskd->bqkgd', p, v)

    o = lax.map(attend, qb)
    return jnp.moveaxis(o, 0, 1).reshape(B, S, H * Dh)

def mixer_conv_window(x, w_in, conv_w, conv_b, cln_g, cln_b, sink, w_out, ang):
    B, S, _ = x.shape
    h = x @ w_in
    u, gate, q, k, v = jnp.split(h, [CONV_DIM, 2 * CONV_DIM, 2 * CONV_DIM + AB_Q,
                                     2 * CONV_DIM + AB_Q + AB_KV], axis=-1)
    conv_out = conv_branch(u, gate, conv_w, conv_b, cln_g, cln_b)
    q = q.reshape(B, S, WIN_HEADS, HEAD_DIM)
    k = k.reshape(B, S, WIN_KV_HEADS, HEAD_DIM)
    v = v.reshape(B, S, WIN_KV_HEADS, HEAD_DIM)
    q = jnp.concatenate([apply_rope(q[..., :ROT_DIM_B], ang), q[..., ROT_DIM_B:]], axis=-1)
    k = jnp.concatenate([apply_rope(k[..., :ROT_DIM_B], ang), k[..., ROT_DIM_B:]], axis=-1)
    attn_out = window_attention(q, k, v, sink)
    return jnp.concatenate([conv_out, attn_out], axis=-1) @ w_out

def mixer_axial(x, w_in, q_norm, k_norm, w_out, ang_row, ang_col):
    B, S, _ = x.shape
    q, k, v = jnp.split(x @ w_in, [C_Q, C_Q + C_KV], axis=-1)
    q = rms_norm(q.reshape(B, S, AX_HEADS, HEAD_DIM), q_norm)
    k = rms_norm(k.reshape(B, S, AX_KV_HEADS, HEAD_DIM), k_norm)
    v = v.reshape(B, S, AX_KV_HEADS, HEAD_DIM)
    hd = HEAD_DIM // 2
    q = jnp.concatenate([apply_rope(q[..., :hd], ang_row), apply_rope(q[..., hd:], ang_col)], axis=-1)
    k = jnp.concatenate([apply_rope(k[..., :hd], ang_row), apply_rope(k[..., hd:], ang_col)], axis=-1)
    return blocked_attention(q, k, v) @ w_out

def expert_choice_ffn(x, w_r, w_gate, w_up, w_down):
    B, S, D = x.shape
    n = B * S
    cap = CAPACITY_FACTOR * n // N_EXPERTS
    xt = x.reshape(n, D)
    aff = jax.nn.softmax((xt @ w_r).astype(jnp.float32), axis=-1)
    g, idx = lax.top_k(aff.T, cap)
    xe = xt[idx]
    h = jax.nn.silu(jnp.einsum('ecd,edf->ecf', xe, w_gate)) * jnp.einsum('ecd,edf->ecf', xe, w_up)
    ye = jnp.einsum('ecf,efd->ecd', h, w_down) * g[..., None].astype(xe.dtype)
    y = jnp.zeros_like(xt).at[idx.reshape(-1)].add(ye.reshape(-1, D).astype(xt.dtype))
    return y.reshape(B, S, D)

def trunk(x, ab_w_in, ab_conv_w, ab_conv_b, ab_conv_ln_g, ab_conv_ln_b, ab_sink, ab_w_out,
          c_w_in, c_q_norm, c_k_norm, c_w_out, ln1_g, ln1_b,
          moe_router, moe_w_gate, moe_w_up, moe_w_down, ln2_g, ln2_b):
    B, S, _ = x.shape
    pos = jnp.arange(S, dtype=jnp.float32)
    ang_b = rope_angles(pos, ROT_DIM_B, ROPE_THETA_B)
    rows = S // GRID_W
    grid_r, grid_c = jnp.meshgrid(jnp.arange(rows), jnp.arange(GRID_W), indexing='ij')
    ang_row = rope_angles(grid_r.reshape(-1).astype(jnp.float32), HEAD_DIM // 2, ROPE_THETA_C)
    ang_col = rope_angles(grid_c.reshape(-1).astype(jnp.float32), HEAD_DIM // 2, ROPE_THETA_C)
    for layer in range(DEPTH):
        i = layer // 2
        if layer % 2 == 0:
            mix = mixer_conv_window(x, ab_w_in[i], ab_conv_w[i], ab_conv_b[i], ab_conv_ln_g[i],
                                    ab_conv_ln_b[i], ab_sink[i], ab_w_out[i], ang_b)
        else:
            mix = mixer_axial(x, c_w_in[i], c_q_norm[i], c_k_norm[i], c_w_out[i], ang_row, ang_col)
        x = layer_norm(ALPHA * x + mix, ln1_g[layer], ln1_b[layer])
        ffn = expert_choice_ffn(x, moe_router[layer], moe_w_gate[layer], moe_w_up[layer], moe_w_down[layer])
        x = layer_norm(ALPHA * x + ffn, ln2_g[layer], ln2_b[layer])
    return x

def setup_inputs(seed: int = 0) -> dict:
    key = jax.random.key(seed)
    ks = jax.random.split(key, 24)
    nrm = jax.random.normal
    f32 = jnp.float32
    d = D_MODEL
    return {
        'x_prompt': nrm(ks[0], (BATCH, SEQ, d), f32),
        'x_sample': nrm(ks[1], (DEC_BATCH, DEC_SEQ, d), f32),
        'ab_w_in': nrm(ks[2], (N_EVEN, d, AB_IN), f32) * d ** -0.5,
        'ab_conv_w': nrm(ks[3], (N_EVEN, CONV_WIDTH, CONV_DIM), f32) * CONV_WIDTH ** -0.5,
        'ab_conv_b': nrm(ks[4], (N_EVEN, CONV_DIM), f32) * 0.02,
        'ab_conv_ln_g': 1.0 + 0.02 * nrm(ks[5], (N_EVEN, CONV_DIM), f32),
        'ab_conv_ln_b': 0.02 * nrm(ks[6], (N_EVEN, CONV_DIM), f32),
        'ab_sink': nrm(ks[7], (N_EVEN, WIN_HEADS), f32),
        'ab_w_out': nrm(ks[8], (N_EVEN, CONV_DIM + AB_Q, d), f32) * (CONV_DIM + AB_Q) ** -0.5 * BETA,
        'c_w_in': nrm(ks[9], (N_ODD, d, C_IN), f32) * d ** -0.5,
        'c_q_norm': 1.0 + 0.02 * nrm(ks[10], (N_ODD, HEAD_DIM), f32),
        'c_k_norm': 1.0 + 0.02 * nrm(ks[11], (N_ODD, HEAD_DIM), f32),
        'c_w_out': nrm(ks[12], (N_ODD, C_Q, d), f32) * C_Q ** -0.5 * BETA,
        'ln1_g': 1.0 + 0.02 * nrm(ks[13], (DEPTH, d), f32),
        'ln1_b': 0.02 * nrm(ks[14], (DEPTH, d), f32),
        'moe_router': nrm(ks[15], (DEPTH, d, N_EXPERTS), f32) * d ** -0.5,
        'moe_w_gate': nrm(ks[16], (DEPTH, N_EXPERTS, d, D_EXPERT), f32) * d ** -0.5,
        'moe_w_up': nrm(ks[17], (DEPTH, N_EXPERTS, d, D_EXPERT), f32) * d ** -0.5,
        'moe_w_down': nrm(ks[18], (DEPTH, N_EXPERTS, D_EXPERT, d), f32) * D_EXPERT ** -0.5 * BETA,
        'ln2_g': 1.0 + 0.02 * nrm(ks[19], (DEPTH, d), f32),
        'ln2_b': 0.02 * nrm(ks[20], (DEPTH, d), f32),
    }

def reference(x_prompt, x_sample, ab_w_in, ab_conv_w, ab_conv_b, ab_conv_ln_g, ab_conv_ln_b, ab_sink,
              ab_w_out, c_w_in, c_q_norm, c_k_norm, c_w_out, ln1_g, ln1_b,
              moe_router, moe_w_gate, moe_w_up, moe_w_down, ln2_g, ln2_b):
    y_prompt = trunk(x_prompt, ab_w_in, ab_conv_w, ab_conv_b, ab_conv_ln_g, ab_conv_ln_b, ab_sink,
                     ab_w_out, c_w_in, c_q_norm, c_k_norm, c_w_out, ln1_g, ln1_b,
                     moe_router, moe_w_gate, moe_w_up, moe_w_down, ln2_g, ln2_b)
    y_sample = trunk(x_sample, ab_w_in, ab_conv_w, ab_conv_b, ab_conv_ln_g, ab_conv_ln_b, ab_sink,
                     ab_w_out, c_w_in, c_q_norm, c_k_norm, c_w_out, ln1_g, ln1_b,
                     moe_router, moe_w_gate, moe_w_up, moe_w_down, ln2_g, ln2_b)
    return (y_prompt, y_sample)


_drawn_inputs = setup_inputs


def setup_inputs(seed=0):
    import zlib

    import numpy as np

    out = dict(_drawn_inputs(seed))
    spreads = {}
    factors = {'ab_conv_b': 8.0,
     'ab_conv_ln_g': 8.0,
     'ab_conv_ln_b': 8.0,
     'ab_sink': 45.566,
     'c_q_norm': 8.0,
     'c_k_norm': 8.0}
    for name, (base, spread) in spreads.items():
        noise = np.random.default_rng([zlib.crc32(name.encode()), seed]).standard_normal(out[name].shape)
        drawn = base * np.exp(spread * noise) if base else spread * noise
        out[name] = __import__('jax').numpy.asarray(drawn.astype(out[name].dtype))
    for name, factor in factors.items():
        out[name] = (out[name] * factor).astype(out[name].dtype)
    return out
```

```python
from contextlib import ExitStack, contextmanager

import numpy as np

import concourse.bass as bass
from concourse import mybir

P = 128
D = 1024
KD = D // P
SEQ = (512, 1024)
GROUP_TILES = tuple(s // P for s in SEQ)
GROUP_FIRST = (0, GROUP_TILES[0])
TILES = sum(GROUP_TILES)
TOK = TILES * P
HALF = 512
DEPTH = 2
DH = 64
CONV = 512
CT = CONV // P
TAPS = 31
WIN_H, WIN_KV = 8, 2
WIN_Q, WIN_KVD = WIN_H * DH, WIN_KV * DH
AB_IN = 2 * CONV + WIN_Q + 2 * WIN_KVD
ROT = DH // 4
AX_H, AX_KV = 16, 4
AX_Q, AX_KVD = AX_H * DH, AX_KV * DH
C_IN = AX_Q + 2 * AX_KVD
GRID_W = 64
EXPERTS = 16
CAP = tuple(2 * s // EXPERTS for s in SEQ)
SLOTS = sum(CAP)
ALPHA = (2 * DEPTH) ** 0.25
SCALE = DH ** -0.5
LN_EPS = 1e-5
RMS_EPS = 1e-6
MASKED = -1.0e30
PROMPT_ROW = 32

F32 = mybir.dt.float32
U32 = mybir.dt.uint32
ALU = mybir.AluOpType
ACT = mybir.ActivationFunctionType
AX = mybir.AxisListType


class Steps:

    def __init__(self, eng, sem):
        self.eng, self.sem, self.base, self.here = eng, sem, 0, 0

    def add(self, instruction):
        instruction.then_inc(self.sem, 1)
        self.here += 1
        return self.base + self.here

    def settle(self):
        self.eng.wait_ge(self.sem, self.base + self.here)

    def link(self, instruction):
        self.add(instruction)
        self.settle()

    @contextmanager
    def loop(self, turns, each):
        start = self.base + self.here
        with self.eng.Fori(0, turns) as i:
            self.base, self.here = start + i * each, 0
            yield i
            assert self.here == each, (self.here, each)
        self.base, self.here = start + turns * each, 0


class Core:

    def __init__(self, nc):
        self.nc, self.count, self.stack, self.sems = nc, 0, None, None

    @contextmanager
    def stage(self):
        outer = self.stack, self.sems
        self.sems = []
        with ExitStack() as self.stack:
            yield
            if self.sems:
                self.nc.clear_and_free_semaphores(self.sems)
                self.nc.all_engine_barrier()
        self.stack, self.sems = outer

    def sb(self, name, shape, dt=F32):
        self.count += 1
        return self.stack.enter_context(self.nc.sbuf_tensor(f"{name}_{self.count}", shape, dt))

    def ps(self, name, cols):
        self.count += 1
        return self.stack.enter_context(self.nc.psum_tensor(f"{name}_{self.count}", [P, cols], F32))

    def sem(self, name):
        self.count += 1
        self.sems.append(self.nc.alloc_semaphore(f"{name}_{self.count}"))
        return self.sems[-1]

    def block(self):
        return self.nc.Block()


def row_broadcast(vector, parts=P):
    return vector.rearrange("(o n) -> o n", o=1).to_broadcast([parts, vector.shape[0]])


def layer_norm_rows(nc, steps, row, out, stats, mv, gain, shift, var_ready, rstd_ready, tile):
    n = row.shape[1] // HALF
    for h in range(n):
        steps.add(nc.vector.bn_stats(stats[:, 6 * h:6 * h + 6], row[:, h * HALF:(h + 1) * HALF]))
    steps.settle()
    nc.vector.memset(mv[:, 2:3], 0.0)
    steps.link(nc.vector.bn_aggr(mv[:, 0:2], stats[:, 0:6 * n]))
    nc.vector.tensor_scalar(mv[:, 2:3], mv[:, 1:2], LN_EPS, None, ALU.add).then_inc(var_ready, 1)
    steps.eng.wait_ge(rstd_ready, tile + 1)
    steps.link(nc.vector.tensor_scalar(out, row, mv[:, 0:1], mv[:, 3:4], ALU.subtract, ALU.mult))
    steps.link(nc.vector.tensor_tensor(out, out, gain, ALU.mult))
    return nc.vector.tensor_tensor(out, out, shift, ALU.add)


def project_conv_window(c, m, glu, keys, values):
    nc = c.nc
    QK = WIN_Q + WIN_KVD
    QK2 = QK + WIN_KVD
    with c.stage():
        w = c.sb("w_in", [P, KD, AB_IN])
        ident = c.sb("ident", [P, P])
        x = c.sb("x", [P, 2, D])
        rope = c.sb("rope", [P, 2, 2 * ROT])
        xT = c.sb("xT", [P, 2, D])
        sig = c.sb("sig", [P, 2, CONV])
        qk = c.sb("qk", [P, 2, QK2])
        ra = c.sb("ra", [P, QK // DH, ROT])
        rb = c.sb("rb", [P, QK // DH, ROT])
        qT = c.sb("qT", [P, 2, WIN_Q])
        xT_ps, ug_ps, qkv_ps, qkT_ps = (c.ps(n, 1024) for n in ("xT_ps", "ug_ps", "qkv_ps", "qkT_ps"))
        w_in, x_in = c.sem("w_in"), [c.sem("x_in0"), c.sem("x_in1")]
        xT_done, xT_ready, ug_done, sig_ready = c.sem("xT_done"), c.sem("xT_ready"), c.sem("ug_done"), c.sem("sig_ready")
        glu_ready, qkv_done, qk_ready, qkT_done = c.sem("glu_ready"), c.sem("qkv_done"), c.sem("qk_ready"), c.sem("qkT_done")
        qT_ready, k_ready, q_stored = c.sem("qT_ready"), c.sem("k_ready"), [c.sem("q_out0"), c.sem("q_out1")]
        dve, zero = c.sem("dve"), c.sem("zero")
        with c.block() as block:

            @block.sync
            def _(sp):
                sp.dma_start(ident[:], m["ident"]).then_inc(w_in, 16)
                win = m["ab_w_in"][0].rearrange("(k p) n -> p k n", p=P)
                sp.dma_start(w[:, :, 2 * CONV:AB_IN], win[:, :, 2 * CONV:AB_IN]).then_inc(w_in, 16)
                sp.dma_start(w[:, :, 0:2 * CONV], win[:, :, 0:2 * CONV]).then_inc(w_in, 16)
                with sp.Fori(0, TILES // 2) as i:
                    for u in range(2):
                        t = i * 2 + u
                        sp.wait_ge(xT_done, t + 1)
                        sp.wait_ge(qk_ready, t + 1)
                        sp.dma_start(x[:, u, :], m["x"][bass.ds(t * P, P), :]).then_inc(x_in[u], 16)
                        sp.dma_start(rope[:, u, :], m["rope_b"][bass.ds(t * P, P), :]).then_inc(x_in[u], 16)

            @block.tensor
            def _(pe):
                pe.sem_inc(xT_done, 2)
                pe.wait_ge(w_in, 48)
                with pe.Fori(0, TILES // 2) as i:
                    for u in range(2):
                        t = i * 2 + u
                        pe.wait_ge(x_in[u], i * 32 + 32)
                        pe.wait_ge(xT_ready, t + 1)
                        for k in range(KD):
                            last = nc.tensor.transpose(xT_ps[:, k * P:(k + 1) * P], x[:, u, k * P:(k + 1) * P], ident[:])
                        last.then_inc(xT_done, 1)
                        pe.wait_ge(xT_ready, t + 2)
                        pe.wait_ge(qk_ready, t + 2)
                        for base, cols in ((0, WIN_Q), (WIN_Q, 2 * WIN_KVD)):
                            for k in range(KD):
                                last = nc.tensor.matmul(qkv_ps[:, base:base + cols], xT[:, u, k * P:(k + 1) * P],
                                                        w[:, k, 2 * CONV + base:2 * CONV + base + cols],
                                                        start=(k == 0), stop=(k == KD - 1))
                        last.then_inc(qkv_done, 1)
                        pe.wait_ge(glu_ready, t + 1)
                        for ct in range(2 * CT):
                            for k in range(KD):
                                last = nc.tensor.matmul(ug_ps[:, ct * P:(ct + 1) * P], w[:, k, ct * P:(ct + 1) * P],
                                                        xT[:, u, k * P:(k + 1) * P], start=(k == 0), stop=(k == KD - 1))
                        last.then_inc(ug_done, 1)
                        pe.wait_ge(qk_ready, t + 3)
                        pe.wait_ge(k_ready, t + 1)
                        for j in range(QK2 // P):
                            last = nc.tensor.transpose(qkT_ps[:, j * P:(j + 1) * P], qk[:, u, j * P:(j + 1) * P], ident[:])
                        last.then_inc(qkT_done, 1)

            @block.scalar
            def _(act):
                act.sem_inc(xT_ready, 1)
                act.sem_inc(k_ready, 1)
                for u in range(2):
                    act.sem_inc(q_stored[u], 16)
                with act.Fori(0, TILES // 2) as i:
                    for u in range(2):
                        t = i * 2 + u
                        act.wait_ge(xT_done, t + 3)
                        nc.scalar.activation(xT[:, u, :], xT_ps[:], ACT.Copy).then_inc(xT_ready, 1)
                        act.wait_ge(ug_done, t + 1)
                        nc.scalar.activation(sig[:, u, :], ug_ps[:, CONV:2 * CONV], ACT.Sigmoid).then_inc(sig_ready, 1)
                        act.wait_ge(qkT_done, t + 1)
                        act.wait_ge(q_stored[u], i * 16 + 16)
                        nc.scalar.activation(qT[:, u, :], qkT_ps[:, 0:WIN_Q], ACT.Copy).then_inc(qT_ready, 1)
                        act.wait_ge(qT_ready, t + 1)
                        act.dma_start(m["qT"][bass.ds(t * P, P), 0:WIN_Q], qT[:, u, :]).then_inc(q_stored[u], 16)
                        act.wait_ge(zero, 2)
                        at = bass.ds((t + 1) * P, P)
                        kT = qkT_ps[:, WIN_Q:QK2].rearrange("p (j n) -> p j n", j=WIN_KV)
                        nc.scalar.activation(keys[0:DH, 0:WIN_KV, at], kT[0:DH], ACT.Copy)
                        nc.scalar.activation(keys[DH:P, WIN_KV:2 * WIN_KV, at], kT[DH:P], ACT.Copy).then_inc(k_ready, 1)
                for u in range(2):
                    act.wait_ge(q_stored[u], 16 * (TILES // 2) + 16)

            @block.vector
            def _(v):
                s = Steps(v, dve)
                nc.vector.memset(keys[:], 0.0).then_inc(zero, 1)
                nc.vector.memset(values[:], 0.0).then_inc(zero, 1)
                v.wait_ge(zero, 2)
                v.sem_inc(qk_ready, 2)
                v.sem_inc(glu_ready, 1)
                heads = QK // DH
                with s.loop(TILES // 2, 2 * 7) as i:
                    for u in range(2):
                        t = i * 2 + u
                        v.wait_ge(qkv_done, t + 1)
                        v.wait_ge(xT_done, t + 3)
                        s.add(nc.vector.tensor_copy(values[:, bass.ds(t + 1, 1), :], qkv_ps[:, QK:QK + WIN_KVD].rearrange("p (o n) -> p o n", o=1)))
                        s.link(nc.vector.tensor_copy(qk[:, u, 0:QK], qkv_ps[:, 0:QK]))
                        v.wait_ge(x_in[u], i * 32 + 32)
                        rot = qk[:, u, 0:QK].rearrange("p (h d) -> p h d", d=DH)
                        cos = rope[:, u, 0:ROT].rearrange("p (o n) -> p o n", o=1).to_broadcast([P, heads, ROT])
                        h2 = ROT // 2
                        s0 = rope[:, u, ROT:ROT + h2].rearrange("p (o n) -> p o n", o=1).to_broadcast([P, heads, h2])
                        s1 = rope[:, u, ROT + h2:2 * ROT].rearrange("p (o n) -> p o n", o=1).to_broadcast([P, heads, h2])
                        s.add(nc.vector.tensor_tensor(ra[:], rot[:, :, 0:ROT], cos, ALU.mult))
                        s.add(nc.vector.tensor_tensor(rb[:, :, 0:h2], rot[:, :, h2:ROT], s0, ALU.mult))
                        s.add(nc.vector.tensor_tensor(rb[:, :, h2:ROT], rot[:, :, 0:h2], s1, ALU.mult))
                        s.settle()
                        s.link(nc.vector.tensor_tensor(rot[:, :, 0:ROT], ra[:], rb[:], ALU.add))
                        s.add(nc.vector.tensor_copy(qk[:, u, QK:QK + DH], qk[:, u, WIN_Q + DH:QK]))
                        nc.vector.tensor_copy(qk[:, u, QK + DH:QK2], qk[:, u, WIN_Q:WIN_Q + DH]).then_inc(qk_ready, 1)
                        v.wait_ge(sig_ready, t + 1)
                        nc.vector.tensor_tensor(glu[:, :, bass.ds(t * P, P)], ug_ps[:, 0:CONV].rearrange("p (c n) -> p c n", c=CT),
                                                sig[:, u, :].rearrange("p (c n) -> p c n", c=CT), ALU.mult).then_inc(glu_ready, 1)


def convolve(c, m, glu, cat):
    nc = c.nc
    with c.stage():
        acc = c.sb("acc", [P, CT, TOK])
        wc = c.sb("conv_w", [P, CT, TAPS])
        par = c.sb("conv_par", [P, 3, CT])
        ones = c.sb("ones", [P, P])
        eps = c.sb("eps", [P, 1])
        sq = c.sb("sq", [P, 2, CT, HALF])
        rstd = c.sb("rstd", [P, TOK // HALF, HALF])
        mean_ps, var_ps = c.ps("mean_ps", HALF), c.ps("var_ps", HALF)
        loaded, dve, conv_done, const = c.sem("loaded"), c.sem("dve"), c.sem("conv_done"), c.sem("const")
        mean_done, centred, squared, var_done, rooted, normed, cat_done = (
            c.sem(n) for n in ("mean_done", "centred", "squared", "var_done", "rooted", "normed", "cat_done"))
        chunks = TOK // HALF
        with c.block() as block:

            @block.sync
            def _(sp):
                sp.dma_start(wc[:], m["conv_w"]).then_inc(loaded, 16)
                for n, name in enumerate(("conv_b", "conv_g", "conv_beta")):
                    sp.dma_start(par[:, n, :], m[name]).then_inc(loaded, 16)

            @block.gpsimd
            def _(pool):
                pool.memset(ones[:], 1.0 / CONV).then_inc(const, 1)
                pool.memset(eps[:], LN_EPS).then_inc(const, 1)

            @block.vector
            def _(v):
                s = Steps(v, dve)
                v.wait_ge(loaded, 64)
                mid = TAPS // 2
                with s.loop(CT, len(SEQ) * TAPS) as ct:
                    one = bass.ds(ct, 1)
                    for g in range(len(SEQ)):
                        a, b = GROUP_FIRST[g] * P, (GROUP_FIRST[g] + GROUP_TILES[g]) * P
                        s.add(nc.vector.tensor_scalar(acc[:, one, a:b], glu[:, one, a:b], wc[:, one, mid:mid + 1],
                                                      par[:, 0, one], ALU.mult, ALU.add))
                    for tap in [x for x in range(TAPS) if x != mid]:
                        shift = tap - mid
                        for g in range(len(SEQ)):
                            a, b = GROUP_FIRST[g] * P, (GROUP_FIRST[g] + GROUP_TILES[g]) * P
                            lo, hi = max(a, a - shift), min(b, b - shift)
                            v.wait_ge(dve, s.base + s.here - 1)
                            s.add(nc.vector.scalar_tensor_tensor(acc[:, one, lo:hi], glu[:, one, lo + shift:hi + shift],
                                                                 wc[:, one, tap:tap + 1], acc[:, one, lo:hi], ALU.mult, ALU.add))
                s.settle()
                nc.vector.engine_nop().then_inc(conv_done, 1)
                for n in range(chunks):
                    part = acc[:, :, n * HALF:(n + 1) * HALF]
                    v.wait_ge(mean_done, n + 1)
                    for ct in range(CT):
                        nc.vector.tensor_tensor(part[:, ct, :], part[:, ct, :], mean_ps[:], ALU.subtract).then_inc(centred, 1)
                for n in range(chunks):
                    part = acc[:, :, n * HALF:(n + 1) * HALF]
                    v.wait_ge(rooted, n + 1)
                    s.link(nc.vector.reciprocal(rstd[:, n, :], rstd[:, n, :]))
                    v.wait_ge(centred, CT * (n + 1))
                    for ct in range(CT):
                        nc.vector.tensor_tensor(part[:, ct, :], part[:, ct, :], rstd[:, n, :], ALU.mult).then_inc(normed, 1)

            @block.tensor
            def _(pe):
                pe.wait_ge(const, 1)
                pe.wait_ge(conv_done, 1)
                for n in range(chunks):
                    part = acc[:, :, n * HALF:(n + 1) * HALF]
                    if n:
                        pe.wait_ge(centred, CT * n)
                    for ct in range(CT):
                        last = nc.tensor.matmul(mean_ps[:], ones[:], part[:, ct, :], start=(ct == 0), stop=(ct == CT - 1))
                    last.then_inc(mean_done, 1)
                    pe.wait_ge(squared, n + 1)
                    if n:
                        pe.wait_ge(rooted, n)
                    for ct in range(CT):
                        last = nc.tensor.matmul(var_ps[:], ones[:], sq[:, n % 2, ct, :], start=(ct == 0), stop=(ct == CT - 1))
                    last.then_inc(var_done, 1)

            @block.scalar
            def _(act):
                act.wait_ge(const, 2)
                for n in range(chunks):
                    part = acc[:, :, n * HALF:(n + 1) * HALF]
                    act.wait_ge(centred, CT * (n + 1))
                    if n >= 2:
                        act.wait_ge(var_done, n - 1)
                    nc.scalar.activation(sq[:, n % 2], part, ACT.Square).then_inc(squared, 1)
                    act.wait_ge(var_done, n + 1)
                    nc.scalar.activation(rstd[:, n, :], var_ps[:], ACT.Sqrt, bias=eps[:]).then_inc(rooted, 1)
                for n in range(chunks):
                    part = acc[:, :, n * HALF:(n + 1) * HALF]
                    act.wait_ge(normed, CT * (n + 1))
                    for ct in range(CT):
                        nc.scalar.activation(cat[:, ct, n * HALF:(n + 1) * HALF], part[:, ct, :], ACT.Silu,
                                             bias=par[:, 2, ct:ct + 1], scale=par[:, 1, ct:ct + 1]).then_inc(cat_done, 1)


def window_attention(c, m, keys, values, cat):
    nc = c.nc
    G = WIN_H // WIN_KV
    NK = 3 * P
    place = {(0, 0): 0, (1, 0): 1, (1, 1): 2, (0, 1): 3}
    with c.stage():
        ident = c.sb("ident", [P, P])
        sink = c.sb("sink", [P, 2, WIN_H])
        q = c.sb("q", [P, 2, WIN_Q])
        mask = c.sb("mask", [P, 2, NK])
        sm = c.sb("sm", [P, 2, G, NK])
        mx = c.sb("mx", [P, 2, 6, G])
        still = c.sb("still", [P, 1])
        pT = c.sb("pT", [P, 2, G * NK])
        o = c.sb("o", [P, 2, WIN_Q])
        s_ps, t_ps, o_ps = c.ps("s_ps", 4 * HALF), c.ps("t_ps", G * NK), c.ps("o_ps", WIN_Q)
        loaded, q_in = c.sem("loaded"), [c.sem("q_in0"), c.sem("q_in1")]
        scores, masked, bias, expd, pT_done, pT_act, pT_dve, o_done, o_ready, oT_done, oT_out, dve = (
            c.sem(n) for n in ("scores", "masked", "bias", "expd", "pT_done", "pT_act", "pT_dve", "o_done", "o_ready",
                               "oT_done", "oT_out", "dve"))
        CUT = 2 * HALF
        with c.block() as block:

            @block.sync
            def _(sp):
                sp.dma_start(ident[:], m["ident"]).then_inc(loaded, 16)
                sp.dma_start(sink[:, 0, :], row_broadcast(m["ab_sink"][0])).then_inc(loaded, 16)
                with sp.Fori(0, TILES // 2) as i:
                    for u in range(2):
                        t = i * 2 + u
                        sp.wait_ge(o_ready, t + 1)
                        sp.dma_start(q[:, u, :], m["qT"][bass.ds(t * P, P), 0:WIN_Q]).then_inc(q_in[u], 16)
                        sp.dma_start(mask[:, u, :], m["mask"][bass.ds(t * P, P), :]).then_inc(q_in[u], 16)

            def unit(n):
                return n // 2, n % 2, n % 2

            @block.tensor
            def _(pe):
                pe.wait_ge(loaded, 32)
                with pe.Fori(0, TILES // 2) as i:

                    def qk(n):
                        u, kv, _ = unit(n)
                        if kv == 0:
                            pe.wait_ge(q_in[u], i * 32 + 32)
                        pe.wait_ge(masked, (i * 4 + n) * G + 1)
                        for h in range(G):
                            head = kv * G + h
                            last = nc.tensor.matmul(s_ps[:, h * HALF:h * HALF + NK], q[:, u, (head // 2) * P:(head // 2 + 1) * P],
                                                    keys[:, place[kv, head % 2], bass.ds(i * 2 * P + u * P, NK)], start=True, stop=True)
                        last.then_inc(scores, 1)

                    def pv(n):
                        u, kv, b = unit(n)
                        pe.wait_ge(expd, i * 4 + n + 1)
                        pe.wait_ge(pT_act, i * 4 + n + 1)
                        pe.wait_ge(pT_dve, i * 4 + n + 1)
                        if kv == 0:
                            pe.wait_ge(oT_out, i * 2 + u + 1)
                        for h in range(G):
                            for k in range(3):
                                last = nc.tensor.transpose(t_ps[:, (h * 3 + k) * P:(h * 3 + k + 1) * P], sm[:, b, h, k * P:(k + 1) * P], ident[:])
                        last.then_inc(pT_done, 1)
                        pe.wait_ge(pT_act, i * 4 + n + 2)
                        pe.wait_ge(pT_dve, i * 4 + n + 2)
                        if kv == 0:
                            pe.wait_ge(o_ready, i * 2 + u + 2)
                        for h in range(G):
                            head = kv * G + h
                            for k in range(3):
                                last = nc.tensor.matmul(o_ps[:, head * DH:(head + 1) * DH], pT[:, b, (h * 3 + k) * P:(h * 3 + k + 1) * P],
                                                        values[:, bass.ds(i * 2 + u + k, 1), kv * DH:(kv + 1) * DH],
                                                        start=(k == 0), stop=(k == 2))
                        last.then_inc(o_done, 1)
                        if kv == 1:
                            pe.wait_ge(o_ready, i * 2 + u + 3)
                            for j in range(CT):
                                last = nc.tensor.transpose(t_ps[:, j * P:(j + 1) * P], o[:, u, j * P:(j + 1) * P], ident[:])
                            last.then_inc(oT_done, 1)

                    qk(0)
                    for n in range(4):
                        if n < 3:
                            qk(n + 1)
                        pv(n)

            @block.vector
            def _(v):
                s = Steps(v, dve)
                v.wait_ge(loaded, 32)
                v.sem_inc(masked, 1)
                v.sem_inc(pT_dve, 1)
                v.sem_inc(o_ready, 2)
                with s.loop(TILES // 2, 16) as i:

                    def soft(n):
                        u, kv, b = unit(n)
                        v.wait_ge(scores, i * 4 + n + 1)
                        v.wait_ge(pT_done, i * 4 + n + 1)
                        if kv == 0:
                            v.wait_ge(q_in[u], i * 32 + 32)
                        nc.vector.memset(still[:], 0.0)
                        for h in range(G):
                            nc.vector.tensor_tensor_reduce(out=sm[:, b, h, :], in0=s_ps[:, h * HALF:h * HALF + NK], in1=mask[:, u, :],
                                                           scale=SCALE, scalar=MASKED, op0=ALU.add, op1=ALU.max,
                                                           accum_out=mx[:, b, 0, h:h + 1]).then_inc(masked, 1)
                        v.wait_ge(masked, (i * 4 + n) * G + G + 1)
                        snk = sink[:, 0, kv * G:(kv + 1) * G]
                        s.link(nc.vector.tensor_tensor(mx[:, b, 1, :], mx[:, b, 0, :], snk, ALU.max))
                        s.add(nc.vector.tensor_scalar(mx[:, b, 2, :], mx[:, b, 1, :], -1.0, None, ALU.mult))
                        nc.vector.tensor_tensor(mx[:, b, 3, :], snk, mx[:, b, 1, :], ALU.subtract).then_inc(bias, 1)

                    def after(n):
                        u, kv, b = unit(n)
                        v.wait_ge(expd, i * 4 + n + 1)
                        s.link(nc.vector.tensor_tensor(mx[:, b, 4, :], mx[:, b, 4, :], mx[:, b, 5, :], ALU.add))
                        s.link(nc.vector.reciprocal(sink[:, 1, kv * G:(kv + 1) * G], mx[:, b, 4, :]))
                        v.wait_ge(pT_done, i * 4 + n + 3)
                        nc.vector.tensor_copy(pT[:, b, CUT:G * NK], t_ps[:, CUT:G * NK]).then_inc(pT_dve, 1)
                        if kv == 1:
                            v.wait_ge(o_done, i * 4 + n + 1)
                            v.wait_ge(oT_done, i * 2 + u + 1)
                            nc.vector.tensor_tensor(o[:, u, :].rearrange("p (h d) -> p h d", d=DH), o_ps[:].rearrange("p (h d) -> p h d", d=DH),
                                                    sink[:, 1, :].rearrange("p (h o) -> p h o", o=1).to_broadcast([P, WIN_H, DH]),
                                                    ALU.mult).then_inc(o_ready, 1)

                    soft(0)
                    for n in range(4):
                        if n < 3:
                            soft(n + 1)
                        after(n)

            @block.scalar
            def _(act):
                act.sem_inc(pT_done, 2)
                act.sem_inc(oT_done, 2)
                act.sem_inc(pT_act, 1)
                act.sem_inc(oT_out, 1)
                with act.Fori(0, TILES // 2) as i:

                    def exps(n):
                        u, kv, b = unit(n)
                        act.wait_ge(bias, i * 4 + n + 1)
                        for h in range(G):
                            nc.scalar.activation(sm[:, b, h, :], sm[:, b, h, :], ACT.Exp, bias=mx[:, b, 2, h:h + 1],
                                                 accum_out=mx[:, b, 4, h:h + 1])
                        nc.scalar.activation(mx[:, b, 5, :], mx[:, b, 3, :], ACT.Exp).then_inc(expd, 1)

                    def after(n):
                        u, kv, b = unit(n)
                        act.wait_ge(pT_done, i * 4 + n + 3)
                        nc.scalar.activation(pT[:, b, 0:CUT], t_ps[:, 0:CUT], ACT.Copy).then_inc(pT_act, 1)
                        if kv == 1:
                            act.wait_ge(oT_done, i * 2 + u + 3)
                            nc.scalar.activation(cat[:, CT:2 * CT, bass.ds(i * 2 * P + u * P, P)],
                                                 t_ps[:, 0:WIN_Q].rearrange("p (c n) -> p c n", c=CT), ACT.Copy).then_inc(oT_out, 1)

                    exps(0)
                    for n in range(4):
                        if n < 3:
                            exps(n + 1)
                        after(n)


def project_out(c, m, layer, w_out, x_src, cat, affinity):
    nc = c.nc
    with c.stage():
        w = c.sb("w_out", [P, KD, D])
        wr = c.sb("router", [P, KD, EXPERTS])
        ident = c.sb("ident", [P, P])
        gain, shift = c.sb("gain", [P, D]), c.sb("shift", [P, D])
        a = c.sb("cat_tile", [P, 2, KD, P])
        x = c.sb("x", [P, 2, D])
        row = c.sb("row", [P, D])
        stats, mv = c.sb("stats", [P, 12]), c.sb("mv", [P, 4])
        half = c.sb("minus_half", [P, 1])
        x1, ax1 = c.sb("x1", [P, 2, D]), c.sb("ax1", [P, 2, D])
        xT = c.sb("xT", [P, 2, D])
        prob, pr = c.sb("prob", [P, 2, EXPERTS]), c.sb("prob_stats", [P, 4])
        y_ps, t_ps = [c.ps("y_ps0", D), c.ps("y_ps1", D)], c.ps("t_ps", D)
        r_ps, rT_ps = c.ps("r_ps", HALF), c.ps("rT_ps", HALF)
        w_in, a_in = c.sem("w_in"), [c.sem("a_in0"), c.sem("a_in1")]
        y_done, res_done, var_ready, rstd_ready, x1_ready, ax_ready, xT_done, xT_ready, r_done, neg_ready, exp_done, prob_ready, rT_done, aff_ready, dve, const = (
            c.sem(n) for n in ("y_done", "res_done", "var_ready", "rstd_ready", "x1_ready", "ax_ready", "xT_done", "xT_ready", "r_done",
                               "neg_ready", "exp_done", "prob_ready", "rT_done", "aff_ready", "dve", "const"))
        x1_out = [c.sem("x1_out0"), c.sem("x1_out1")]
        with c.block() as block:

            @block.sync
            def _(sp):
                wv = w_out.rearrange("(k p) n -> p k n", p=P)
                sp.dma_start(w[:], wv).then_inc(w_in, 16)
                sp.dma_start(wr[:], m["moe_router"][layer].rearrange("(k p) n -> p k n", p=P)).then_inc(w_in, 16)
                sp.dma_start(ident[:], m["ident"]).then_inc(w_in, 16)
                sp.dma_start(gain[:], row_broadcast(m["ln1_g"][layer])).then_inc(w_in, 16)
                sp.dma_start(shift[:], row_broadcast(m["ln1_b"][layer])).then_inc(w_in, 16)
                with sp.Fori(0, TILES // 2) as i:
                    for u in range(2):
                        t = i * 2 + u
                        sp.wait_ge(res_done, t + 1)
                        sp.dma_start(a[:, u, :, :], cat[:, :, bass.ds(t * P, P)]).then_inc(a_in[u], 16)
                        sp.dma_start(x[:, u, :], x_src[bass.ds(t * P, P), :]).then_inc(a_in[u], 16)

            @block.gpsimd
            def _(pool):
                pool.memset(half[:], -0.5).then_inc(const, 1)
                pool.wait_ge(const, 1)
                with pool.Fori(0, TILES // 2) as i:
                    for u in range(2):
                        t = i * 2 + u
                        pool.wait_ge(var_ready, t + 1)
                        pool.tensor_tensor(mv[:, 3:4], mv[:, 2:3], half[:], ALU.pow).then_inc(rstd_ready, 1)

            @block.tensor
            def _(pe):
                pe.wait_ge(w_in, 80)
                with pe.Fori(0, TILES // 2) as i:
                    for u in range(2):
                        t = i * 2 + u
                        pe.wait_ge(a_in[u], i * 32 + 32)
                        pe.wait_ge(res_done, t + 1)
                        for h in range(2):
                            for k in range(KD):
                                last = nc.tensor.matmul(y_ps[u][:, h * HALF:(h + 1) * HALF], a[:, u, k, :], w[:, k, h * HALF:(h + 1) * HALF],
                                                        start=(k == 0), stop=(k == KD - 1))
                        last.then_inc(y_done, 1)
                        if u == 1:
                            for b in range(2):
                                tb = i * 2 + b
                                pe.wait_ge(x1_ready, tb + 1)
                                pe.wait_ge(xT_ready, tb + 1)
                                for k in range(KD):
                                    last = nc.tensor.transpose(t_ps[:, k * P:(k + 1) * P], x1[:, b, k * P:(k + 1) * P], ident[:])
                                last.then_inc(xT_done, 1)
                                pe.wait_ge(xT_ready, tb + 2)
                                pe.wait_ge(prob_ready, tb + 1)
                                for k in range(KD):
                                    last = nc.tensor.matmul(r_ps[:, 0:EXPERTS], xT[:, b, k * P:(k + 1) * P], wr[:, k, :],
                                                            start=(k == 0), stop=(k == KD - 1))
                                last.then_inc(r_done, 1)
                                pe.wait_ge(prob_ready, tb + 2)
                                pe.wait_ge(aff_ready, tb + 1)
                                nc.tensor.transpose(rT_ps[0:EXPERTS, 0:P], prob[:, b, :], ident[:]).then_inc(rT_done, 1)

            @block.vector
            def _(v):
                s = Steps(v, dve)
                v.wait_ge(w_in, 80)
                v.sem_inc(res_done, 2)
                v.sem_inc(prob_ready, 1)
                with s.loop(TILES // 2, 2 * 5 + 2) as i:
                    for u in range(2):
                        t = i * 2 + u
                        v.wait_ge(y_done, t + 1)
                        v.wait_ge(a_in[u], i * 32 + 32)
                        nc.vector.scalar_tensor_tensor(row[:], x[:, u, :], ALPHA, y_ps[u][:], ALU.mult, ALU.add).then_inc(res_done, 1)
                        v.wait_ge(res_done, t + 3)
                        v.wait_ge(x1_out[u], i * 32 + 32)
                        v.wait_ge(xT_done, t + 1)
                        v.wait_ge(ax_ready, t + 1)
                        last = layer_norm_rows(nc, s, row[:], x1[:, u, :], stats, mv, gain[:], shift[:], var_ready, rstd_ready, t)
                        last.then_inc(x1_ready, 1)
                    for b in range(2):
                        tb = i * 2 + b
                        v.wait_ge(r_done, tb + 1)
                        nc.vector.tensor_reduce(pr[:, 0:1], r_ps[:, 0:EXPERTS], AX.X, ALU.max, negate=True).then_inc(neg_ready, 1)
                        v.wait_ge(exp_done, tb + 1)
                        s.link(nc.vector.reciprocal(pr[:, 2:3], pr[:, 1:2]))
                        nc.vector.tensor_scalar(prob[:, b, :], prob[:, b, :], pr[:, 2:3], None, ALU.mult).then_inc(prob_ready, 1)

            @block.scalar
            def _(act):
                act.sem_inc(xT_ready, 1)
                act.sem_inc(xT_done, 2)
                act.sem_inc(ax_ready, 2)
                act.sem_inc(aff_ready, 1)
                act.sem_inc(rT_done, 2)
                for u in range(2):
                    act.sem_inc(x1_out[u], 32)
                with act.Fori(0, TILES // 2) as i:
                    for u in range(2):
                        t = i * 2 + u
                        act.wait_ge(x1_ready, t + 1)
                        act.wait_ge(x1_out[u], i * 32 + 32)
                        nc.scalar.activation(ax1[:, u, :], x1[:, u, :], ACT.Copy, scale=ALPHA).then_inc(ax_ready, 1)
                        act.dma_start(m["x1"][bass.ds(t * P, P), :], x1[:, u, :]).then_inc(x1_out[u], 16)
                        act.wait_ge(ax_ready, t + 3)
                        act.dma_start(m["acc"][bass.ds(t * P, P), :], ax1[:, u, :]).then_inc(x1_out[u], 16)
                    for b in range(2):
                        tb = i * 2 + b
                        act.wait_ge(xT_done, tb + 3)
                        nc.scalar.activation(xT[:, b, :], t_ps[:], ACT.Copy).then_inc(xT_ready, 1)
                        act.wait_ge(neg_ready, tb + 1)
                        act.wait_ge(rT_done, tb + 1)
                        nc.scalar.activation(prob[:, b, :], r_ps[:, 0:EXPERTS], ACT.Exp, bias=pr[:, 0:1], accum_out=pr[:, 1:2]).then_inc(exp_done, 1)
                        act.wait_ge(rT_done, tb + 3)
                        nc.scalar.activation(affinity[:, bass.ds(tb * P, P)], rT_ps[0:EXPERTS, 0:P], ACT.Copy).then_inc(aff_ready, 1)
                for u in range(2):
                    act.wait_ge(x1_out[u], 32 * (TILES // 2) + 32)


def choose(c, m, affinity, gates, rows):
    nc = c.nc
    R = PROMPT_ROW + EXPERTS
    N = SEQ[1]
    BEST = CAP[1]
    with c.stage():
        ident = c.sb("ident", [P, P])
        left = c.sb("left", [R, 2, N])
        best = c.sb("best", [R, BEST])
        where = c.sb("where", [R, BEST], U32)
        wheref = c.sb("wheref", [R, BEST])
        t_ps = c.ps("t_ps", HALF)
        loaded, dve, turned = c.sem("loaded"), c.sem("dve"), c.sem("turned")
        with c.block() as block:

            @block.sync
            def _(sp):
                sp.dma_start(ident[:], m["ident"]).then_inc(loaded, 16)

            @block.vector
            def _(v):
                s = Steps(v, dve)
                s.add(nc.vector.memset(rows[:], 0))
                s.add(nc.vector.memset(gates[:], 0.0))
                s.link(nc.vector.memset(left[:], -1.0))
                s.add(nc.vector.tensor_copy(left[0:EXPERTS, 0, :], affinity[:, SEQ[0]:TOK]))
                s.link(nc.vector.tensor_copy(left[PROMPT_ROW:R, 0, 0:SEQ[0]], affinity[:, 0:SEQ[0]]))
                for r in range(BEST // 8):
                    now, eight = left[:, r % 2, :], slice(8 * r, 8 * r + 8)
                    s.link(nc.vector.max(out=best[:, eight], in_=now))
                    s.add(nc.vector.max_index(out=where[:, eight], in_max=best[:, eight], in_values=now))
                    if r + 1 < BEST // 8:
                        s.link(nc.vector.match_replace(out=left[:, (r + 1) % 2, :], in_to_replace=best[:, eight], in_values=now, imm_value=-2.0))
                s.settle()
                s.link(nc.vector.tensor_copy(wheref[:], where[:]))
                s.link(nc.vector.tensor_scalar(wheref[0:EXPERTS, :], wheref[0:EXPERTS, :], float(SEQ[0]), None, ALU.add))
                v.wait_ge(turned, 1)
                nc.vector.tensor_copy(gates[:, 0:R], t_ps[:, 0:R])
                s.link(nc.vector.tensor_copy(rows[:, 0:R], t_ps[:, 64:64 + R]))

            @block.tensor
            def _(pe):
                pe.wait_ge(loaded, 16)
                pe.wait_ge(dve, 5 + 3 * (BEST // 8) - 1 + 2)
                nc.tensor.transpose(t_ps[:, 0:R], best[:], ident[0:R, 0:R])
                nc.tensor.transpose(t_ps[:, 64:64 + R], wheref[:], ident[0:R, 0:R]).then_inc(turned, 1)


def experts(c, m, layer, gates, rows):
    nc = c.nc
    SC, PC = CAP[1], CAP[0]
    FH = KD // 2
    with c.stage():
        ident = c.sb("ident", [P, P])
        w = [c.sb(f"w{n}", [P, KD * HALF]) for n in range(6)]
        ids = c.sb("ids", [P, 2, 2], U32)
        gsel = c.sb("gsel", [P, 2, 2])
        xs, xp = [c.sb(f"xs{u}", [P, D]) for u in range(2)], [c.sb(f"xp{u}", [PC, D]) for u in range(2)]
        xT = c.sb("xT", [P, KD, SLOTS])
        sg = c.sb("sg", [P, 2, SLOTS])
        hT = c.sb("hT", [P, KD, SLOTS])
        ys, yp = c.sb("ys", [P, D]), c.sb("yp", [PC, D])
        h_ps = [c.ps(f"h_ps{b}", HALF) for b in range(2)]
        t_ps = [c.ps(f"t_ps{b}", HALF) for b in range(2)]
        y_ps, yp_ps = c.ps("y_ps", D), c.ps("yp_ps", D)
        loaded = c.sem("loaded")
        w_in = [c.sem(f"w_in{n}") for n in range(6)]
        x_in = [c.sem("x_in0"), c.sem("x_in1")]
        ids_ready, turned, xT_ready, h_done, silu_ready, h_ready, y_done, ys_ready, yp_ready, added = (
            c.sem(n) for n in ("ids_ready", "turned", "xT_ready", "h_done", "silu_ready", "h_ready", "y_done", "ys_ready",
                               "yp_ready", "added"))
        turn_done = c.sem("turn_done")
        still = c.sb("still", [P, 5])
        QUADS = KD // 2
        picks, gate_cols = rows[:].rearrange("p (g e) -> p g e", g=2), gates[:].rearrange("p (g e) -> p g e", g=2)
        with c.block() as block:

            @block.sync
            def _(sp):
                sp.dma_start(ident[:], m["ident"]).then_inc(loaded, 16)
                gate_up = [m[n].rearrange("l e (k p) f -> (l e) p k f", p=P) for n in ("moe_w_gate", "moe_w_up")]
                down = m["moe_w_down"].rearrange("l e (h k p) d -> (l e) p h k d", p=P, h=2)
                with sp.Fori(0, EXPERTS) as e:
                    which = bass.ds(e + layer * EXPERTS, 1)
                    for part in range(2):
                        sp.wait_ge(h_done, e * KD + FH * part + FH)
                        for n in range(2):
                            sp.dma_start(w[2 * part + n][:].rearrange("p (o k f) -> p o k f", o=1, k=KD),
                                         gate_up[n][which, :, :, part * HALF:(part + 1) * HALF].rearrange("o p k f -> p o k f")).then_inc(w_in[2 * part + n], 16)
                    for part in range(2):
                        sp.wait_ge(y_done, e * 2 + part + 1)
                        sp.dma_start(w[4 + part][:].rearrange("p (o k d) -> p o k d", o=1, k=FH),
                                     down[which, :, part, :, :].rearrange("o p k d -> p o k d")).then_inc(w_in[4 + part], 16)

            @block.gpsimd
            def _(pool):
                def hold(at):
                    return pool.tensor_tensor(still[:, at:at + 1], still[:, 0:1], still[:, 0:1], ALU.add)

                def gather(u, e, at):
                    pool.wait_ge(ids_ready, e + 1)
                    pool.wait_ge(turned, e * QUADS + QUADS)
                    pool.wait_ge(turn_done, e + 1)
                    hold(at)
                    pool.indirect_dma_start(out=xs[u][:], out_offset=None, in_=m["x1"],
                                            in_offset=bass.IndirectOffsetOnAxis(ap=ids[:, u, 0:1], axis=0)).then_inc(x_in[u], 16)
                    pool.indirect_dma_start(out=xp[u][:], out_offset=None, in_=m["x1"],
                                            in_offset=bass.IndirectOffsetOnAxis(ap=ids[0:PC, u, 1:2], axis=0)).then_inc(x_in[u], 16)

                pool.sem_inc(turn_done, 2)
                pool.memset(still[:], 0.0).then_inc(loaded, 1)
                pool.wait_ge(loaded, 17)
                gather(0, 0, 4)
                with pool.Fori(0, EXPERTS // 2) as i:
                    for u in range(2):
                        e = i * 2 + u
                        gather(1 - u, e + 1, 1)
                        pool.wait_ge(ys_ready, e + 2)
                        pool.wait_ge(yp_ready, e + 2)
                        hold(2)
                        pool.indirect_dma_start(out=m["acc"], out_offset=bass.IndirectOffsetOnAxis(ap=ids[:, u, 0:1], axis=0),
                                                in_=ys[:], in_offset=None, compute_op=ALU.add).then_inc(added, 16)
                        pool.indirect_dma_start(out=m["acc"], out_offset=bass.IndirectOffsetOnAxis(ap=ids[0:PC, u, 1:2], axis=0),
                                                in_=yp[:], in_offset=None, compute_op=ALU.add).then_inc(added, 16)
                        pool.wait_ge(added, e * 32 + 32)
                        hold(3).then_inc(turn_done, 1)

            @block.tensor
            def _(pe):
                def turn(u, arrived, first):
                    pe.wait_ge(x_in[u], arrived)
                    for q in range(QUADS):
                        bank = t_ps[q % 2]
                        pe.wait_ge(xT_ready, first + q)
                        for j in range(2):
                            k = q * 2 + j
                            nc.tensor.transpose(bank[:, j * SLOTS:j * SLOTS + SC], xs[u][:, k * P:(k + 1) * P], ident[:])
                            last = nc.tensor.transpose(bank[:, j * SLOTS + SC:(j + 1) * SLOTS], xp[u][:, k * P:(k + 1) * P], ident[0:PC, 0:PC])
                        last.then_inc(turned, 1)

                pe.sem_inc(h_done, KD)
                pe.sem_inc(y_done, 2)
                pe.sem_inc(turned, 2 * QUADS)
                pe.wait_ge(loaded, 16)
                turn(0, 32, 1)
                with pe.Fori(0, EXPERTS // 2) as i:
                    for u in range(2):
                        e = i * 2 + u
                        pe.wait_ge(xT_ready, e * QUADS + QUADS + 2)
                        for f in range(KD):
                            part, col = f // FH, f % FH * P
                            if f % FH == 0:
                                for n in range(2):
                                    pe.wait_ge(w_in[2 * part + n], e * 16 + 16)
                            pe.wait_ge(h_ready, e * KD + f + 1)
                            for n in range(2):
                                for k in range(KD):
                                    at = k * HALF + col
                                    last = nc.tensor.matmul(h_ps[f % 2][:, n * SLOTS:(n + 1) * SLOTS], w[2 * part + n][:, at:at + P],
                                                            xT[:, k, :], start=(k == 0), stop=(k == KD - 1))
                            last.then_inc(h_done, 1)
                        turn(1 - u, i * 32 + 32 + 32 * u, e * QUADS + QUADS + 1)
                        pe.wait_ge(ys_ready, e + 1)
                        pe.wait_ge(yp_ready, e + 1)
                        for f in range(KD):
                            if f % FH == 0:
                                pe.wait_ge(w_in[4 + f // FH], e * 16 + 16)
                            pe.wait_ge(h_ready, e * KD + f + 3)
                            for ps, lo, n in ((y_ps, 0, SC), (yp_ps, SC, PC)):
                                for h in range(2):
                                    at = f % FH * D + h * HALF
                                    last = nc.tensor.matmul(ps[0:n, h * HALF:(h + 1) * HALF], hT[:, f, lo:lo + n], w[4 + f // FH][:, at:at + HALF],
                                                            start=(f == 0), stop=(f == KD - 1))
                            if f % FH == FH - 1:
                                last.then_inc(y_done, 1)

            @block.scalar
            def _(act):
                def turn(first):
                    for q in range(QUADS):
                        act.wait_ge(turned, first + q + 2 * QUADS + 1)
                        nc.scalar.activation(xT[:, 2 * q:2 * q + 2, :], t_ps[q % 2][:, 0:2 * SLOTS].rearrange("p (k n) -> p k n", k=2), ACT.Copy)\
                            .then_inc(xT_ready, 1)

                act.sem_inc(xT_ready, 2)
                act.sem_inc(ys_ready, 1)
                turn(0)
                with act.Fori(0, EXPERTS // 2) as i:
                    for u in range(2):
                        e = i * 2 + u
                        for f in range(KD):
                            act.wait_ge(h_done, e * KD + f + 1 + KD)
                            nc.scalar.activation(sg[:, f % 2, :], h_ps[f % 2][:, 0:SLOTS], ACT.Silu).then_inc(silu_ready, 1)
                        turn(e * QUADS + QUADS)
                        act.wait_ge(y_done, e * 2 + 4)
                        act.wait_ge(turn_done, e + 2)
                        nc.scalar.activation(ys[:], y_ps[:], ACT.Copy, scale=gsel[:, u, 0:1]).then_inc(ys_ready, 1)

            @block.vector
            def _(v):
                def pick(u, e):
                    v.wait_ge(turn_done, e + 1)
                    nc.vector.tensor_copy(gsel[:, u, :], gate_cols[:, :, bass.ds(e, 1)].rearrange("p g o -> p (g o)"))
                    nc.vector.tensor_copy(ids[:, u, :], picks[:, :, bass.ds(e, 1)].rearrange("p g o -> p (g o)")).then_inc(ids_ready, 1)

                v.sem_inc(h_ready, 2)
                v.sem_inc(yp_ready, 1)
                pick(0, 0)
                with v.Fori(0, EXPERTS // 2) as i:
                    for u in range(2):
                        e = i * 2 + u
                        for f in range(KD):
                            v.wait_ge(silu_ready, e * KD + f + 1)
                            nc.vector.tensor_tensor(hT[:, f, :], sg[:, f % 2, :], h_ps[f % 2][:, SLOTS:2 * SLOTS], ALU.mult).then_inc(h_ready, 1)
                            if f == FH:
                                pick(1 - u, e + 1)
                        v.wait_ge(y_done, e * 2 + 4)
                        v.wait_ge(turn_done, e + 2)
                        nc.vector.tensor_scalar(yp[:], yp_ps[0:PC, :], gsel[0:PC, u, 1:2], None, ALU.mult).then_inc(yp_ready, 1)


def project_axial(c, m, keys, values):
    nc = c.nc
    QK = AX_Q + AX_KVD
    HEADS = QK // DH
    NT = (QK + AX_KVD) // P
    with c.stage():
        w = c.sb("w_in", [P, KD, C_IN])
        ident = c.sb("ident", [P, P])
        gain, shift = c.sb("gain", [P, D]), c.sb("shift", [P, D])
        norm2 = c.sb("norm2", [P, 2, DH])
        norm = c.sb("norm", [P, HEADS, DH])
        r = c.sb("r", [P, 2, D])
        rope = c.sb("rope", [P, 2, 2 * DH])
        x2 = c.sb("x2", [P, 2, D])
        stats, mv = c.sb("stats", [P, 12]), c.sb("mv", [P, 4])
        half = c.sb("minus_half", [P, HEADS])
        ms = c.sb("ms", [P, 2, HEADS])
        xT = c.sb("xT", [P, 2, D])
        qk = c.sb("qk", [P, 2, QK + AX_KVD])
        ra, rb = c.sb("ra", [P, HEADS, DH]), c.sb("rb", [P, HEADS, DH])
        qT = c.sb("qT", [P, 2, AX_Q])
        xT_ps, qkv_ps, qkT_ps = c.ps("xT_ps", D), c.ps("qkv_ps", C_IN), c.ps("qkT_ps", NT * P)
        w_in, r_in, x2_out, q_out = c.sem("w_in"), [c.sem("r_in0"), c.sem("r_in1")], [c.sem("x2_out0"), c.sem("x2_out1")], [c.sem("q_out0"), c.sem("q_out1")]
        const, dve, var_ready, rstd_ready, x2_ready, xT_done, xT_ready, qkv_done, copied, squared, ms_ready, rms_ready, qk_ready, qkT_done, qT_ready, k_ready = (
            c.sem(n) for n in ("const", "dve", "var_ready", "rstd_ready", "x2_ready", "xT_done", "xT_ready", "qkv_done", "copied",
                               "squared", "ms_ready", "rms_ready", "qk_ready", "qkT_done", "qT_ready", "k_ready"))
        turns = TILES // 2
        with c.block() as block:

            @block.sync
            def _(sp):
                sp.dma_start(gain[:], row_broadcast(m["ln2_g"][0])).then_inc(w_in, 16)
                sp.dma_start(shift[:], row_broadcast(m["ln2_b"][0])).then_inc(w_in, 16)
                sp.dma_start(norm2[:, 0, :], row_broadcast(m["c_q_norm"][0])).then_inc(w_in, 16)
                sp.dma_start(norm2[:, 1, :], row_broadcast(m["c_k_norm"][0])).then_inc(w_in, 16)
                sp.dma_start(ident[:], m["ident"]).then_inc(w_in, 16)
                sp.dma_start(w[:], m["c_w_in"][0].rearrange("(k p) n -> p k n", p=P)).then_inc(w_in, 16)
                with sp.Fori(0, turns) as i:
                    for u in range(2):
                        t = i * 2 + u
                        sp.wait_ge(x2_ready, t + 1)
                        sp.wait_ge(qk_ready, t + 1)
                        sp.dma_start(r[:, u, :], m["acc"][bass.ds(t * P, P), :]).then_inc(r_in[u], 16)
                        sp.dma_start(rope[:, u, :], m["rope_c"][bass.ds(t * P, P), :]).then_inc(r_in[u], 16)

            @block.gpsimd
            def _(pool):
                pool.memset(half[:], -0.5).then_inc(const, 1)
                pool.wait_ge(const, 1)
                with pool.Fori(0, turns) as i:
                    for u in range(2):
                        t = i * 2 + u
                        pool.wait_ge(var_ready, t + 1)
                        pool.tensor_tensor(mv[:, 3:4], mv[:, 2:3], half[:, 0:1], ALU.pow).then_inc(rstd_ready, 1)
                        pool.wait_ge(ms_ready, t + 1)
                        pool.tensor_tensor(ms[:, 1, :], ms[:, 0, :], half[:], ALU.pow).then_inc(rms_ready, 1)

            @block.tensor
            def _(pe):
                pe.wait_ge(w_in, 96)
                with pe.Fori(0, turns) as i:
                    for u in range(2):
                        t = i * 2 + u
                        pe.wait_ge(x2_ready, t + 3)
                        pe.wait_ge(xT_ready, t + 1)
                        for k in range(KD):
                            last = nc.tensor.transpose(xT_ps[:, k * P:(k + 1) * P], x2[:, u, k * P:(k + 1) * P], ident[:])
                        last.then_inc(xT_done, 1)
                        pe.wait_ge(xT_ready, t + 2)
                        pe.wait_ge(copied, t + 1)
                        for n in range(C_IN // HALF):
                            for k in range(KD):
                                last = nc.tensor.matmul(qkv_ps[:, n * HALF:(n + 1) * HALF], xT[:, u, k * P:(k + 1) * P],
                                                        w[:, k, n * HALF:(n + 1) * HALF], start=(k == 0), stop=(k == KD - 1))
                        last.then_inc(qkv_done, 1)
                        if u == 1:
                            for b in range(2):
                                tb = i * 2 + b
                                pe.wait_ge(qk_ready, tb + 3)
                                pe.wait_ge(qT_ready, tb + 1)
                                pe.wait_ge(k_ready, tb + 1)
                                for j in range(NT):
                                    last = nc.tensor.transpose(qkT_ps[:, j * P:(j + 1) * P], qk[:, b, j * P:(j + 1) * P], ident[:])
                                last.then_inc(qkT_done, 1)

            @block.scalar
            def _(act):
                act.sem_inc(xT_ready, 1)
                act.sem_inc(copied, 1)
                act.sem_inc(qT_ready, 1)
                for u in range(2):
                    act.sem_inc(x2_out[u], 16)
                    act.sem_inc(q_out[u], 16)
                with act.Fori(0, turns) as i:
                    for u in range(2):
                        t = i * 2 + u
                        act.wait_ge(x2_ready, t + 3)
                        act.dma_start(m["x2"][bass.ds(t * P, P), :], x2[:, u, :]).then_inc(x2_out[u], 16)
                        act.wait_ge(xT_done, t + 3)
                        nc.scalar.activation(xT[:, u, :], xT_ps[:], ACT.Copy).then_inc(xT_ready, 1)
                        act.wait_ge(qkv_done, t + 1)
                        act.wait_ge(qkT_done, t + 1)
                        nc.scalar.activation(values[:, bass.ds(t, 1), :], qkv_ps[:, QK:C_IN].rearrange("p (o n) -> p o n", o=1), ACT.Copy)
                        nc.scalar.activation(qk[:, u, 0:QK], qkv_ps[:, 0:QK], ACT.Copy).then_inc(copied, 1)
                        act.wait_ge(copied, t + 2)
                        act.wait_ge(qk_ready, t + 2)
                        nc.scalar.activation(ra[:].rearrange("p h d -> p (h d)"), qk[:, u, 0:QK], ACT.Square).then_inc(squared, 1)
                    for b in range(2):
                        tb = i * 2 + b
                        act.wait_ge(qkT_done, tb + 3)
                        act.wait_ge(q_out[b], i * 16 + 16)
                        nc.scalar.activation(qT[:, b, :], qkT_ps[:, 0:AX_Q], ACT.Copy).then_inc(qT_ready, 1)
                        act.wait_ge(qT_ready, tb + 2)
                        act.dma_start(m["qT"][bass.ds(tb * P, P), :], qT[:, b, :]).then_inc(q_out[b], 16)
                for u in range(2):
                    act.wait_ge(x2_out[u], 16 * turns + 16)
                    act.wait_ge(q_out[u], 16 * turns + 16)

            @block.vector
            def _(v):
                s = Steps(v, dve)
                s.add(nc.vector.memset(keys[:], 0.0))
                v.wait_ge(w_in, 96)
                s.add(nc.vector.tensor_copy(norm[:, 0:AX_H, :], norm2[:, 0:1, :].to_broadcast([P, AX_H, DH])))
                s.link(nc.vector.tensor_copy(norm[:, AX_H:HEADS, :], norm2[:, 1:2, :].to_broadcast([P, AX_KV, DH])))
                v.sem_inc(x2_ready, 2)
                v.sem_inc(qk_ready, 2)
                v.sem_inc(xT_done, 2)
                v.sem_inc(qkT_done, 2)
                v.sem_inc(k_ready, 1)
                with s.loop(turns, 2 * (5 + 11)) as i:
                    for u in range(2):
                        t = i * 2 + u
                        v.wait_ge(r_in[u], i * 32 + 32)
                        v.wait_ge(x2_out[u], i * 16 + 16)
                        v.wait_ge(xT_done, t + 1)
                        layer_norm_rows(nc, s, r[:, u, :], x2[:, u, :], stats, mv, gain[:], shift[:], var_ready, rstd_ready, t).then_inc(x2_ready, 1)
                        v.wait_ge(squared, t + 1)
                        heads = qk[:, u, 0:QK].rearrange("p (h d) -> p h d", d=DH)
                        s.link(nc.vector.tensor_reduce(ms[:, 0, :], ra[:], AX.X, ALU.add))
                        nc.vector.tensor_scalar(ms[:, 0, :], ms[:, 0, :], 1.0 / DH, RMS_EPS, ALU.mult, ALU.add).then_inc(ms_ready, 1)
                        v.wait_ge(rms_ready, t + 1)
                        s.link(nc.vector.tensor_tensor(heads, heads, ms[:, 1, :].rearrange("p (h o) -> p h o", o=1).to_broadcast([P, HEADS, DH]), ALU.mult))
                        s.link(nc.vector.tensor_tensor(heads, heads, norm[:], ALU.mult))
                        cos = rope[:, u, 0:DH].rearrange("p (o n) -> p o n", o=1).to_broadcast([P, HEADS, DH])
                        s.add(nc.vector.tensor_tensor(ra[:], heads, cos, ALU.mult))
                        for axis in range(2):
                            lo = axis * DH // 2
                            mid, hi = lo + DH // 4, lo + DH // 2
                            for a, b, x, y in ((lo, mid, mid, hi), (mid, hi, lo, mid)):
                                sin = rope[:, u, DH + a:DH + b].rearrange("p (o n) -> p o n", o=1).to_broadcast([P, HEADS, b - a])
                                s.add(nc.vector.tensor_tensor(rb[:, :, a:b], heads[:, :, x:y], sin, ALU.mult))
                        s.settle()
                        s.link(nc.vector.tensor_tensor(heads, ra[:], rb[:], ALU.add))
                        k = qk[:, u, AX_Q:AX_Q + 2 * AX_KVD].rearrange("p (j h d) -> p j h d", j=4, d=DH)
                        s.link(nc.vector.tensor_copy(k[:, 2, :, :], k[:, 1, :, :]))
                        s.add(nc.vector.tensor_copy(k[:, 1, 0, :], k[:, 0, 1, :]))
                        nc.vector.tensor_copy(k[:, 1, 1, :], k[:, 0, 0, :])
                        nc.vector.tensor_copy(k[:, 3, 0, :], k[:, 2, 1, :])
                        nc.vector.tensor_copy(k[:, 3, 1, :], k[:, 2, 0, :]).then_inc(qk_ready, 1)
                    for b in range(2):
                        tb = i * 2 + b
                        v.wait_ge(qkT_done, tb + 3)
                        kT = qkT_ps[:, AX_Q:NT * P].rearrange("p (j n) -> p j n", j=4)
                        nc.vector.tensor_copy(keys[0:DH, 0:AX_KV, bass.ds(tb * P, P)], kT[0:DH])
                        nc.vector.tensor_copy(keys[DH:P, AX_KV:2 * AX_KV, bass.ds(tb * P, P)], kT[DH:P]).then_inc(k_ready, 1)


def axial_attention(c, m, keys, values, cat):
    nc = c.nc
    LAST = 2 * AX_H - 1
    NB = 4
    with c.stage():
        ident = c.sb("ident", [P, P])
        q = c.sb("q", [P, 2, AX_Q])
        p = c.sb("p", [P, NB, SEQ[1]])
        pT = c.sb("pT", [P, NB, SEQ[1]])
        col = c.sb("col", [P, NB, 4])
        s_ps, t_ps, o_ps = [c.ps("s_ps0", SEQ[1]), c.ps("s_ps1", SEQ[1])], c.ps("t_ps", SEQ[1]), c.ps("o_ps", D)
        loaded, q_in = c.sem("loaded"), [c.sem("q_in0"), c.sem("q_in1")]
        dve, scores, bias, expd, p_ready, pT_done, pT_act, pT_dve, pv_done, o_out = (
            c.sem(n) for n in ("dve", "scores", "bias", "expd", "p_ready", "pT_done", "pT_act", "pT_dve", "pv_done", "o_out"))

        def place(kv, half):
            return kv if half == 0 else AX_KV + (kv ^ 1)

        with c.block() as block:

            @block.sync
            def _(sp):
                sp.dma_start(ident[:], m["ident"]).then_inc(loaded, 16)
                with sp.Fori(0, TILES // 2) as i:
                    for u in range(2):
                        t = i * 2 + u
                        sp.wait_ge(scores, t * AX_H + AX_H)
                        sp.dma_start(q[:, u, :], m["qT"][bass.ds(t * P, P), :]).then_inc(q_in[u], 16)

            @block.tensor
            def _(pe):
                pe.sem_inc(scores, 2 * AX_H)
                pe.sem_inc(pT_done, NB)
                pe.wait_ge(loaded, 16)
                for g in range(len(SEQ)):
                    nk, first = SEQ[g], GROUP_FIRST[g]
                    with pe.Fori(0, GROUP_TILES[g] // 2) as i:
                        U = i * (2 * AX_H) + first * AX_H

                        def qk(n):
                            u, h = n // AX_H, n % AX_H
                            if h == 0:
                                pe.wait_ge(q_in[u], i * 16 + first * 8 + 16)
                            pe.wait_ge(expd, U + n + 1)
                            for b in range(nk // HALF):
                                at = first * P + b * HALF
                                last = nc.tensor.matmul(s_ps[n % 2][:, b * HALF:(b + 1) * HALF], q[:, u, (h // 2) * P:(h // 2 + 1) * P],
                                                        keys[:, place(h // 4, h % 2), at:at + HALF], start=True, stop=True)
                            last.then_inc(scores, 1)

                        def turn(n):
                            pe.wait_ge(p_ready, U + n + 1)
                            pe.wait_ge(pT_act, U + n + 1)
                            pe.wait_ge(pT_dve, U + n + 1)
                            for k in range(nk // P):
                                at = k // (nk // P // 2) * HALF + k % (nk // P // 2) * P
                                last = nc.tensor.transpose(t_ps[:, at:at + P], p[:, n % NB, k * P:(k + 1) * P], ident[:])
                            last.then_inc(pT_done, 1)

                        def pv(n):
                            pe.wait_ge(pT_act, U + n + 2)
                            pe.wait_ge(pT_dve, U + n + 2)
                            u, h = n // AX_H, n % AX_H
                            if h == 1:
                                pe.wait_ge(o_out, i * 2 + first + u + 1)
                            pair, kv = h // 2, h // 4
                            for k in range(nk // P):
                                for side in range(2):
                                    last = nc.tensor.matmul(o_ps[DH * side:DH * side + DH, pair * P:(pair + 1) * P],
                                                            values[:, first + k, kv * DH:(kv + 1) * DH],
                                                            pT[:, (n - 1 + side) % NB, k * P:(k + 1) * P], start=(k == 0), stop=(k == nk // P - 1))
                            last.then_inc(pv_done, 1)

                        qk(0)
                        for n in range(LAST + 1):
                            if n < LAST:
                                qk(n + 1)
                            turn(n)
                            if n % 2 == 0 and n:
                                pv(n - 1)
                        pv(LAST)

            @block.vector
            def _(v):
                s = Steps(v, dve)
                v.sem_inc(pT_dve, 1)
                for g in range(len(SEQ)):
                    nk, first = SEQ[g], GROUP_FIRST[g]
                    with s.loop(GROUP_TILES[g] // 2, 2 * (LAST + 1)) as i:
                        U = i * (2 * AX_H) + first * AX_H

                        def top(n):
                            b = n % NB
                            v.wait_ge(scores, U + n + 1 + 2 * AX_H)
                            s.link(nc.vector.tensor_reduce(col[:, b, 0:1], s_ps[n % 2][:, 0:nk], AX.X, ALU.max, negate=True))
                            nc.vector.tensor_scalar(col[:, b, 1:2], col[:, b, 0:1], SCALE, None, ALU.mult).then_inc(bias, 1)

                        def norm(n):
                            b = n % NB
                            v.wait_ge(expd, U + n + 3)
                            s.link(nc.vector.reciprocal(col[:, b, 3:4], col[:, b, 2:3]))
                            nc.vector.tensor_scalar(p[:, b, 0:nk], p[:, b, 0:nk], col[:, b, 3:4], None, ALU.mult).then_inc(p_ready, 1)

                        def copy(n):
                            v.wait_ge(pT_done, U + n + 1 + NB)
                            nc.vector.tensor_copy(pT[:, n % NB, nk // 2:nk], t_ps[:, HALF:HALF + nk // 2]).then_inc(pT_dve, 1)

                        top(0)
                        for n in range(LAST + 1):
                            if n < LAST:
                                top(n + 1)
                            norm(n)
                            if n:
                                copy(n - 1)
                        copy(LAST)

            @block.scalar
            def _(act):
                act.sem_inc(expd, 2)
                act.sem_inc(pT_act, 1)
                act.sem_inc(o_out, 1)
                for g in range(len(SEQ)):
                    nk, first = SEQ[g], GROUP_FIRST[g]
                    with act.Fori(0, GROUP_TILES[g] // 2) as i:
                        U = i * (2 * AX_H) + first * AX_H

                        def exps(n):
                            b = n % NB
                            act.wait_ge(bias, U + n + 1)
                            act.wait_ge(pT_done, U + n + 1)
                            nc.scalar.activation(p[:, b, 0:nk], s_ps[n % 2][:, 0:nk], ACT.Exp, bias=col[:, b, 1:2], scale=SCALE,
                                                 accum_out=col[:, b, 2:3]).then_inc(expd, 1)

                        def copy(n):
                            act.wait_ge(pT_done, U + n + 1 + NB)
                            nc.scalar.activation(pT[:, n % NB, 0:nk // 2], t_ps[:, 0:nk // 2], ACT.Copy).then_inc(pT_act, 1)

                        def out(u):
                            act.wait_ge(pv_done, i * AX_H + first * 8 + (u + 1) * 8)
                            nc.scalar.activation(cat[:, :, bass.ds(i * 2 * P + (first + u) * P, P)], o_ps[:].rearrange("p (k n) -> p k n", k=KD), ACT.Copy)\
                                .then_inc(o_out, 1)

                        exps(0)
                        for n in range(LAST + 1):
                            if n < LAST:
                                exps(n + 1)
                            copy(n)
                            if n == AX_H:
                                out(0)
                        out(1)


def final_norm(c, m):
    nc = c.nc
    with c.stage():
        gain, shift = c.sb("gain", [P, D]), c.sb("shift", [P, D])
        r, y = c.sb("r", [P, 2, D]), c.sb("y", [P, 2, D])
        stats, mv, half = c.sb("stats", [P, 12]), c.sb("mv", [P, 4]), c.sb("minus_half", [P, 1])
        loaded, r_in, y_out = c.sem("loaded"), [c.sem("r_in0"), c.sem("r_in1")], [c.sem("y_out0"), c.sem("y_out1")]
        dve, var_ready, rstd_ready, y_ready, const = (c.sem(n) for n in ("dve", "var_ready", "rstd_ready", "y_ready", "const"))
        turns = TILES // 2
        with c.block() as block:

            @block.sync
            def _(sp):
                sp.dma_start(gain[:], row_broadcast(m["ln2_g"][1])).then_inc(loaded, 16)
                sp.dma_start(shift[:], row_broadcast(m["ln2_b"][1])).then_inc(loaded, 16)
                sp.sem_inc(y_ready, 2)
                with sp.Fori(0, turns) as i:
                    for u in range(2):
                        sp.wait_ge(y_ready, i * 2 + u + 1)
                        sp.dma_start(r[:, u, :], m["acc"][bass.ds(i * 2 * P + u * P, P), :]).then_inc(r_in[u], 16)

            @block.gpsimd
            def _(pool):
                pool.memset(half[:], -0.5).then_inc(const, 1)
                pool.wait_ge(const, 1)
                with pool.Fori(0, TILES) as t:
                    pool.wait_ge(var_ready, t + 1)
                    pool.tensor_tensor(mv[:, 3:4], mv[:, 2:3], half[:], ALU.pow).then_inc(rstd_ready, 1)

            @block.vector
            def _(v):
                s = Steps(v, dve)
                v.wait_ge(loaded, 32)
                with s.loop(turns, 2 * 5) as i:
                    for u in range(2):
                        t = i * 2 + u
                        v.wait_ge(r_in[u], i * 16 + 16)
                        v.wait_ge(y_out[u], i * 16 + 16)
                        layer_norm_rows(nc, s, r[:, u, :], y[:, u, :], stats, mv, gain[:], shift[:], var_ready, rstd_ready, t).then_inc(y_ready, 1)

            @block.scalar
            def _(act):
                for u in range(2):
                    act.sem_inc(y_out[u], 16)
                with act.Fori(0, turns) as i:
                    for u in range(2):
                        act.wait_ge(y_ready, i * 2 + u + 3)
                        act.dma_start(m["y"][bass.ds(i * 2 * P + u * P, P), :], y[:, u, :]).then_inc(y_out[u], 16)
                for u in range(2):
                    act.wait_ge(y_out[u], 16 * turns + 16)


def trunk(nc, m, stop=99):
    m = dict(m)
    for name in ("x1", "x2", "acc", "qT"):
        m[name] = nc.dram_tensor(f"rows_{name}", (TOK, D), F32).ap()
    c = Core(nc)
    with c.stage():
        gates, rows = c.sb("gates", [P, 2 * PROMPT_ROW]), c.sb("rows", [P, 2 * PROMPT_ROW], U32)
        affinity = c.sb("affinity", [EXPERTS, TOK])
        with c.stage():
            cat = c.sb("cat", [P, KD, TOK])
            with c.stage():
                keys, values = c.sb("keys", [P, 2 * WIN_KV, TOK + 2 * P]), c.sb("values", [P, TILES + 2, WIN_KVD])
                glu = c.sb("glu", [P, CT, TOK])
                project_conv_window(c, m, glu, keys, values)
                if stop > 1: window_attention(c, m, keys, values, cat)
                if stop > 2: convolve(c, m, glu, cat)
            if stop > 3: project_out(c, m, 0, m["ab_w_out"][0], m["x"], cat, affinity)
        if stop > 4: choose(c, m, affinity, gates, rows)
        if stop > 5: experts(c, m, 0, gates, rows)
        with c.stage():
            if stop > 6:
                keys, values = c.sb("keys", [P, 2 * AX_KV, TOK]), c.sb("values", [P, TILES, AX_KVD])
                project_axial(c, m, keys, values)
            if stop > 7:
                cat = c.sb("cat", [P, KD, TOK])
                axial_attention(c, m, keys, values, cat)
            if stop > 8: project_out(c, m, 1, m["c_w_out"][0], m["x2"], cat, affinity)
        if stop > 9: choose(c, m, affinity, gates, rows)
        if stop > 10: experts(c, m, 1, gates, rows)
        if stop > 11: final_norm(c, m)


def host_arrays(inputs):
    f32 = np.float32
    a = {n: np.ascontiguousarray(inputs[n]) for n in
         ("ab_w_in", "ab_sink", "ab_w_out", "c_w_in", "c_q_norm", "c_k_norm", "c_w_out", "ln1_g", "ln1_b",
          "moe_router", "moe_w_gate", "moe_w_up", "moe_w_down", "ln2_g", "ln2_b")}
    a["x"] = np.concatenate([np.asarray(inputs["x_prompt"]).reshape(-1, D), np.asarray(inputs["x_sample"]).reshape(-1, D)])
    a["conv_w"] = np.ascontiguousarray(np.asarray(inputs["ab_conv_w"])[0].reshape(TAPS, CT, P).transpose(2, 1, 0))
    for n, name in (("conv_b", "ab_conv_b"), ("conv_g", "ab_conv_ln_g"), ("conv_beta", "ab_conv_ln_b")):
        a[n] = np.ascontiguousarray(np.asarray(inputs[name])[0].reshape(CT, P).T)
    a["ident"] = np.eye(P, dtype=f32)
    pos = np.concatenate([np.arange(n) for n in SEQ])

    def angles(at, dim, theta):
        inv = f32(theta) ** (-np.arange(0, dim, 2, dtype=f32) / f32(dim))
        return at.astype(f32)[:, None] * inv[None, :]

    def table(*ang):
        cos = np.concatenate([np.concatenate([np.cos(x), np.cos(x)], 1) for x in ang], 1)
        sin = np.concatenate([np.concatenate([-np.sin(x), np.sin(x)], 1) for x in ang], 1)
        return np.concatenate([cos, sin], 1).astype(f32)

    a["rope_b"] = table(angles(pos, ROT, 500000.0))
    a["rope_c"] = table(angles(pos // GRID_W, DH // 2, 10000.0), angles(pos % GRID_W, DH // 2, 10000.0))
    mask = np.zeros((TILES, P, 3 * P), f32)
    for g, n in enumerate(SEQ):
        for b in range(n // P):
            qpos = b * P + np.arange(P)[:, None]
            kpos = (b - 1) * P + np.arange(3 * P)[None, :]
            mask[GROUP_FIRST[g] + b] = np.where((np.abs(kpos - qpos) <= P) & (kpos >= 0) & (kpos < n), 0.0, MASKED)
    a["mask"] = mask.reshape(TILES * P, 3 * P)
    return a


def kernel(**inputs):
    import concourse.bacc as bacc
    from concourse.bass_utils import run_bass_kernel_spmd

    nc = bacc.Bacc("TRN2", target_bir_lowering=False, num_devices=1)
    arrays = host_arrays(inputs)
    m = {n: nc.dram_tensor(n, a.shape, mybir.dt.from_np(a.dtype), kind="ExternalInput").ap() for n, a in arrays.items()}
    m["y"] = nc.dram_tensor("y", (TOK, D), F32, kind="ExternalOutput").ap()
    trunk(nc, m)
    y = run_bass_kernel_spmd(nc, [arrays], core_ids=[0]).results[0]["y"]
    return y[:SEQ[0]].reshape(1, SEQ[0], D), y[SEQ[0]:].reshape(1, SEQ[1], D)
```

```python
from contextlib import ExitStack, contextmanager

import numpy as np

import concourse.bass as bass
from concourse import mybir

P = 128
D = 1024
KD = D // P
SEQ = (512, 1024)
GROUP_TILES = tuple(s // P for s in SEQ)
GROUP_FIRST = (0, GROUP_TILES[0])
TILES = sum(GROUP_TILES)
TOK = TILES * P
HALF = 512
DEPTH = 2
DH = 64
CONV = 512
CT = CONV // P
TAPS = 31
WIN_H, WIN_KV = 8, 2
WIN_Q, WIN_KVD = WIN_H * DH, WIN_KV * DH
AB_IN = 2 * CONV + WIN_Q + 2 * WIN_KVD
ROT = DH // 4
AX_H, AX_KV = 16, 4
AX_Q, AX_KVD = AX_H * DH, AX_KV * DH
C_IN = AX_Q + 2 * AX_KVD
GRID_W = 64
EXPERTS = 16
CAP = tuple(2 * s // EXPERTS for s in SEQ)
SLOTS = sum(CAP)
ALPHA = (2 * DEPTH) ** 0.25
SCALE = DH ** -0.5
LN_EPS = 1e-5
RMS_EPS = 1e-6
MASKED = -1.0e30
PROMPT_ROW = 32

F32 = mybir.dt.float32
F32R = mybir.dt.float32r
U32 = mybir.dt.uint32
ALU = mybir.AluOpType
ACT = mybir.ActivationFunctionType
AX = mybir.AxisListType


class Steps:

    def __init__(self, eng, sem):
        self.eng, self.sem, self.base, self.here = eng, sem, 0, 0

    def add(self, instruction):
        instruction.then_inc(self.sem, 1)
        self.here += 1
        return self.base + self.here

    def settle(self):
        self.eng.wait_ge(self.sem, self.base + self.here)

    def link(self, instruction):
        self.add(instruction)
        self.settle()

    @contextmanager
    def loop(self, turns, each):
        start = self.base + self.here
        with self.eng.Fori(0, turns) as i:
            self.base, self.here = start + i * each, 0
            yield i
            assert self.here == each, (self.here, each)
        self.base, self.here = start + turns * each, 0


class Core:

    def __init__(self, nc):
        self.nc, self.count, self.stack, self.sems = nc, 0, None, None

    @contextmanager
    def stage(self):
        outer = self.stack, self.sems
        self.sems = []
        with ExitStack() as self.stack:
            yield
            if self.sems:
                self.nc.clear_and_free_semaphores(self.sems)
                self.nc.all_engine_barrier()
        self.stack, self.sems = outer

    def sb(self, name, shape, dt=F32):
        self.count += 1
        return self.stack.enter_context(self.nc.sbuf_tensor(f"{name}_{self.count}", shape, dt))

    def ps(self, name, cols):
        self.count += 1
        return self.stack.enter_context(self.nc.psum_tensor(f"{name}_{self.count}", [P, cols], F32))

    def sem(self, name):
        self.count += 1
        self.sems.append(self.nc.alloc_semaphore(f"{name}_{self.count}"))
        return self.sems[-1]

    def block(self):
        return self.nc.Block()


def row_broadcast(vector, parts=P):
    return vector.rearrange("(o n) -> o n", o=1).to_broadcast([parts, vector.shape[0]])


def layer_norm_rows(nc, steps, row, out, stats, mv, gain, shift, var_ready, rstd_ready, tile):
    n = row.shape[1] // HALF
    for h in range(n):
        steps.add(nc.vector.bn_stats(stats[:, 6 * h:6 * h + 6], row[:, h * HALF:(h + 1) * HALF]))
    steps.settle()
    nc.vector.memset(mv[:, 2:3], 0.0)
    steps.link(nc.vector.bn_aggr(mv[:, 0:2], stats[:, 0:6 * n]))
    nc.vector.tensor_scalar(mv[:, 2:3], mv[:, 1:2], LN_EPS, None, ALU.add).then_inc(var_ready, 1)
    steps.eng.wait_ge(rstd_ready, tile + 1)
    steps.link(nc.vector.tensor_scalar(out, row, mv[:, 0:1], mv[:, 3:4], ALU.subtract, ALU.mult))
    steps.link(nc.vector.tensor_tensor(out, out, gain, ALU.mult))
    return nc.vector.tensor_tensor(out, out, shift, ALU.add)


def project_conv_window(c, m, glu, keys, values):
    nc = c.nc
    QK = WIN_Q + WIN_KVD
    QK2 = QK + WIN_KVD
    with c.stage():
        w = c.sb("w_in", [P, KD, AB_IN])
        ident = c.sb("ident", [P, P])
        x = c.sb("x", [P, 2, D])
        rope = c.sb("rope", [P, 2, 2 * ROT])
        xT = c.sb("xT", [P, 2, D])
        sig = c.sb("sig", [P, 2, CONV])
        qk = c.sb("qk", [P, 2, QK2])
        ra = c.sb("ra", [P, QK // DH, ROT])
        rb = c.sb("rb", [P, QK // DH, ROT])
        qT = c.sb("qT", [P, 2, WIN_Q])
        xT_ps, ug_ps, qkv_ps, qkT_ps = (c.ps(n, 1024) for n in ("xT_ps", "ug_ps", "qkv_ps", "qkT_ps"))
        w_in, x_in = c.sem("w_in"), [c.sem("x_in0"), c.sem("x_in1")]
        xT_done, xT_ready, ug_done, sig_ready = c.sem("xT_done"), c.sem("xT_ready"), c.sem("ug_done"), c.sem("sig_ready")
        glu_ready, qkv_done, qk_ready, qkT_done = c.sem("glu_ready"), c.sem("qkv_done"), c.sem("qk_ready"), c.sem("qkT_done")
        qT_ready, k_ready, q_stored = c.sem("qT_ready"), c.sem("k_ready"), [c.sem("q_out0"), c.sem("q_out1")]
        dve, zero = c.sem("dve"), c.sem("zero")
        with c.block() as block:

            @block.sync
            def _(sp):
                sp.dma_start(ident[:], m["ident"]).then_inc(w_in, 16)
                win = m["ab_w_in"][0].rearrange("(k p) n -> p k n", p=P)
                sp.dma_start(w[:, :, 2 * CONV:AB_IN], win[:, :, 2 * CONV:AB_IN]).then_inc(w_in, 16)
                sp.dma_start(w[:, :, 0:2 * CONV], win[:, :, 0:2 * CONV]).then_inc(w_in, 16)
                with sp.Fori(0, TILES // 2) as i:
                    for u in range(2):
                        t = i * 2 + u
                        sp.wait_ge(xT_done, t + 1)
                        sp.wait_ge(qk_ready, t + 1)
                        sp.dma_start(x[:, u, :], m["x"][bass.ds(t * P, P), :]).then_inc(x_in[u], 16)
                        sp.dma_start(rope[:, u, :], m["rope_b"][bass.ds(t * P, P), :]).then_inc(x_in[u], 16)

            @block.tensor
            def _(pe):
                pe.sem_inc(xT_done, 2)
                pe.wait_ge(w_in, 48)
                with pe.Fori(0, TILES // 2) as i:
                    for u in range(2):
                        t = i * 2 + u
                        pe.wait_ge(x_in[u], i * 32 + 32)
                        pe.wait_ge(xT_ready, t + 1)
                        for k in range(KD):
                            last = nc.tensor.transpose(xT_ps[:, k * P:(k + 1) * P], x[:, u, k * P:(k + 1) * P], ident[:])
                        last.then_inc(xT_done, 1)
                        pe.wait_ge(xT_ready, t + 2)
                        pe.wait_ge(qk_ready, t + 2)
                        for base, cols in ((0, WIN_Q), (WIN_Q, 2 * WIN_KVD)):
                            for k in range(KD):
                                last = nc.tensor.matmul(qkv_ps[:, base:base + cols], xT[:, u, k * P:(k + 1) * P],
                                                        w[:, k, 2 * CONV + base:2 * CONV + base + cols],
                                                        start=(k == 0), stop=(k == KD - 1))
                        last.then_inc(qkv_done, 1)
                        pe.wait_ge(glu_ready, t + 1)
                        for ct in range(2 * CT):
                            for k in range(KD):
                                last = nc.tensor.matmul(ug_ps[:, ct * P:(ct + 1) * P], w[:, k, ct * P:(ct + 1) * P],
                                                        xT[:, u, k * P:(k + 1) * P], start=(k == 0), stop=(k == KD - 1))
                        last.then_inc(ug_done, 1)
                        pe.wait_ge(qk_ready, t + 3)
                        pe.wait_ge(k_ready, t + 1)
                        for j in range(QK2 // P):
                            last = nc.tensor.transpose(qkT_ps[:, j * P:(j + 1) * P], qk[:, u, j * P:(j + 1) * P], ident[:])
                        last.then_inc(qkT_done, 1)

            @block.scalar
            def _(act):
                act.sem_inc(xT_ready, 1)
                act.sem_inc(k_ready, 1)
                for u in range(2):
                    act.sem_inc(q_stored[u], 16)
                with act.Fori(0, TILES // 2) as i:
                    for u in range(2):
                        t = i * 2 + u
                        act.wait_ge(xT_done, t + 3)
                        nc.scalar.activation(xT[:, u, :], xT_ps[:], ACT.Copy).then_inc(xT_ready, 1)
                        act.wait_ge(ug_done, t + 1)
                        nc.scalar.activation(sig[:, u, :], ug_ps[:, CONV:2 * CONV], ACT.Sigmoid).then_inc(sig_ready, 1)
                        act.wait_ge(qkT_done, t + 1)
                        act.wait_ge(q_stored[u], i * 16 + 16)
                        nc.scalar.activation(qT[:, u, :], qkT_ps[:, 0:WIN_Q], ACT.Copy).then_inc(qT_ready, 1)
                        act.wait_ge(qT_ready, t + 1)
                        act.dma_start(m["qT"][bass.ds(t * P, P), 0:WIN_Q], qT[:, u, :]).then_inc(q_stored[u], 16)
                        act.wait_ge(zero, 2)
                        at = bass.ds((t + 1) * P, P)
                        kT = qkT_ps[:, WIN_Q:QK2].rearrange("p (j n) -> p j n", j=WIN_KV)
                        nc.scalar.activation(keys[0:DH, 0:WIN_KV, at], kT[0:DH], ACT.Copy)
                        nc.scalar.activation(keys[DH:P, WIN_KV:2 * WIN_KV, at], kT[DH:P], ACT.Copy).then_inc(k_ready, 1)
                for u in range(2):
                    act.wait_ge(q_stored[u], 16 * (TILES // 2) + 16)

            @block.vector
            def _(v):
                s = Steps(v, dve)
                nc.vector.memset(keys[:], 0.0).then_inc(zero, 1)
                nc.vector.memset(values[:], 0.0).then_inc(zero, 1)
                v.wait_ge(zero, 2)
                v.sem_inc(qk_ready, 2)
                v.sem_inc(glu_ready, 1)
                heads = QK // DH
                with s.loop(TILES // 2, 2 * 7) as i:
                    for u in range(2):
                        t = i * 2 + u
                        v.wait_ge(qkv_done, t + 1)
                        v.wait_ge(xT_done, t + 3)
                        s.add(nc.vector.tensor_copy(values[:, bass.ds(t + 1, 1), :], qkv_ps[:, QK:QK + WIN_KVD].rearrange("p (o n) -> p o n", o=1)))
                        s.link(nc.vector.tensor_copy(qk[:, u, 0:QK], qkv_ps[:, 0:QK]))
                        v.wait_ge(x_in[u], i * 32 + 32)
                        rot = qk[:, u, 0:QK].rearrange("p (h d) -> p h d", d=DH)
                        cos = rope[:, u, 0:ROT].rearrange("p (o n) -> p o n", o=1).to_broadcast([P, heads, ROT])
                        h2 = ROT // 2
                        s0 = rope[:, u, ROT:ROT + h2].rearrange("p (o n) -> p o n", o=1).to_broadcast([P, heads, h2])
                        s1 = rope[:, u, ROT + h2:2 * ROT].rearrange("p (o n) -> p o n", o=1).to_broadcast([P, heads, h2])
                        s.add(nc.vector.tensor_tensor(ra[:], rot[:, :, 0:ROT], cos, ALU.mult))
                        s.add(nc.vector.tensor_tensor(rb[:, :, 0:h2], rot[:, :, h2:ROT], s0, ALU.mult))
                        s.add(nc.vector.tensor_tensor(rb[:, :, h2:ROT], rot[:, :, 0:h2], s1, ALU.mult))
                        s.settle()
                        s.link(nc.vector.tensor_tensor(rot[:, :, 0:ROT], ra[:], rb[:], ALU.add))
                        s.add(nc.vector.tensor_copy(qk[:, u, QK:QK + DH], qk[:, u, WIN_Q + DH:QK]))
                        nc.vector.tensor_copy(qk[:, u, QK + DH:QK2], qk[:, u, WIN_Q:WIN_Q + DH]).then_inc(qk_ready, 1)
                        v.wait_ge(sig_ready, t + 1)
                        nc.vector.tensor_tensor(glu[:, :, bass.ds(t * P, P)], ug_ps[:, 0:CONV].rearrange("p (c n) -> p c n", c=CT),
                                                sig[:, u, :].rearrange("p (c n) -> p c n", c=CT), ALU.mult).then_inc(glu_ready, 1)


def convolve(c, m, glu, cat):
    nc = c.nc
    with c.stage():
        acc = c.sb("acc", [P, CT, TOK])
        wc = c.sb("conv_w", [P, CT, TAPS])
        par = c.sb("conv_par", [P, 3, CT])
        ones = c.sb("ones", [P, P])
        eps = c.sb("eps", [P, 1])
        sq = c.sb("sq", [P, 2, CT, HALF])
        rstd = c.sb("rstd", [P, TOK // HALF, HALF])
        mean_ps, var_ps = c.ps("mean_ps", HALF), c.ps("var_ps", HALF)
        loaded, dve, conv_done, const = c.sem("loaded"), c.sem("dve"), c.sem("conv_done"), c.sem("const")
        mean_done, centred, squared, var_done, rooted, normed, cat_done = (
            c.sem(n) for n in ("mean_done", "centred", "squared", "var_done", "rooted", "normed", "cat_done"))
        chunks = TOK // HALF
        with c.block() as block:

            @block.sync
            def _(sp):
                sp.dma_start(wc[:], m["conv_w"]).then_inc(loaded, 16)
                for n, name in enumerate(("conv_b", "conv_g", "conv_beta")):
                    sp.dma_start(par[:, n, :], m[name]).then_inc(loaded, 16)

            @block.gpsimd
            def _(pool):
                pool.memset(ones[:], 1.0 / CONV).then_inc(const, 1)
                pool.memset(eps[:], LN_EPS).then_inc(const, 1)

            @block.vector
            def _(v):
                s = Steps(v, dve)
                v.wait_ge(loaded, 64)
                mid = TAPS // 2
                with s.loop(CT, len(SEQ) * TAPS) as ct:
                    one = bass.ds(ct, 1)
                    for g in range(len(SEQ)):
                        a, b = GROUP_FIRST[g] * P, (GROUP_FIRST[g] + GROUP_TILES[g]) * P
                        s.add(nc.vector.tensor_scalar(acc[:, one, a:b], glu[:, one, a:b], wc[:, one, mid:mid + 1],
                                                      par[:, 0, one], ALU.mult, ALU.add))
                    for tap in [x for x in range(TAPS) if x != mid]:
                        shift = tap - mid
                        for g in range(len(SEQ)):
                            a, b = GROUP_FIRST[g] * P, (GROUP_FIRST[g] + GROUP_TILES[g]) * P
                            lo, hi = max(a, a - shift), min(b, b - shift)
                            v.wait_ge(dve, s.base + s.here - 1)
                            s.add(nc.vector.scalar_tensor_tensor(acc[:, one, lo:hi], glu[:, one, lo + shift:hi + shift],
                                                                 wc[:, one, tap:tap + 1], acc[:, one, lo:hi], ALU.mult, ALU.add))
                s.settle()
                nc.vector.engine_nop().then_inc(conv_done, 1)
                for n in range(chunks):
                    part = acc[:, :, n * HALF:(n + 1) * HALF]
                    v.wait_ge(mean_done, n + 1)
                    for ct in range(CT):
                        nc.vector.tensor_tensor(part[:, ct, :], part[:, ct, :], mean_ps[:], ALU.subtract).then_inc(centred, 1)
                for n in range(chunks):
                    part = acc[:, :, n * HALF:(n + 1) * HALF]
                    v.wait_ge(rooted, n + 1)
                    s.link(nc.vector.reciprocal(rstd[:, n, :], rstd[:, n, :]))
                    v.wait_ge(centred, CT * (n + 1))
                    for ct in range(CT):
                        nc.vector.tensor_tensor(part[:, ct, :], part[:, ct, :], rstd[:, n, :], ALU.mult).then_inc(normed, 1)

            @block.tensor
            def _(pe):
                pe.wait_ge(const, 1)
                pe.wait_ge(conv_done, 1)
                for n in range(chunks):
                    part = acc[:, :, n * HALF:(n + 1) * HALF]
                    if n:
                        pe.wait_ge(centred, CT * n)
                    for ct in range(CT):
                        last = nc.tensor.matmul(mean_ps[:], ones[:], part[:, ct, :], start=(ct == 0), stop=(ct == CT - 1))
                    last.then_inc(mean_done, 1)
                    pe.wait_ge(squared, n + 1)
                    if n:
                        pe.wait_ge(rooted, n)
                    for ct in range(CT):
                        last = nc.tensor.matmul(var_ps[:], ones[:], sq[:, n % 2, ct, :], start=(ct == 0), stop=(ct == CT - 1))
                    last.then_inc(var_done, 1)

            @block.scalar
            def _(act):
                act.wait_ge(const, 2)
                for n in range(chunks):
                    part = acc[:, :, n * HALF:(n + 1) * HALF]
                    act.wait_ge(centred, CT * (n + 1))
                    if n >= 2:
                        act.wait_ge(var_done, n - 1)
                    nc.scalar.activation(sq[:, n % 2], part, ACT.Square).then_inc(squared, 1)
                    act.wait_ge(var_done, n + 1)
                    nc.scalar.activation(rstd[:, n, :], var_ps[:], ACT.Sqrt, bias=eps[:]).then_inc(rooted, 1)
                for n in range(chunks):
                    part = acc[:, :, n * HALF:(n + 1) * HALF]
                    act.wait_ge(normed, CT * (n + 1))
                    for ct in range(CT):
                        nc.scalar.activation(cat[:, ct, n * HALF:(n + 1) * HALF], part[:, ct, :], ACT.Silu,
                                             bias=par[:, 2, ct:ct + 1], scale=par[:, 1, ct:ct + 1]).then_inc(cat_done, 1)


def window_attention(c, m, keys, values, cat):
    nc = c.nc
    G = WIN_H // WIN_KV
    NK = 3 * P
    place = {(0, 0): 0, (1, 0): 1, (1, 1): 2, (0, 1): 3}
    with c.stage():
        ident = c.sb("ident", [P, P])
        sink = c.sb("sink", [P, 2, WIN_H])
        q = c.sb("q", [P, 2, WIN_Q])
        mask = c.sb("mask", [P, 2, NK])
        sm = c.sb("sm", [P, 2, G, NK])
        mx = c.sb("mx", [P, 2, 6, G])
        still = c.sb("still", [P, 1])
        pT = c.sb("pT", [P, 2, G * NK])
        o = c.sb("o", [P, 2, WIN_Q])
        s_ps, t_ps, o_ps = c.ps("s_ps", 4 * HALF), c.ps("t_ps", G * NK), c.ps("o_ps", WIN_Q)
        loaded, q_in = c.sem("loaded"), [c.sem("q_in0"), c.sem("q_in1")]
        scores, masked, bias, expd, pT_done, pT_act, pT_dve, o_done, o_ready, oT_done, oT_out, dve = (
            c.sem(n) for n in ("scores", "masked", "bias", "expd", "pT_done", "pT_act", "pT_dve", "o_done", "o_ready",
                               "oT_done", "oT_out", "dve"))
        CUT = 2 * HALF
        with c.block() as block:

            @block.sync
            def _(sp):
                sp.dma_start(ident[:], m["ident"]).then_inc(loaded, 16)
                sp.dma_start(sink[:, 0, :], row_broadcast(m["ab_sink"][0])).then_inc(loaded, 16)
                with sp.Fori(0, TILES // 2) as i:
                    for u in range(2):
                        t = i * 2 + u
                        sp.wait_ge(o_ready, t + 1)
                        sp.dma_start(q[:, u, :], m["qT"][bass.ds(t * P, P), 0:WIN_Q]).then_inc(q_in[u], 16)
                        sp.dma_start(mask[:, u, :], m["mask"][bass.ds(t * P, P), :]).then_inc(q_in[u], 16)

            def unit(n):
                return n // 2, n % 2, n % 2

            @block.tensor
            def _(pe):
                pe.wait_ge(loaded, 32)
                with pe.Fori(0, TILES // 2) as i:

                    def qk(n):
                        u, kv, _ = unit(n)
                        if kv == 0:
                            pe.wait_ge(q_in[u], i * 32 + 32)
                        pe.wait_ge(masked, (i * 4 + n) * G + 1)
                        for h in range(G):
                            head = kv * G + h
                            last = nc.tensor.matmul(s_ps[:, h * HALF:h * HALF + NK], q[:, u, (head // 2) * P:(head // 2 + 1) * P],
                                                    keys[:, place[kv, head % 2], bass.ds(i * 2 * P + u * P, NK)], start=True, stop=True)
                        last.then_inc(scores, 1)

                    def pv(n):
                        u, kv, b = unit(n)
                        pe.wait_ge(expd, i * 4 + n + 1)
                        pe.wait_ge(pT_act, i * 4 + n + 1)
                        pe.wait_ge(pT_dve, i * 4 + n + 1)
                        if kv == 0:
                            pe.wait_ge(oT_out, i * 2 + u + 1)
                        for h in range(G):
                            for k in range(3):
                                last = nc.tensor.transpose(t_ps[:, (h * 3 + k) * P:(h * 3 + k + 1) * P], sm[:, b, h, k * P:(k + 1) * P], ident[:])
                        last.then_inc(pT_done, 1)
                        pe.wait_ge(pT_act, i * 4 + n + 2)
                        pe.wait_ge(pT_dve, i * 4 + n + 2)
                        if kv == 0:
                            pe.wait_ge(o_ready, i * 2 + u + 2)
                        for h in range(G):
                            head = kv * G + h
                            for k in range(3):
                                last = nc.tensor.matmul(o_ps[:, head * DH:(head + 1) * DH], pT[:, b, (h * 3 + k) * P:(h * 3 + k + 1) * P],
                                                        values[:, bass.ds(i * 2 + u + k, 1), kv * DH:(kv + 1) * DH],
                                                        start=(k == 0), stop=(k == 2))
                        last.then_inc(o_done, 1)
                        if kv == 1:
                            pe.wait_ge(o_ready, i * 2 + u + 3)
                            for j in range(CT):
                                last = nc.tensor.transpose(t_ps[:, j * P:(j + 1) * P], o[:, u, j * P:(j + 1) * P], ident[:])
                            last.then_inc(oT_done, 1)

                    qk(0)
                    for n in range(4):
                        if n < 3:
                            qk(n + 1)
                        pv(n)

            @block.vector
            def _(v):
                s = Steps(v, dve)
                v.wait_ge(loaded, 32)
                v.sem_inc(masked, 1)
                v.sem_inc(pT_dve, 1)
                v.sem_inc(o_ready, 2)
                with s.loop(TILES // 2, 16) as i:

                    def soft(n):
                        u, kv, b = unit(n)
                        v.wait_ge(scores, i * 4 + n + 1)
                        v.wait_ge(pT_done, i * 4 + n + 1)
                        if kv == 0:
                            v.wait_ge(q_in[u], i * 32 + 32)
                        nc.vector.memset(still[:], 0.0)
                        for h in range(G):
                            nc.vector.tensor_tensor_reduce(out=sm[:, b, h, :], in0=s_ps[:, h * HALF:h * HALF + NK], in1=mask[:, u, :],
                                                           scale=SCALE, scalar=MASKED, op0=ALU.add, op1=ALU.max,
                                                           accum_out=mx[:, b, 0, h:h + 1]).then_inc(masked, 1)
                        v.wait_ge(masked, (i * 4 + n) * G + G + 1)
                        snk = sink[:, 0, kv * G:(kv + 1) * G]
                        s.link(nc.vector.tensor_tensor(mx[:, b, 1, :], mx[:, b, 0, :], snk, ALU.max))
                        s.add(nc.vector.tensor_scalar(mx[:, b, 2, :], mx[:, b, 1, :], -1.0, None, ALU.mult))
                        nc.vector.tensor_tensor(mx[:, b, 3, :], snk, mx[:, b, 1, :], ALU.subtract).then_inc(bias, 1)

                    def after(n):
                        u, kv, b = unit(n)
                        v.wait_ge(expd, i * 4 + n + 1)
                        s.link(nc.vector.tensor_tensor(mx[:, b, 4, :], mx[:, b, 4, :], mx[:, b, 5, :], ALU.add))
                        s.link(nc.vector.reciprocal(sink[:, 1, kv * G:(kv + 1) * G], mx[:, b, 4, :]))
                        v.wait_ge(pT_done, i * 4 + n + 3)
                        nc.vector.tensor_copy(pT[:, b, CUT:G * NK], t_ps[:, CUT:G * NK]).then_inc(pT_dve, 1)
                        if kv == 1:
                            v.wait_ge(o_done, i * 4 + n + 1)
                            v.wait_ge(oT_done, i * 2 + u + 1)
                            nc.vector.tensor_tensor(o[:, u, :].rearrange("p (h d) -> p h d", d=DH), o_ps[:].rearrange("p (h d) -> p h d", d=DH),
                                                    sink[:, 1, :].rearrange("p (h o) -> p h o", o=1).to_broadcast([P, WIN_H, DH]),
                                                    ALU.mult).then_inc(o_ready, 1)

                    soft(0)
                    for n in range(4):
                        if n < 3:
                            soft(n + 1)
                        after(n)

            @block.scalar
            def _(act):
                act.sem_inc(pT_done, 2)
                act.sem_inc(oT_done, 2)
                act.sem_inc(pT_act, 1)
                act.sem_inc(oT_out, 1)
                with act.Fori(0, TILES // 2) as i:

                    def exps(n):
                        u, kv, b = unit(n)
                        act.wait_ge(bias, i * 4 + n + 1)
                        for h in range(G):
                            nc.scalar.activation(sm[:, b, h, :], sm[:, b, h, :], ACT.Exp, bias=mx[:, b, 2, h:h + 1],
                                                 accum_out=mx[:, b, 4, h:h + 1])
                        nc.scalar.activation(mx[:, b, 5, :], mx[:, b, 3, :], ACT.Exp).then_inc(expd, 1)

                    def after(n):
                        u, kv, b = unit(n)
                        act.wait_ge(pT_done, i * 4 + n + 3)
                        nc.scalar.activation(pT[:, b, 0:CUT], t_ps[:, 0:CUT], ACT.Copy).then_inc(pT_act, 1)
                        if kv == 1:
                            act.wait_ge(oT_done, i * 2 + u + 3)
                            nc.scalar.activation(cat[:, CT:2 * CT, bass.ds(i * 2 * P + u * P, P)],
                                                 t_ps[:, 0:WIN_Q].rearrange("p (c n) -> p c n", c=CT), ACT.Copy).then_inc(oT_out, 1)

                    exps(0)
                    for n in range(4):
                        if n < 3:
                            exps(n + 1)
                        after(n)


def project_out(c, m, layer, w_out, x_src, cat, affinity):
    nc = c.nc
    with c.stage():
        w = c.sb("w_out", [P, KD, D])
        wr = c.sb("router", [P, KD, EXPERTS])
        ident = c.sb("ident", [P, P])
        gain, shift = c.sb("gain", [P, D]), c.sb("shift", [P, D])
        a = c.sb("cat_tile", [P, 2, KD, P])
        x = c.sb("x", [P, 2, D])
        row = c.sb("row", [P, D])
        stats, mv = c.sb("stats", [P, 12]), c.sb("mv", [P, 4])
        half = c.sb("minus_half", [P, 1])
        x1, ax1 = c.sb("x1", [P, 2, D]), c.sb("ax1", [P, 2, D])
        xT = c.sb("xT", [P, 2, D])
        prob, pr = c.sb("prob", [P, 2, EXPERTS]), c.sb("prob_stats", [P, 4])
        y_ps, t_ps = [c.ps("y_ps0", D), c.ps("y_ps1", D)], c.ps("t_ps", D)
        r_ps, rT_ps = c.ps("r_ps", HALF), c.ps("rT_ps", HALF)
        w_in, a_in = c.sem("w_in"), [c.sem("a_in0"), c.sem("a_in1")]
        y_done, res_done, var_ready, rstd_ready, x1_ready, ax_ready, xT_done, xT_ready, r_done, neg_ready, exp_done, prob_ready, rT_done, aff_ready, dve, const = (
            c.sem(n) for n in ("y_done", "res_done", "var_ready", "rstd_ready", "x1_ready", "ax_ready", "xT_done", "xT_ready", "r_done",
                               "neg_ready", "exp_done", "prob_ready", "rT_done", "aff_ready", "dve", "const"))
        x1_out = [c.sem("x1_out0"), c.sem("x1_out1")]
        with c.block() as block:

            @block.sync
            def _(sp):
                if layer == 0:
                    wv = w_out.rearrange("(k p) n -> p k n", p=P)
                    for part in range(4):
                        sp.dma_start(w[:, 2 * part:2 * part + 2, :], wv[:, 2 * part:2 * part + 2, :]).then_inc(w_in, 16)
                else:
                    wv = w_out.rearrange("(a s j p) n -> a s p j n", a=2, s=2, p=DH)
                    for a2 in range(2):
                        for side in range(2):
                            sp.dma_start(w[DH * side:DH * (side + 1), 4 * a2:4 * a2 + 4, :], wv[a2, side]).then_inc(w_in, 16)
                sp.dma_start(wr[:], m["moe_router"][layer].rearrange("(k p) n -> p k n", p=P)).then_inc(w_in, 16)
                sp.dma_start(ident[:], m["ident"]).then_inc(w_in, 16)
                sp.dma_start(gain[:], row_broadcast(m["ln1_g"][layer])).then_inc(w_in, 16)
                sp.dma_start(shift[:], row_broadcast(m["ln1_b"][layer])).then_inc(w_in, 16)
                with sp.Fori(0, TILES // 2) as i:
                    for u in range(2):
                        t = i * 2 + u
                        sp.wait_ge(res_done, t + 1)
                        sp.dma_start(a[:, u, :, :], cat[:, :, bass.ds(t * P, P)]).then_inc(a_in[u], 16)
                        sp.dma_start(x[:, u, :], x_src[bass.ds(t * P, P), :]).then_inc(a_in[u], 16)

            @block.gpsimd
            def _(pool):
                pool.memset(half[:], -0.5).then_inc(const, 1)
                pool.wait_ge(const, 1)
                with pool.Fori(0, TILES // 2) as i:
                    for u in range(2):
                        t = i * 2 + u
                        pool.wait_ge(var_ready, t + 1)
                        pool.tensor_tensor(mv[:, 3:4], mv[:, 2:3], half[:], ALU.pow).then_inc(rstd_ready, 1)

            @block.tensor
            def _(pe):
                pe.wait_ge(w_in, 128)
                with pe.Fori(0, TILES // 2) as i:
                    for u in range(2):
                        t = i * 2 + u
                        pe.wait_ge(a_in[u], i * 32 + 32)
                        pe.wait_ge(res_done, t + 1)
                        for h in range(2):
                            for k in range(KD):
                                last = nc.tensor.matmul(y_ps[u][:, h * HALF:(h + 1) * HALF], a[:, u, k, :], w[:, k, h * HALF:(h + 1) * HALF],
                                                        start=(k == 0), stop=(k == KD - 1))
                        last.then_inc(y_done, 1)
                        if u == 1:
                            for b in range(2):
                                tb = i * 2 + b
                                pe.wait_ge(x1_ready, tb + 1)
                                pe.wait_ge(xT_ready, tb + 1)
                                for k in range(KD):
                                    last = nc.tensor.transpose(t_ps[:, k * P:(k + 1) * P], x1[:, b, k * P:(k + 1) * P], ident[:])
                                last.then_inc(xT_done, 1)
                                pe.wait_ge(xT_ready, tb + 2)
                                pe.wait_ge(prob_ready, tb + 1)
                                for k in range(KD):
                                    last = nc.tensor.matmul(r_ps[:, 0:EXPERTS], xT[:, b, k * P:(k + 1) * P], wr[:, k, :],
                                                            start=(k == 0), stop=(k == KD - 1))
                                last.then_inc(r_done, 1)
                                pe.wait_ge(prob_ready, tb + 2)
                                pe.wait_ge(aff_ready, tb + 1)
                                nc.tensor.transpose(rT_ps[0:EXPERTS, 0:P], prob[:, b, :], ident[:]).then_inc(rT_done, 1)

            @block.vector
            def _(v):
                s = Steps(v, dve)
                v.wait_ge(w_in, 128)
                v.sem_inc(res_done, 2)
                v.sem_inc(prob_ready, 1)
                with s.loop(TILES // 2, 2 * 5 + 2) as i:
                    for u in range(2):
                        t = i * 2 + u
                        v.wait_ge(y_done, t + 1)
                        v.wait_ge(a_in[u], i * 32 + 32)
                        nc.vector.scalar_tensor_tensor(row[:], x[:, u, :], ALPHA, y_ps[u][:], ALU.mult, ALU.add).then_inc(res_done, 1)
                        v.wait_ge(res_done, t + 3)
                        v.wait_ge(x1_out[u], i * 32 + 32)
                        v.wait_ge(xT_done, t + 1)
                        v.wait_ge(ax_ready, t + 1)
                        last = layer_norm_rows(nc, s, row[:], x1[:, u, :], stats, mv, gain[:], shift[:], var_ready, rstd_ready, t)
                        last.then_inc(x1_ready, 1)
                    for b in range(2):
                        tb = i * 2 + b
                        v.wait_ge(r_done, tb + 1)
                        nc.vector.tensor_reduce(pr[:, 0:1], r_ps[:, 0:EXPERTS], AX.X, ALU.max, negate=True).then_inc(neg_ready, 1)
                        v.wait_ge(exp_done, tb + 1)
                        s.link(nc.vector.reciprocal(pr[:, 2:3], pr[:, 1:2]))
                        nc.vector.tensor_scalar(prob[:, b, :], prob[:, b, :], pr[:, 2:3], None, ALU.mult).then_inc(prob_ready, 1)

            @block.scalar
            def _(act):
                act.sem_inc(xT_ready, 1)
                act.sem_inc(xT_done, 2)
                act.sem_inc(ax_ready, 2)
                act.sem_inc(aff_ready, 1)
                act.sem_inc(rT_done, 2)
                for u in range(2):
                    act.sem_inc(x1_out[u], 32)
                with act.Fori(0, TILES // 2) as i:
                    for u in range(2):
                        t = i * 2 + u
                        act.wait_ge(x1_ready, t + 1)
                        act.wait_ge(x1_out[u], i * 32 + 32)
                        nc.scalar.activation(ax1[:, u, :], x1[:, u, :], ACT.Copy, scale=ALPHA).then_inc(ax_ready, 1)
                        act.dma_start(m["x1"][bass.ds(t * P, P), :], x1[:, u, :]).then_inc(x1_out[u], 16)
                        act.wait_ge(ax_ready, t + 3)
                        act.dma_start(m["acc"][bass.ds(t * P, P), :], ax1[:, u, :]).then_inc(x1_out[u], 16)
                    for b in range(2):
                        tb = i * 2 + b
                        act.wait_ge(xT_done, tb + 3)
                        nc.scalar.activation(xT[:, b, :], t_ps[:], ACT.Copy).then_inc(xT_ready, 1)
                        act.wait_ge(neg_ready, tb + 1)
                        act.wait_ge(rT_done, tb + 1)
                        nc.scalar.activation(prob[:, b, :], r_ps[:, 0:EXPERTS], ACT.Exp, bias=pr[:, 0:1], accum_out=pr[:, 1:2]).then_inc(exp_done, 1)
                        act.wait_ge(rT_done, tb + 3)
                        nc.scalar.activation(affinity[:, bass.ds(tb * P, P)], rT_ps[0:EXPERTS, 0:P], ACT.Copy).then_inc(aff_ready, 1)
                for u in range(2):
                    act.wait_ge(x1_out[u], 32 * (TILES // 2) + 32)


def choose(c, m, affinity, gates, rows):
    nc = c.nc
    R = PROMPT_ROW + EXPERTS
    N = SEQ[1]
    BEST = CAP[1]
    with c.stage():
        ident = c.sb("ident", [P, P])
        left = c.sb("left", [R, 2, N])
        best = c.sb("best", [R, BEST])
        where = c.sb("where", [R, BEST], U32)
        wheref = c.sb("wheref", [R, BEST])
        t_ps = c.ps("t_ps", HALF)
        loaded, dve, turned = c.sem("loaded"), c.sem("dve"), c.sem("turned")
        with c.block() as block:

            @block.sync
            def _(sp):
                sp.dma_start(ident[:], m["ident"]).then_inc(loaded, 16)

            @block.vector
            def _(v):
                s = Steps(v, dve)
                s.add(nc.vector.memset(rows[:], 0))
                s.add(nc.vector.memset(gates[:], 0.0))
                s.link(nc.vector.memset(left[:], -1.0))
                s.add(nc.vector.tensor_copy(left[0:EXPERTS, 0, :], affinity[:, SEQ[0]:TOK]))
                s.link(nc.vector.tensor_copy(left[PROMPT_ROW:R, 0, 0:SEQ[0]], affinity[:, 0:SEQ[0]]))
                for r in range(BEST // 8):
                    now, eight = left[:, r % 2, :], slice(8 * r, 8 * r + 8)
                    s.link(nc.vector.max(out=best[:, eight], in_=now))
                    s.add(nc.vector.max_index(out=where[:, eight], in_max=best[:, eight], in_values=now))
                    if r + 1 < BEST // 8:
                        s.link(nc.vector.match_replace(out=left[:, (r + 1) % 2, :], in_to_replace=best[:, eight], in_values=now, imm_value=-2.0))
                s.settle()
                s.link(nc.vector.tensor_copy(wheref[:], where[:]))
                s.link(nc.vector.tensor_scalar(wheref[0:EXPERTS, :], wheref[0:EXPERTS, :], float(SEQ[0]), None, ALU.add))
                v.wait_ge(turned, 1)
                nc.vector.tensor_copy(gates[:, 0:R], t_ps[:, 0:R])
                s.link(nc.vector.tensor_copy(rows[:, 0:R], t_ps[:, 64:64 + R]))

            @block.tensor
            def _(pe):
                pe.wait_ge(loaded, 16)
                pe.wait_ge(dve, 5 + 3 * (BEST // 8) - 1 + 2)
                nc.tensor.transpose(t_ps[:, 0:R], best[:], ident[0:R, 0:R])
                nc.tensor.transpose(t_ps[:, 64:64 + R], wheref[:], ident[0:R, 0:R]).then_inc(turned, 1)


def experts(c, m, layer, gates, rows):
    nc = c.nc
    SC, PC = CAP[1], CAP[0]
    FH = KD // 2
    with c.stage():
        ident = c.sb("ident", [P, P])
        w = [c.sb(f"w{n}", [P, KD * HALF]) for n in range(6)]
        ids = c.sb("ids", [P, 2, 2], U32)
        gsel = c.sb("gsel", [P, 2, 2])
        xs, xp = [c.sb(f"xs{u}", [P, D]) for u in range(2)], [c.sb(f"xp{u}", [PC, D]) for u in range(2)]
        xT = c.sb("xT", [P, KD, SLOTS])
        sg = c.sb("sg", [P, 2, SLOTS])
        hT = c.sb("hT", [P, KD, SLOTS])
        ys, yp = c.sb("ys", [P, D]), c.sb("yp", [PC, D])
        h_ps = [c.ps(f"h_ps{b}", HALF) for b in range(2)]
        t_ps = [c.ps(f"t_ps{b}", HALF) for b in range(2)]
        y_ps, yp_ps = c.ps("y_ps", D), c.ps("yp_ps", D)
        loaded = c.sem("loaded")
        w_in = [c.sem(f"w_in{n}") for n in range(6)]
        x_in = [c.sem("x_in0"), c.sem("x_in1")]
        ids_ready, turned, xT_ready, h_done, silu_ready, h_ready, y_done, ys_ready, yp_ready, added = (
            c.sem(n) for n in ("ids_ready", "turned", "xT_ready", "h_done", "silu_ready", "h_ready", "y_done", "ys_ready",
                               "yp_ready", "added"))
        turn_done = c.sem("turn_done")
        still = c.sb("still", [P, 5])
        QUADS = KD // 2
        picks, gate_cols = rows[:].rearrange("p (g e) -> p g e", g=2), gates[:].rearrange("p (g e) -> p g e", g=2)
        with c.block() as block:

            @block.sync
            def _(sp):
                sp.dma_start(ident[:], m["ident"]).then_inc(loaded, 16)
                gate_up = [m[n].rearrange("l e (k p) f -> (l e) p k f", p=P) for n in ("moe_w_gate", "moe_w_up")]
                down = m["moe_w_down"].rearrange("l e (h k p) d -> (l e) p h k d", p=P, h=2)
                with sp.Fori(0, EXPERTS) as e:
                    which = bass.ds(e + layer * EXPERTS, 1)
                    for part in range(2):
                        sp.wait_ge(h_done, e * KD + FH * part + FH)
                        for n in range(2):
                            sp.dma_start(w[2 * part + n][:].rearrange("p (o k f) -> p o k f", o=1, k=KD),
                                         gate_up[n][which, :, :, part * HALF:(part + 1) * HALF].rearrange("o p k f -> p o k f")).then_inc(w_in[2 * part + n], 16)
                    for part in range(2):
                        sp.wait_ge(y_done, e * 2 + part + 1)
                        sp.dma_start(w[4 + part][:].rearrange("p (o k d) -> p o k d", o=1, k=FH),
                                     down[which, :, part, :, :].rearrange("o p k d -> p o k d")).then_inc(w_in[4 + part], 16)

            @block.gpsimd
            def _(pool):
                def hold(at):
                    return pool.tensor_tensor(still[:, at:at + 1], still[:, 0:1], still[:, 0:1], ALU.add)

                def gather(u, e, at):
                    pool.wait_ge(ids_ready, e + 1)
                    pool.wait_ge(turned, e * QUADS + QUADS)
                    pool.wait_ge(turn_done, e + 1)
                    hold(at)
                    pool.indirect_dma_start(out=xs[u][:], out_offset=None, in_=m["x1"],
                                            in_offset=bass.IndirectOffsetOnAxis(ap=ids[:, u, 0:1], axis=0)).then_inc(x_in[u], 16)
                    pool.indirect_dma_start(out=xp[u][:], out_offset=None, in_=m["x1"],
                                            in_offset=bass.IndirectOffsetOnAxis(ap=ids[0:PC, u, 1:2], axis=0)).then_inc(x_in[u], 16)

                pool.sem_inc(turn_done, 2)
                pool.memset(still[:], 0.0).then_inc(loaded, 1)
                pool.wait_ge(loaded, 17)
                gather(0, 0, 4)
                with pool.Fori(0, EXPERTS // 2) as i:
                    for u in range(2):
                        e = i * 2 + u
                        gather(1 - u, e + 1, 1)
                        pool.wait_ge(ys_ready, e + 2)
                        pool.wait_ge(yp_ready, e + 2)
                        hold(2)
                        pool.indirect_dma_start(out=m["acc"], out_offset=bass.IndirectOffsetOnAxis(ap=ids[:, u, 0:1], axis=0),
                                                in_=ys[:], in_offset=None, compute_op=ALU.add).then_inc(added, 16)
                        pool.indirect_dma_start(out=m["acc"], out_offset=bass.IndirectOffsetOnAxis(ap=ids[0:PC, u, 1:2], axis=0),
                                                in_=yp[:], in_offset=None, compute_op=ALU.add).then_inc(added, 16)
                        pool.wait_ge(added, e * 32 + 32)
                        hold(3).then_inc(turn_done, 1)

            @block.tensor
            def _(pe):
                def turn(u, arrived, first):
                    pe.wait_ge(x_in[u], arrived)
                    for q in range(QUADS):
                        bank = t_ps[q % 2]
                        pe.wait_ge(xT_ready, first + q)
                        for j in range(2):
                            k = q * 2 + j
                            nc.tensor.transpose(bank[:, j * SLOTS:j * SLOTS + SC], xs[u][:, k * P:(k + 1) * P], ident[:])
                            last = nc.tensor.transpose(bank[:, j * SLOTS + SC:(j + 1) * SLOTS], xp[u][:, k * P:(k + 1) * P], ident[0:PC, 0:PC])
                        last.then_inc(turned, 1)

                pe.sem_inc(h_done, KD)
                pe.sem_inc(y_done, 2)
                pe.sem_inc(turned, 2 * QUADS)
                pe.wait_ge(loaded, 16)
                turn(0, 32, 1)
                with pe.Fori(0, EXPERTS // 2) as i:
                    for u in range(2):
                        e = i * 2 + u
                        pe.wait_ge(xT_ready, e * QUADS + QUADS + 2)
                        for f in range(KD):
                            part, col = f // FH, f % FH * P
                            if f % FH == 0:
                                for n in range(2):
                                    pe.wait_ge(w_in[2 * part + n], e * 16 + 16)
                            pe.wait_ge(h_ready, e * KD + f + 1)
                            for n in range(2):
                                for k in range(KD):
                                    at = k * HALF + col
                                    last = nc.tensor.matmul(h_ps[f % 2][:, n * SLOTS:(n + 1) * SLOTS], w[2 * part + n][:, at:at + P],
                                                            xT[:, k, :], start=(k == 0), stop=(k == KD - 1))
                            last.then_inc(h_done, 1)
                        turn(1 - u, i * 32 + 32 + 32 * u, e * QUADS + QUADS + 1)
                        pe.wait_ge(ys_ready, e + 1)
                        pe.wait_ge(yp_ready, e + 1)
                        for f in range(KD):
                            if f % FH == 0:
                                pe.wait_ge(w_in[4 + f // FH], e * 16 + 16)
                            pe.wait_ge(h_ready, e * KD + f + 3)
                            for ps, lo, n in ((y_ps, 0, SC), (yp_ps, SC, PC)):
                                for h in range(2):
                                    at = f % FH * D + h * HALF
                                    last = nc.tensor.matmul(ps[0:n, h * HALF:(h + 1) * HALF], hT[:, f, lo:lo + n], w[4 + f // FH][:, at:at + HALF],
                                                            start=(f == 0), stop=(f == KD - 1))
                            if f % FH == FH - 1:
                                last.then_inc(y_done, 1)

            @block.scalar
            def _(act):
                def turn(first):
                    for q in range(QUADS):
                        act.wait_ge(turned, first + q + 2 * QUADS + 1)
                        nc.scalar.activation(xT[:, 2 * q:2 * q + 2, :], t_ps[q % 2][:, 0:2 * SLOTS].rearrange("p (k n) -> p k n", k=2), ACT.Copy)\
                            .then_inc(xT_ready, 1)

                act.sem_inc(xT_ready, 2)
                act.sem_inc(ys_ready, 1)
                turn(0)
                with act.Fori(0, EXPERTS // 2) as i:
                    for u in range(2):
                        e = i * 2 + u
                        for f in range(KD):
                            act.wait_ge(h_done, e * KD + f + 1 + KD)
                            nc.scalar.activation(sg[:, f % 2, :], h_ps[f % 2][:, 0:SLOTS], ACT.Silu).then_inc(silu_ready, 1)
                        turn(e * QUADS + QUADS)
                        act.wait_ge(y_done, e * 2 + 4)
                        act.wait_ge(turn_done, e + 2)
                        nc.scalar.activation(ys[:], y_ps[:], ACT.Copy, scale=gsel[:, u, 0:1]).then_inc(ys_ready, 1)

            @block.vector
            def _(v):
                def pick(u, e):
                    v.wait_ge(turn_done, e + 1)
                    nc.vector.tensor_copy(gsel[:, u, :], gate_cols[:, :, bass.ds(e, 1)].rearrange("p g o -> p (g o)"))
                    nc.vector.tensor_copy(ids[:, u, :], picks[:, :, bass.ds(e, 1)].rearrange("p g o -> p (g o)")).then_inc(ids_ready, 1)

                v.sem_inc(h_ready, 2)
                v.sem_inc(yp_ready, 1)
                pick(0, 0)
                with v.Fori(0, EXPERTS // 2) as i:
                    for u in range(2):
                        e = i * 2 + u
                        for f in range(KD):
                            v.wait_ge(silu_ready, e * KD + f + 1)
                            nc.vector.tensor_tensor(hT[:, f, :], sg[:, f % 2, :], h_ps[f % 2][:, SLOTS:2 * SLOTS], ALU.mult).then_inc(h_ready, 1)
                            if f == FH:
                                pick(1 - u, e + 1)
                        v.wait_ge(y_done, e * 2 + 4)
                        v.wait_ge(turn_done, e + 2)
                        nc.vector.tensor_scalar(yp[:], yp_ps[0:PC, :], gsel[0:PC, u, 1:2], None, ALU.mult).then_inc(yp_ready, 1)


class Tile:

    def __init__(self, i, n):
        self.t, self.pair, self.slot = i * 2 + n, i + n // 2, n % 2
        self.i, self.n = i, n

    def next(self, by=1):
        return Tile(self.i, self.n + by)


def project_axial(c, m, keys, values):
    nc = c.nc
    QK = AX_Q + AX_KVD
    HEADS = QK // DH
    BATCH = 12
    QW = 2 * AX_Q
    with c.stage():
        w = c.sb("w_in", [P, KD, C_IN])
        ident = c.sb("ident", [P, P])
        gain, shift = c.sb("gain", [P, D]), c.sb("shift", [P, D])
        norm2 = c.sb("norm2", [P, 2, DH])
        r = c.sb("r", [P, 2, D])
        rope = c.sb("rope", [P, 2, 2 * DH])
        x2 = c.sb("x2", [P, 2, D])
        stats, mv = c.sb("stats", [P, 12]), c.sb("mv", [P, 4])
        half = c.sb("minus_half", [P, HEADS])
        ms = c.sb("ms", [P, 2, HEADS])
        xT = c.sb("xT", [P, D])
        qk = c.sb("qk", [P, QK])
        parts = c.sb("parts", [P, QW + 4 * AX_KVD], F32R)
        ra, rb = c.sb("ra", [P, HEADS, DH]), c.sb("rb", [P, HEADS, DH])
        qT = c.sb("qT", [P, 2, QW], F32R)
        xT_ps, qkv_ps, qkT_ps = c.ps("xT_ps", D), c.ps("qkv_ps", C_IN), c.ps("qkT_ps", BATCH * P)
        w_in, r_in, x2_out, q_out = c.sem("w_in"), [c.sem("r_in0"), c.sem("r_in1")], [c.sem("x2_out0"), c.sem("x2_out1")], [c.sem("q_out0"), c.sem("q_out1")]
        const, dve, var_ready, rstd_ready, x2_ready, xT_done, xT_ready, qkv_done, copied, squared, ms_ready, rms_ready = (
            c.sem(n) for n in ("const", "dve", "var_ready", "rstd_ready", "x2_ready", "xT_done", "xT_ready", "qkv_done", "copied",
                               "squared", "ms_ready", "rms_ready"))
        rotated, high_ready, parts_ready, qkT_done, qT_ready, k_ready = (
            c.sem(n) for n in ("rotated", "high_ready", "parts_ready", "qkT_done", "qT_ready", "k_ready"))
        turns = TILES // 2
        LAST = TILES - 1
        q_parts = parts[:, 0:QW].rearrange("p (h s d) -> p h s d", s=2, d=DH)
        k_parts = parts[:, QW:].rearrange("p (h s d) -> p h s d", s=4, d=DH)
        with c.block() as block:

            @block.sync
            def _(sp):
                sp.dma_start(gain[:], row_broadcast(m["ln2_g"][0])).then_inc(w_in, 16)
                sp.dma_start(shift[:], row_broadcast(m["ln2_b"][0])).then_inc(w_in, 16)
                sp.dma_start(norm2[:, 0, :], row_broadcast(m["c_q_norm"][0])).then_inc(w_in, 16)
                sp.dma_start(norm2[:, 1, :], row_broadcast(m["c_k_norm"][0])).then_inc(w_in, 16)
                sp.dma_start(ident[:], m["ident"]).then_inc(w_in, 16)
                sp.dma_start(w[:], m["c_w_in"][0].rearrange("(k p) n -> p k n", p=P)).then_inc(w_in, 16)
                with sp.Fori(0, turns) as i:
                    for u in range(2):
                        t = i * 2 + u
                        sp.wait_ge(x2_ready, t + 1)
                        sp.wait_ge(rotated, t + 1)
                        sp.dma_start(r[:, u, :], m["acc"][bass.ds(t * P, P), :]).then_inc(r_in[u], 16)
                        sp.dma_start(rope[:, u, :], m["rope_c"][bass.ds(t * P, P), :]).then_inc(r_in[u], 16)

            @block.gpsimd
            def _(pool):
                pool.memset(half[:], -0.5).then_inc(const, 1)
                pool.wait_ge(const, 1)

                def layer_norm_root(t):
                    pool.wait_ge(var_ready, t + 1)
                    pool.tensor_tensor(mv[:, 3:4], mv[:, 2:3], half[:, 0:1], ALU.pow).then_inc(rstd_ready, 1)

                def head_norm_root(t):
                    pool.wait_ge(ms_ready, t + 1)
                    pool.tensor_tensor(ms[:, 1, :], ms[:, 0, :], half[:], ALU.pow).then_inc(rms_ready, 1)

                layer_norm_root(0)
                layer_norm_root(1)
                with pool.Fori(0, TILES - 2) as t:
                    head_norm_root(t)
                    layer_norm_root(t + 2)
                head_norm_root(TILES - 2)
                head_norm_root(TILES - 1)

            @block.tensor
            def _(pe):
                def turn_x(a):
                    pe.wait_ge(x2_ready, a.t + 3)
                    for k in range(KD):
                        last = nc.tensor.transpose(xT_ps[:, k * P:(k + 1) * P], x2[:, a.slot, k * P:(k + 1) * P], ident[:])
                    last.then_inc(xT_done, 1)

                def turn_qk(a, batch):
                    if batch == 0:
                        pe.wait_ge(parts_ready, a.t + 2)
                        pe.wait_ge(k_ready, a.t + 1)
                    pe.wait_ge(qT_ready, a.t * 2 + batch + 1)
                    for j in range(BATCH):
                        at = (batch * BATCH + j) * P
                        last = nc.tensor.transpose(qkT_ps[:, j * P:(j + 1) * P], parts[:, at:at + P].bitcast(F32), ident[:])
                    last.then_inc(qkT_done, 1)

                def step(a, products=True, prior=True, following=True):
                    for n in range(C_IN // HALF):
                        if products:
                            if n == 0:
                                pe.wait_ge(xT_ready, a.t + 1)
                                pe.wait_ge(copied, a.t + 1)
                            for k in range(KD):
                                last = nc.tensor.matmul(qkv_ps[:, n * HALF:(n + 1) * HALF], xT[:, k * P:(k + 1) * P],
                                                        w[:, k, n * HALF:(n + 1) * HALF], start=(k == 0), stop=(k == KD - 1))
                            if n == C_IN // HALF - 1:
                                last.then_inc(qkv_done, 1)
                        if prior and n == 1:
                            turn_qk(a.next(-1), 0)
                    if following:
                        turn_x(a.next())
                    if prior:
                        turn_qk(a.next(-1), 1)

                pe.wait_ge(w_in, 96)
                turn_x(Tile(0, 0))
                step(Tile(0, 0), prior=False)
                with pe.Fori(0, turns - 1) as i:
                    step(Tile(i, 1))
                    step(Tile(i, 2))
                step(Tile(0, LAST), following=False)
                step(Tile(0, TILES), products=False, following=False)

            @block.scalar
            def _(act):
                def copy_x(a):
                    act.wait_ge(x2_ready, a.t + 3)
                    act.dma_start(m["x2"][bass.ds(a.t * P, P), :], x2[:, a.slot, :]).then_inc(x2_out[a.slot], 16)
                    act.wait_ge(xT_done, a.t + 3)
                    nc.scalar.activation(xT[:], xT_ps[:], ACT.Copy).then_inc(xT_ready, 1)

                def copy_qkv(a):
                    act.wait_ge(qkv_done, a.t + 1)
                    act.wait_ge(parts_ready, a.t + 1)
                    nc.scalar.activation(values[:, bass.ds(a.t, 1), :], qkv_ps[:, QK:C_IN].rearrange("p (o n) -> p o n", o=1), ACT.Copy)
                    nc.scalar.activation(qk[:], qkv_ps[:, 0:QK], ACT.Copy).then_inc(copied, 1)

                def square(a):
                    act.wait_ge(copied, a.t + 2)
                    nc.scalar.activation(ra[:].rearrange("p h d -> p (h d)"), qk[:], ACT.Square).then_inc(squared, 1)

                def high(a):
                    act.wait_ge(rotated, a.t + 3)
                    act.wait_ge(qkT_done, a.t * 2 + 1)
                    heads = qk[:].rearrange("p (h d) -> p h d", d=DH)
                    nc.scalar.activation(q_parts[:, :, 0, :], heads[:, 0:AX_H, :], ACT.Copy)
                    nc.scalar.activation(k_parts[:, :, 0, :], heads[:, AX_H:HEADS, :], ACT.Copy)
                    nc.scalar.activation(k_parts[:, :, 1, :], heads[:, AX_H:HEADS, :], ACT.Copy).then_inc(high_ready, 1)

                def copy_q(a, batch):
                    lo, hi = ((0, BATCH * P), (BATCH * P, QW))[batch]
                    act.wait_ge(qkT_done, a.t * 2 + batch + 2)
                    if batch == 0:
                        act.wait_ge(q_out[a.slot], a.pair * 16 + 16)
                    nc.scalar.activation(qT[:, a.slot, lo:hi], qkT_ps[:, 0:hi - lo], ACT.Copy, scale=SCALE).then_inc(qT_ready, 1)
                    if batch == 1:
                        act.wait_ge(qT_ready, a.t * 2 + 3)
                        act.dma_start(m["qT_parts"][bass.ds(a.t * P, P), :], qT[:, a.slot, :].bitcast(F32)).then_inc(q_out[a.slot], 16)

                def step(a, products=True, prior=True, following=True):
                    if prior:
                        high(a.next(-1))
                        copy_q(a.next(-1), 0)
                    if products:
                        copy_qkv(a)
                    if following:
                        copy_x(a.next())
                    if products:
                        square(a)
                    if prior:
                        copy_q(a.next(-1), 1)

                act.sem_inc(copied, 1)
                act.sem_inc(qT_ready, 1)
                act.sem_inc(qkT_done, 1)
                for u in range(2):
                    act.sem_inc(x2_out[u], 16)
                    act.sem_inc(q_out[u], 16)
                copy_x(Tile(0, 0))
                step(Tile(0, 0), prior=False)
                with act.Fori(0, turns - 1) as i:
                    step(Tile(i, 1))
                    step(Tile(i, 2))
                step(Tile(0, LAST), following=False)
                step(Tile(0, TILES), products=False, following=False)
                for u in range(2):
                    act.wait_ge(x2_out[u], 16 * turns + 16)
                    act.wait_ge(q_out[u], 16 * turns + 16)

            @block.vector
            def _(v):
                s = Steps(v, dve)
                heads = qk[:].rearrange("p (h d) -> p h d", d=DH)

                def norm(a):
                    v.wait_ge(r_in[a.slot], a.pair * 32 + 32)
                    v.wait_ge(x2_out[a.slot], a.pair * 16 + 16)
                    v.wait_ge(xT_done, a.t + 1)
                    layer_norm_rows(nc, s, r[:, a.slot, :], x2[:, a.slot, :], stats, mv, gain[:], shift[:], var_ready, rstd_ready, a.t).then_inc(x2_ready, 1)

                def rotate(a):
                    v.wait_ge(squared, a.t + 1)
                    s.link(nc.vector.tensor_reduce(ms[:, 0, :], ra[:], AX.X, ALU.add))
                    nc.vector.tensor_scalar(ms[:, 0, :], ms[:, 0, :], 1.0 / DH, RMS_EPS, ALU.mult, ALU.add).then_inc(ms_ready, 1)
                    v.wait_ge(rms_ready, a.t + 1)
                    s.link(nc.vector.tensor_tensor(heads, heads, ms[:, 1, :].rearrange("p (h o) -> p h o", o=1).to_broadcast([P, HEADS, DH]), ALU.mult))
                    for n, lo, hi in ((0, 0, AX_H), (1, AX_H, HEADS)):
                        s.add(nc.vector.tensor_tensor(heads[:, lo:hi, :], heads[:, lo:hi, :], norm2[:, n:n + 1, :].to_broadcast([P, hi - lo, DH]), ALU.mult))
                    s.settle()
                    cos = rope[:, a.slot, 0:DH].rearrange("p (o n) -> p o n", o=1).to_broadcast([P, HEADS, DH])
                    s.add(nc.vector.tensor_tensor(ra[:], heads, cos, ALU.mult))
                    for axis in range(2):
                        lo = axis * DH // 2
                        mid, hi = lo + DH // 4, lo + DH // 2
                        for b, e, x, y in ((lo, mid, mid, hi), (mid, hi, lo, mid)):
                            sin = rope[:, a.slot, DH + b:DH + e].rearrange("p (o n) -> p o n", o=1).to_broadcast([P, HEADS, e - b])
                            s.add(nc.vector.tensor_tensor(rb[:, :, b:e], heads[:, :, x:y], sin, ALU.mult))
                    s.settle()
                    nc.vector.tensor_tensor(heads, ra[:], rb[:], ALU.add).then_inc(rotated, 1)
                    v.wait_ge(high_ready, a.t + 1)
                    nc.vector.tensor_tensor(q_parts[:, :, 1, :], heads[:, 0:AX_H, :], q_parts[:, :, 0, :].bitcast(F32), ALU.subtract)
                    for n in range(2):
                        last = nc.vector.tensor_tensor(k_parts[:, :, 2 + n, :], heads[:, AX_H:HEADS, :], k_parts[:, :, 0, :].bitcast(F32), ALU.subtract)
                    last.then_inc(parts_ready, 1)

                def copy_k(a):
                    v.wait_ge(qkT_done, a.t * 2 + 3)
                    nc.vector.tensor_copy(keys[:, :, bass.ds(a.t * P, P)], qkT_ps[:, QW - BATCH * P:].rearrange("p (j n) -> p j n", j=2 * AX_KV)).then_inc(k_ready, 1)

                def step(a, prior=True, following=True):
                    if prior:
                        rotate(a.next(-1))
                    if following:
                        norm(a.next())
                    if prior:
                        copy_k(a.next(-1))

                v.wait_ge(w_in, 96)
                v.sem_inc(x2_ready, 2)
                v.sem_inc(rotated, 2)
                v.sem_inc(xT_done, 2)
                v.sem_inc(parts_ready, 1)
                v.sem_inc(k_ready, 1)
                norm(Tile(0, 0))
                step(Tile(0, 0), prior=False)
                with s.loop(turns - 1, 2 * (5 + 9)) as i:
                    step(Tile(i, 1))
                    step(Tile(i, 2))
                step(Tile(0, LAST), following=False)
                step(Tile(0, TILES), following=False)


def axial_attention(c, m, keys, values, cat):
    nc = c.nc
    SET = AX_H // 2
    SHARE = SET // 2
    AHEAD = 2
    NB = 4
    with c.stage():
        ident = c.sb("ident", [P, P])
        q = c.sb("q", [P, 2, SET * P], F32R)
        p = c.sb("p", [P, NB, SEQ[1]])
        pT = c.sb("pT", [P, 2, SEQ[1] // P, SET, P])
        col = c.sb("col", [P, NB, 4])
        s_ps, t_ps, o_ps = [c.ps("s_ps0", SEQ[1]), c.ps("s_ps1", SEQ[1])], c.ps("t_ps", SEQ[1]), [c.ps("o_ps0", HALF), c.ps("o_ps1", HALF)]
        loaded, q_in = c.sem("loaded"), [c.sem("q_in0"), c.sem("q_in1")]
        scores, top_ready, expd, inverse, p_ready, pT_done, pT_ready, pv_done, o_out = (
            c.sem(n) for n in ("scores", "top_ready", "expd", "inverse", "p_ready", "pT_done", "pT_ready", "pv_done", "o_out"))

        def schedule(eng, g, run):
            first, tiles = GROUP_FIRST[g], GROUP_TILES[g]
            run(first, 0, 0, False)
            run(first, 1, 1, False)
            with eng.Fori(0, tiles - 2) as i:
                run(i + (first + 1), 0, 2, False)
                run(i + (first + 1), 1, 2, False)
            run(first + tiles - 1, 0, 2, False)
            run(first + tiles - 1, 1, 2, True)

        def set_before(tile, side):
            return (tile, 0) if side == 1 else (tile - 1, 1)

        def number(tile, side, n=0):
            return tile * AX_H + (side * SET + n)

        with c.block() as block:

            @block.sync
            def _(sp):
                sp.dma_start(ident[:], m["ident"]).then_inc(loaded, 16)
                with sp.Fori(0, TILES) as t:
                    for side in range(2):
                        sp.wait_ge(scores, number(t, side, SET))
                        sp.dma_start(q[:, side, :].bitcast(F32), m["qT_parts"][bass.ds(t * P, P), side * SET * P:(side + 1) * SET * P]).then_inc(q_in[side], 16)

            @block.tensor
            def _(pe):
                pe.sem_inc(scores, 2 * SET)
                pe.sem_inc(pT_done, NB)
                pe.sem_inc(pv_done, 2)
                pe.wait_ge(loaded, 16)
                for g in range(len(SEQ)):
                    nk, first = SEQ[g], GROUP_FIRST[g]

                    def qk(tile, side, n):
                        if n >= SET:
                            tile, side, n = (tile, 1, n - SET) if side == 0 else (tile + 1, 0, n - SET)
                        if n == 0:
                            pe.wait_ge(q_in[side], tile * 16 + 16)
                        pe.wait_ge(expd, number(tile, side, n + 1))
                        for b in range(nk // HALF):
                            at = first * P + b * HALF
                            for part in range(2):
                                last = nc.tensor.matmul(s_ps[n % 2][:, b * HALF:(b + 1) * HALF], q[:, side, n * P:(n + 1) * P],
                                                        keys[:, 2 * (2 * side + n // SHARE) + part, at:at + HALF], start=(part == 0), stop=(part == 1))
                        last.then_inc(scores, 1)

                    def turn(tile, side, n):
                        pe.wait_ge(p_ready, number(tile, side, n + 1))
                        pe.wait_ge(pT_ready, number(tile, side, n + 1))
                        for k in range(nk // P):
                            last = nc.tensor.transpose(t_ps[:, k * P:(k + 1) * P], p[:, n % NB, k * P:(k + 1) * P], ident[:])
                        last.then_inc(pT_done, 1)

                    def pv(tile, side, k):
                        if k == 0:
                            pe.wait_ge(o_out, tile * 2 + side + 1)
                        for kv in range(2):
                            last = nc.tensor.matmul(o_ps[side][DH * kv:DH * (kv + 1), :], values[:, first + k, (2 * side + kv) * DH:(2 * side + kv + 1) * DH],
                                                    pT[:, side, k, SHARE * kv:SHARE * (kv + 1), :].rearrange("p h n -> p (h n)"),
                                                    start=(k == 0), stop=(k == nk // P - 1))
                        if k == nk // P - 1:
                            last.then_inc(pv_done, 1)

                    def run(tile, side, before, at_last):
                        for n in range(SET):
                            if not (at_last and n + AHEAD >= SET):
                                qk(tile, side, n + AHEAD)
                            turn(tile, side, n)
                            if before and n < nk // P:
                                pv(*set_before(tile, side), n)

                    for n in range(AHEAD):
                        qk(first, 0, n)
                    schedule(pe, g, run)
                    pe.wait_ge(pT_ready, number(first + GROUP_TILES[g], 0, 1))
                    for k in range(nk // P):
                        pv(first + GROUP_TILES[g] - 1, 1, k)

            @block.vector
            def _(v):
                v.sem_inc(pT_ready, 1)
                for g in range(len(SEQ)):
                    nk, first = SEQ[g], GROUP_FIRST[g]

                    def top(tile, side, n):
                        v.wait_ge(scores, number(tile, side, n + 1 + 2 * SET))
                        nc.vector.tensor_reduce(col[:, n % NB, 0:1], s_ps[n % 2][:, 0:nk], AX.X, ALU.max, negate=True).then_inc(top_ready, 1)

                    def invert(tile, side, n):
                        v.wait_ge(expd, number(tile, side, n + 3))
                        nc.vector.reciprocal(col[:, n % NB, 2:3], col[:, n % NB, 1:2]).then_inc(inverse, 1)

                    def copy(tile, side, n):
                        v.wait_ge(pT_done, number(tile, side, n + 1 + NB))
                        if n == 0:
                            v.wait_ge(pv_done, tile * 2 + side + 1)
                        nc.vector.tensor_copy(pT[:, side, 0:nk // P, n, :], t_ps[:, 0:nk].rearrange("p (k n) -> p k n", k=nk // P)).then_inc(pT_ready, 1)

                    def run(tile, side, before, at_last):
                        for n in range(SET):
                            top(tile, side, n)
                            if n >= AHEAD:
                                copy(tile, side, n - AHEAD)
                            elif before:
                                copy(*set_before(tile, side), n - AHEAD + SET)
                            invert(tile, side, n)
                        if at_last:
                            for n in range(SET - AHEAD, SET):
                                copy(tile, side, n)

                    schedule(v, g, run)

            @block.scalar
            def _(act):
                act.sem_inc(expd, 2)
                act.sem_inc(o_out, 2)
                for g in range(len(SEQ)):
                    nk, first = SEQ[g], GROUP_FIRST[g]

                    def exps(tile, side, n):
                        act.wait_ge(top_ready, number(tile, side, n + 1))
                        act.wait_ge(pT_done, number(tile, side, n + 1))
                        nc.scalar.activation(p[:, n % NB, 0:nk], s_ps[n % 2][:, 0:nk], ACT.Exp, bias=col[:, n % NB, 0:1],
                                             accum_out=col[:, n % NB, 1:2]).then_inc(expd, 1)

                    def norm(tile, side, n):
                        act.wait_ge(inverse, number(tile, side, n + 1))
                        nc.scalar.activation(p[:, n % NB, 0:nk], p[:, n % NB, 0:nk], ACT.Copy, scale=col[:, n % NB, 2:3]).then_inc(p_ready, 1)

                    def out(tile, side):
                        act.wait_ge(pv_done, tile * 2 + side + 3)
                        nc.scalar.activation(cat[:, SHARE * side:SHARE * (side + 1), bass.ds(tile * P, P)],
                                             o_ps[side][:].rearrange("p (j n) -> p j n", j=SHARE), ACT.Copy).then_inc(o_out, 1)

                    def run(tile, side, before, at_last):
                        for n in range(SET):
                            exps(tile, side, n)
                            norm(tile, side, n)
                            if n == AHEAD and before == 2:
                                out(tile - 1, side)

                    schedule(act, g, run)
                    for side in range(2):
                        out(first + GROUP_TILES[g] - 1, side)


def final_norm(c, m):
    nc = c.nc
    with c.stage():
        gain, shift = c.sb("gain", [P, D]), c.sb("shift", [P, D])
        r, y = c.sb("r", [P, 2, D]), c.sb("y", [P, 2, D])
        stats, mv, half = c.sb("stats", [P, 12]), c.sb("mv", [P, 4]), c.sb("minus_half", [P, 1])
        loaded, r_in, y_out = c.sem("loaded"), [c.sem("r_in0"), c.sem("r_in1")], [c.sem("y_out0"), c.sem("y_out1")]
        dve, var_ready, rstd_ready, y_ready, const = (c.sem(n) for n in ("dve", "var_ready", "rstd_ready", "y_ready", "const"))
        turns = TILES // 2
        with c.block() as block:

            @block.sync
            def _(sp):
                sp.dma_start(gain[:], row_broadcast(m["ln2_g"][1])).then_inc(loaded, 16)
                sp.dma_start(shift[:], row_broadcast(m["ln2_b"][1])).then_inc(loaded, 16)
                sp.sem_inc(y_ready, 2)
                with sp.Fori(0, turns) as i:
                    for u in range(2):
                        sp.wait_ge(y_ready, i * 2 + u + 1)
                        sp.dma_start(r[:, u, :], m["acc"][bass.ds(i * 2 * P + u * P, P), :]).then_inc(r_in[u], 16)

            @block.gpsimd
            def _(pool):
                pool.memset(half[:], -0.5).then_inc(const, 1)
                pool.wait_ge(const, 1)
                with pool.Fori(0, TILES) as t:
                    pool.wait_ge(var_ready, t + 1)
                    pool.tensor_tensor(mv[:, 3:4], mv[:, 2:3], half[:], ALU.pow).then_inc(rstd_ready, 1)

            @block.vector
            def _(v):
                s = Steps(v, dve)
                v.wait_ge(loaded, 32)
                with s.loop(turns, 2 * 5) as i:
                    for u in range(2):
                        t = i * 2 + u
                        v.wait_ge(r_in[u], i * 16 + 16)
                        v.wait_ge(y_out[u], i * 16 + 16)
                        layer_norm_rows(nc, s, r[:, u, :], y[:, u, :], stats, mv, gain[:], shift[:], var_ready, rstd_ready, t).then_inc(y_ready, 1)

            @block.scalar
            def _(act):
                for u in range(2):
                    act.sem_inc(y_out[u], 16)
                with act.Fori(0, turns) as i:
                    for u in range(2):
                        act.wait_ge(y_ready, i * 2 + u + 3)
                        act.dma_start(m["y"][bass.ds(i * 2 * P + u * P, P), :], y[:, u, :]).then_inc(y_out[u], 16)
                for u in range(2):
                    act.wait_ge(y_out[u], 16 * turns + 16)


def trunk(nc, m, stop=99):
    m = dict(m)
    for name in ("x1", "x2", "acc", "qT"):
        m[name] = nc.dram_tensor(f"rows_{name}", (TOK, D), F32).ap()
    m["qT_parts"] = nc.dram_tensor("rows_qT_parts", (TOK, 2 * AX_Q), F32).ap()
    c = Core(nc)
    with c.stage():
        gates, rows = c.sb("gates", [P, 2 * PROMPT_ROW]), c.sb("rows", [P, 2 * PROMPT_ROW], U32)
        affinity = c.sb("affinity", [EXPERTS, TOK])
        with c.stage():
            cat = c.sb("cat", [P, KD, TOK])
            with c.stage():
                keys, values = c.sb("keys", [P, 2 * WIN_KV, TOK + 2 * P]), c.sb("values", [P, TILES + 2, WIN_KVD])
                glu = c.sb("glu", [P, CT, TOK])
                project_conv_window(c, m, glu, keys, values)
                if stop > 1: window_attention(c, m, keys, values, cat)
                if stop > 2: convolve(c, m, glu, cat)
            if stop > 3: project_out(c, m, 0, m["ab_w_out"][0], m["x"], cat, affinity)
        if stop > 4: choose(c, m, affinity, gates, rows)
        if stop > 5: experts(c, m, 0, gates, rows)
        with c.stage():
            if stop > 6:
                keys, values = c.sb("keys", [P, 2 * AX_KV, TOK], F32R), c.sb("values", [P, TILES, AX_KVD])
                project_axial(c, m, keys, values)
            if stop > 7:
                cat = c.sb("cat", [P, KD, TOK])
                axial_attention(c, m, keys, values, cat)
            if stop > 8: project_out(c, m, 1, m["c_w_out"][0], m["x2"], cat, affinity)
        if stop > 9: choose(c, m, affinity, gates, rows)
        if stop > 10: experts(c, m, 1, gates, rows)
        if stop > 11: final_norm(c, m)


def host_arrays(inputs):
    f32 = np.float32
    a = {n: np.ascontiguousarray(inputs[n]) for n in
         ("ab_w_in", "ab_sink", "ab_w_out", "c_w_in", "c_q_norm", "c_k_norm", "c_w_out", "ln1_g", "ln1_b",
          "moe_router", "moe_w_gate", "moe_w_up", "moe_w_down", "ln2_g", "ln2_b")}
    a["x"] = np.concatenate([np.asarray(inputs["x_prompt"]).reshape(-1, D), np.asarray(inputs["x_sample"]).reshape(-1, D)])
    a["conv_w"] = np.ascontiguousarray(np.asarray(inputs["ab_conv_w"])[0].reshape(TAPS, CT, P).transpose(2, 1, 0))
    for n, name in (("conv_b", "ab_conv_b"), ("conv_g", "ab_conv_ln_g"), ("conv_beta", "ab_conv_ln_b")):
        a[n] = np.ascontiguousarray(np.asarray(inputs[name])[0].reshape(CT, P).T)
    a["ident"] = np.eye(P, dtype=f32)
    pos = np.concatenate([np.arange(n) for n in SEQ])

    def angles(at, dim, theta):
        inv = f32(theta) ** (-np.arange(0, dim, 2, dtype=f32) / f32(dim))
        return at.astype(f32)[:, None] * inv[None, :]

    def table(*ang):
        cos = np.concatenate([np.concatenate([np.cos(x), np.cos(x)], 1) for x in ang], 1)
        sin = np.concatenate([np.concatenate([-np.sin(x), np.sin(x)], 1) for x in ang], 1)
        return np.concatenate([cos, sin], 1).astype(f32)

    a["rope_b"] = table(angles(pos, ROT, 500000.0))
    a["rope_c"] = table(angles(pos // GRID_W, DH // 2, 10000.0), angles(pos % GRID_W, DH // 2, 10000.0))
    mask = np.zeros((TILES, P, 3 * P), f32)
    for g, n in enumerate(SEQ):
        for b in range(n // P):
            qpos = b * P + np.arange(P)[:, None]
            kpos = (b - 1) * P + np.arange(3 * P)[None, :]
            mask[GROUP_FIRST[g] + b] = np.where((np.abs(kpos - qpos) <= P) & (kpos >= 0) & (kpos < n), 0.0, MASKED)
    a["mask"] = mask.reshape(TILES * P, 3 * P)
    return a


def kernel(**inputs):
    import concourse.bacc as bacc
    from concourse.bass_utils import run_bass_kernel_spmd

    nc = bacc.Bacc("TRN2", target_bir_lowering=False, num_devices=1)
    arrays = host_arrays(inputs)
    m = {n: nc.dram_tensor(n, a.shape, mybir.dt.from_np(a.dtype), kind="ExternalInput").ap() for n, a in arrays.items()}
    m["y"] = nc.dram_tensor("y", (TOK, D), F32, kind="ExternalOutput").ap()
    trunk(nc, m)
    y = run_bass_kernel_spmd(nc, [arrays], core_ids=[0]).results[0]["y"]
    return y[:SEQ[0]].reshape(1, SEQ[0], D), y[SEQ[0]:].reshape(1, SEQ[1], D)
```

```python
from contextlib import ExitStack, contextmanager

import numpy as np

import concourse.bass as bass
from concourse import mybir

P = 128
D = 1024
KD = D // P
SEQ = (512, 1024)
GROUP_TILES = tuple(s // P for s in SEQ)
GROUP_FIRST = (0, GROUP_TILES[0])
TILES = sum(GROUP_TILES)
TOK = TILES * P
HALF = 512
DEPTH = 2
DH = 64
CONV = 512
CT = CONV // P
TAPS = 31
WIN_H, WIN_KV = 8, 2
WIN_Q, WIN_KVD = WIN_H * DH, WIN_KV * DH
AB_IN = 2 * CONV + WIN_Q + 2 * WIN_KVD
ROT = DH // 4
AX_H, AX_KV = 16, 4
AX_Q, AX_KVD = AX_H * DH, AX_KV * DH
C_IN = AX_Q + 2 * AX_KVD
GRID_W = 64
EXPERTS = 16
CAP = tuple(2 * s // EXPERTS for s in SEQ)
SLOTS = sum(CAP)
ALPHA = (2 * DEPTH) ** 0.25
SCALE = DH ** -0.5
LN_EPS = 1e-5
RMS_EPS = 1e-6
MASKED = -1.0e30
PROMPT_ROW = 32

F32 = mybir.dt.float32
F32R = mybir.dt.float32r
U32 = mybir.dt.uint32
ALU = mybir.AluOpType
ACT = mybir.ActivationFunctionType
AX = mybir.AxisListType


class Steps:

    def __init__(self, eng, sem):
        self.eng, self.sem, self.base, self.here = eng, sem, 0, 0

    def add(self, instruction):
        instruction.then_inc(self.sem, 1)
        self.here += 1
        return self.base + self.here

    def settle(self):
        self.eng.wait_ge(self.sem, self.base + self.here)

    def link(self, instruction):
        self.add(instruction)
        self.settle()

    @contextmanager
    def loop(self, turns, each):
        start = self.base + self.here
        with self.eng.Fori(0, turns) as i:
            self.base, self.here = start + i * each, 0
            yield i
            assert self.here == each, (self.here, each)
        self.base, self.here = start + turns * each, 0


class Tile:

    def __init__(self, i, n):
        self.t, self.pair, self.slot = i * 2 + n, i + n // 2, n % 2
        self.i, self.n = i, n

    def next(self, by=1):
        return Tile(self.i, self.n + by)


def tile_steps(loop, step):
    step(Tile(0, 0), True, True, False, False)
    step(Tile(0, 1), True, True, True, False)
    with loop as i:
        step(Tile(i, 2), True, True, True, True)
        step(Tile(i, 3), True, True, True, True)
    step(Tile(0, TILES - 2), True, True, True, True)
    step(Tile(0, TILES - 1), True, False, True, True)
    step(Tile(0, TILES), False, False, True, True)
    step(Tile(0, TILES + 1), False, False, False, True)


class Core:

    def __init__(self, nc):
        self.nc, self.count, self.stack, self.sems = nc, 0, None, None

    @contextmanager
    def stage(self):
        outer = self.stack, self.sems
        self.sems = []
        with ExitStack() as self.stack:
            yield
            if self.sems:
                self.nc.clear_and_free_semaphores(self.sems)
                self.nc.all_engine_barrier()
        self.stack, self.sems = outer

    def sb(self, name, shape, dt=F32):
        self.count += 1
        return self.stack.enter_context(self.nc.sbuf_tensor(f"{name}_{self.count}", shape, dt))

    def ps(self, name, cols):
        self.count += 1
        return self.stack.enter_context(self.nc.psum_tensor(f"{name}_{self.count}", [P, cols], F32))

    def sem(self, name):
        self.count += 1
        self.sems.append(self.nc.alloc_semaphore(f"{name}_{self.count}"))
        return self.sems[-1]

    def block(self):
        return self.nc.Block()


def row_broadcast(vector, parts=P):
    return vector.rearrange("(o n) -> o n", o=1).to_broadcast([parts, vector.shape[0]])


def layer_norm_rows(nc, steps, row, out, stats, mv, gain, shift, var_ready, rstd_ready, tile):
    n = row.shape[1] // HALF
    for h in range(n):
        steps.add(nc.vector.bn_stats(stats[:, 6 * h:6 * h + 6], row[:, h * HALF:(h + 1) * HALF]))
    steps.settle()
    nc.vector.memset(mv[:, 2:3], 0.0)
    steps.link(nc.vector.bn_aggr(mv[:, 0:2], stats[:, 0:6 * n]))
    nc.vector.tensor_scalar(mv[:, 2:3], mv[:, 1:2], LN_EPS, None, ALU.add).then_inc(var_ready, 1)
    steps.eng.wait_ge(rstd_ready, tile + 1)
    steps.link(nc.vector.tensor_scalar(out, row, mv[:, 0:1], mv[:, 3:4], ALU.subtract, ALU.mult))
    if shift is None:
        return nc.vector.tensor_tensor(out, out, gain, ALU.mult)
    steps.link(nc.vector.tensor_tensor(out, out, gain, ALU.mult))
    return nc.vector.tensor_tensor(out, out, shift, ALU.add)


def project_conv_window(c, m, glu, keys, values):
    nc = c.nc
    QK = WIN_Q + WIN_KVD
    QK2 = QK + WIN_KVD
    with c.stage():
        w = c.sb("w_in", [P, KD, AB_IN])
        ident = c.sb("ident", [P, P])
        x = c.sb("x", [P, 2, D])
        rope = c.sb("rope", [P, 2, 2 * ROT])
        xT = c.sb("xT", [P, 2, D])
        sig = c.sb("sig", [P, 2, CONV])
        qk = c.sb("qk", [P, 2, QK2])
        ra = c.sb("ra", [P, QK // DH, ROT])
        rb = c.sb("rb", [P, QK // DH, ROT])
        qT = c.sb("qT", [P, 2, WIN_Q])
        xT_ps, ug_ps, qkv_ps, qkT_ps = (c.ps(n, 1024) for n in ("xT_ps", "ug_ps", "qkv_ps", "qkT_ps"))
        ident_in, qkv_in, w_in, x_in = c.sem("ident_in"), c.sem("qkv_in"), c.sem("w_in"), [c.sem("x_in0"), c.sem("x_in1")]
        xT_done, xT_ready, ug_done, sig_ready = c.sem("xT_done"), c.sem("xT_ready"), c.sem("ug_done"), c.sem("sig_ready")
        glu_ready, qkv_done, qk_ready, qkT_done = c.sem("glu_ready"), c.sem("qkv_done"), c.sem("qk_ready"), c.sem("qkT_done")
        qT_ready, k_ready, q_stored = c.sem("qT_ready"), c.sem("k_ready"), [c.sem("q_out0"), c.sem("q_out1")]
        dve, zero = c.sem("dve"), c.sem("zero")
        with c.block() as block:

            @block.sync
            def _(sp):
                def load(a):
                    sp.dma_start(x[:, a.slot, :], m["x"][bass.ds(a.t * P, P), :]).then_inc(x_in[a.slot], 16)
                    sp.dma_start(rope[:, a.slot, :], m["rope_b"][bass.ds(a.t * P, P), :]).then_inc(x_in[a.slot], 16)

                sp.dma_start(ident[:], m["ident"]).then_inc(ident_in, 16)
                load(Tile(0, 0))
                win = m["ab_w_in"][0].rearrange("(k p) n -> p k n", p=P)
                sp.dma_start(w[:, :, 2 * CONV:AB_IN], win[:, :, 2 * CONV:AB_IN]).then_inc(qkv_in, 16)
                load(Tile(0, 1))
                sp.dma_start(w[:, :, 0:2 * CONV], win[:, :, 0:2 * CONV]).then_inc(w_in, 16)
                with sp.Fori(0, TILES // 2 - 1) as i:
                    for n in range(2):
                        a = Tile(i, 2 + n)
                        sp.wait_ge(xT_done, a.t + 1)
                        sp.wait_ge(qk_ready, a.t + 1)
                        load(a)

            @block.tensor
            def _(pe):
                def turn_x(a):
                    pe.wait_ge(x_in[a.slot], a.pair * 32 + 32)
                    for k in range(KD):
                        last = nc.tensor.transpose(xT_ps[:, k * P:(k + 1) * P], x[:, a.slot, k * P:(k + 1) * P], ident[:])
                    last.then_inc(xT_done, 1)

                def step(a, following=True):
                    u, t = a.slot, a.t
                    pe.wait_ge(xT_ready, t + 1)
                    pe.wait_ge(qk_ready, t + 2)
                    for base, cols in ((0, WIN_Q), (WIN_Q, 2 * WIN_KVD)):
                        for k in range(KD):
                            last = nc.tensor.matmul(qkv_ps[:, base:base + cols], xT[:, u, k * P:(k + 1) * P],
                                                    w[:, k, 2 * CONV + base:2 * CONV + base + cols],
                                                    start=(k == 0), stop=(k == KD - 1))
                    last.then_inc(qkv_done, 1)
                    if following:
                        turn_x(a.next())
                    pe.wait_ge(w_in, 16)
                    pe.wait_ge(glu_ready, t + 1)
                    for ct in range(2 * CT):
                        for k in range(KD):
                            last = nc.tensor.matmul(ug_ps[:, ct * P:(ct + 1) * P], w[:, k, ct * P:(ct + 1) * P],
                                                    xT[:, u, k * P:(k + 1) * P], start=(k == 0), stop=(k == KD - 1))
                    last.then_inc(ug_done, 1)
                    pe.wait_ge(qk_ready, t + 3)
                    pe.wait_ge(k_ready, t + 1)
                    for j in range(QK2 // P):
                        last = nc.tensor.transpose(qkT_ps[:, j * P:(j + 1) * P], qk[:, u, j * P:(j + 1) * P], ident[:])
                    last.then_inc(qkT_done, 1)

                pe.sem_inc(xT_done, 2)
                pe.wait_ge(ident_in, 16)
                turn_x(Tile(0, 0))
                pe.wait_ge(qkv_in, 16)
                with pe.Fori(0, TILES // 2 - 1) as i:
                    step(Tile(i, 0))
                    step(Tile(i, 1))
                step(Tile(0, TILES - 2))
                step(Tile(0, TILES - 1), following=False)

            @block.scalar
            def _(act):
                def copy_x(a):
                    act.wait_ge(xT_done, a.t + 3)
                    nc.scalar.activation(xT[:, a.slot, :], xT_ps[:], ACT.Copy).then_inc(xT_ready, 1)

                def step(a, following=True):
                    u, t = a.slot, a.t
                    if following:
                        copy_x(a.next())
                    act.wait_ge(ug_done, t + 1)
                    nc.scalar.activation(sig[:, u, :], ug_ps[:, CONV:2 * CONV], ACT.Sigmoid).then_inc(sig_ready, 1)
                    act.wait_ge(qkT_done, t + 1)
                    act.wait_ge(q_stored[u], a.pair * 16 + 16)
                    nc.scalar.activation(qT[:, u, :], qkT_ps[:, 0:WIN_Q], ACT.Copy).then_inc(qT_ready, 1)
                    act.wait_ge(qT_ready, t + 1)
                    act.dma_start(m["qT"][bass.ds(t * P, P), 0:WIN_Q], qT[:, u, :]).then_inc(q_stored[u], 16)
                    act.wait_ge(zero, 2)
                    at = bass.ds((t + 1) * P, P)
                    kT = qkT_ps[:, WIN_Q:QK2].rearrange("p (j n) -> p j n", j=WIN_KV)
                    nc.scalar.activation(keys[0:DH, 0:WIN_KV, at], kT[0:DH], ACT.Copy)
                    nc.scalar.activation(keys[DH:P, WIN_KV:2 * WIN_KV, at], kT[DH:P], ACT.Copy).then_inc(k_ready, 1)

                act.sem_inc(k_ready, 1)
                for u in range(2):
                    act.sem_inc(q_stored[u], 16)
                copy_x(Tile(0, 0))
                with act.Fori(0, TILES // 2 - 1) as i:
                    step(Tile(i, 0))
                    step(Tile(i, 1))
                step(Tile(0, TILES - 2))
                step(Tile(0, TILES - 1), following=False)
                for u in range(2):
                    act.wait_ge(q_stored[u], 16 * (TILES // 2) + 16)

            @block.vector
            def _(v):
                s = Steps(v, dve)
                nc.vector.memset(keys[:], 0.0).then_inc(zero, 1)
                nc.vector.memset(values[:], 0.0).then_inc(zero, 1)
                v.wait_ge(zero, 2)
                v.sem_inc(qk_ready, 2)
                v.sem_inc(glu_ready, 1)
                heads = QK // DH
                with s.loop(TILES // 2, 2 * 7) as i:
                    for u in range(2):
                        t = i * 2 + u
                        v.wait_ge(qkv_done, t + 1)
                        v.wait_ge(xT_done, t + 3)
                        s.add(nc.vector.tensor_copy(values[:, bass.ds(t + 1, 1), :], qkv_ps[:, QK:QK + WIN_KVD].rearrange("p (o n) -> p o n", o=1)))
                        s.link(nc.vector.tensor_copy(qk[:, u, 0:QK], qkv_ps[:, 0:QK]))
                        v.wait_ge(x_in[u], i * 32 + 32)
                        rot = qk[:, u, 0:QK].rearrange("p (h d) -> p h d", d=DH)
                        cos = rope[:, u, 0:ROT].rearrange("p (o n) -> p o n", o=1).to_broadcast([P, heads, ROT])
                        h2 = ROT // 2
                        s0 = rope[:, u, ROT:ROT + h2].rearrange("p (o n) -> p o n", o=1).to_broadcast([P, heads, h2])
                        s1 = rope[:, u, ROT + h2:2 * ROT].rearrange("p (o n) -> p o n", o=1).to_broadcast([P, heads, h2])
                        s.add(nc.vector.tensor_tensor(ra[:], rot[:, :, 0:ROT], cos, ALU.mult))
                        s.add(nc.vector.tensor_tensor(rb[:, :, 0:h2], rot[:, :, h2:ROT], s0, ALU.mult))
                        s.add(nc.vector.tensor_tensor(rb[:, :, h2:ROT], rot[:, :, 0:h2], s1, ALU.mult))
                        s.settle()
                        s.link(nc.vector.tensor_tensor(rot[:, :, 0:ROT], ra[:], rb[:], ALU.add))
                        s.add(nc.vector.tensor_copy(qk[:, u, QK:QK + DH], qk[:, u, WIN_Q + DH:QK]))
                        nc.vector.tensor_copy(qk[:, u, QK + DH:QK2], qk[:, u, WIN_Q:WIN_Q + DH]).then_inc(qk_ready, 1)
                        v.wait_ge(sig_ready, t + 1)
                        nc.vector.tensor_tensor(glu[:, :, bass.ds(t * P, P)], ug_ps[:, 0:CONV].rearrange("p (c n) -> p c n", c=CT),
                                                sig[:, u, :].rearrange("p (c n) -> p c n", c=CT), ALU.mult).then_inc(glu_ready, 1)


def window_and_taps(c, m, keys, values, glu, conv, cat):
    nc = c.nc
    G = WIN_H // WIN_KV
    NK = 3 * P
    TURN = TILES // CT
    UNITS = TURN * WIN_KV
    MID = TAPS // 2
    RING = 6
    CUT_TOKENS = SEQ[0] + 192
    SOONER = 2
    place = {(0, 0): 0, (1, 0): 1, (1, 1): 2, (0, 1): 3}
    with c.stage():
        ident = c.sb("ident", [P, P])
        sink = c.sb("sink", [P, 2, WIN_H])
        q = c.sb("q", [P, TURN, WIN_Q])
        mask = c.sb("mask", [P, TURN, NK])
        taps = c.sb("taps", [P, CT, TAPS])
        conv_b = c.sb("conv_b", [P, CT])
        product = c.sb("product", [P, RING, CUT_TOKENS + MID])
        sm = c.sb("sm", [P, 2, G, NK])
        mx = c.sb("mx", [P, 2, 6, G])
        still = c.sb("still", [P, 1])
        pT = c.sb("pT", [P, 2, G * NK])
        o = c.sb("o", [P, TURN, WIN_Q])
        s_ps, t_ps, o_ps = c.ps("s_ps", 4 * HALF), c.ps("t_ps", G * NK), c.ps("o_ps", WIN_Q)
        loaded, q_in = c.sem("loaded"), [c.sem(f"q_in{u}") for u in range(TURN)]
        scores, masked, bias, expd, pT_done, pT_act, pT_dve, o_done, o_ready, oT_done, oT_out, dve, tapped, scaled, summed = (
            c.sem(n) for n in ("scores", "masked", "bias", "expd", "pT_done", "pT_act", "pT_dve", "o_done", "o_ready",
                               "oT_done", "oT_out", "dve", "tapped", "scaled", "summed"))
        CUT = 2 * HALF
        with c.block() as block:

            @block.sync
            def _(sp):
                sp.dma_start(ident[:], m["ident"]).then_inc(loaded, 16)
                sp.dma_start(sink[:, 0, :], row_broadcast(m["ab_sink"][0])).then_inc(loaded, 16)
                sp.dma_start(taps[:], m["conv_w"]).then_inc(loaded, 16)
                sp.dma_start(conv_b[:], m["conv_b"]).then_inc(loaded, 16)
                with sp.Fori(0, CT) as i:
                    for u in range(TURN):
                        t = i * TURN + u
                        sp.wait_ge(o_ready, t + 1)
                        sp.dma_start(q[:, u, :], m["qT"][bass.ds(t * P, P), 0:WIN_Q]).then_inc(q_in[u], 16)
                        sp.dma_start(mask[:, u, :], m["mask"][bass.ds(t * P, P), :]).then_inc(q_in[u], 16)

            order = [MID] + [x for x in range(TAPS) if x != MID]
            BY_POOL = ((0, SEQ[0]), (SEQ[0], CUT_TOKENS))
            BY_VECTOR = ((CUT_TOKENS, (CUT_TOKENS + TOK) // 2), ((CUT_TOKENS + TOK) // 2, TOK))

            def reach(part, step):
                g = 0 if part[0] < SEQ[0] else 1
                a, b = GROUP_FIRST[g] * P, (GROUP_FIRST[g] + GROUP_TILES[g]) * P
                return max(part[0], a - step), min(part[1], b - step)

            @block.gpsimd
            def _(pool):
                pool.sem_inc(summed, 2 * RING)
                for i in range(CT):
                    for at in range(1, TAPS):
                        pool.wait_ge(scaled, i * TAPS + at + 1)
                        step, before = order[at] - MID, i * (2 * TAPS - 2) + 2 * (at - 1)
                        for j, part in enumerate(BY_POOL):
                            lo, hi = reach(part, step)
                            pool.wait_ge(summed, before + (j - 1 + 2 * RING))
                            pool.tensor_tensor(conv[:, i:i + 1, lo:hi], conv[:, i:i + 1, lo:hi],
                                               product[:, at % RING:at % RING + 1, lo + step:hi + step], ALU.add).then_inc(summed, 1)

            def unit(n):
                return n // 2, n % 2, n % 2

            def turns(loop, turn):
                turn(0, None)
                with loop as i:
                    turn(i, False)
                turn(CT - 1, True)

            @block.tensor
            def _(pe):
                pe.wait_ge(loaded, 64)
                def turn(i, at_last):

                    def qk(n):
                        u, kv, _ = unit(n)
                        if kv == 0:
                            pe.wait_ge(q_in[u % TURN], i * 32 + (u // TURN * 32 + 32))
                        pe.wait_ge(masked, (i * UNITS + n) * G + 1)
                        for h in range(G):
                            head = kv * G + h
                            last = nc.tensor.matmul(s_ps[:, h * HALF:h * HALF + NK], q[:, u % TURN, (head // 2) * P:(head // 2 + 1) * P],
                                                    keys[:, place[kv, head % 2], bass.ds((i * TURN + u) * P, NK)], start=True, stop=True)
                        last.then_inc(scores, 1)

                    def pv(n):
                        u, kv, b = unit(n)
                        pe.wait_ge(expd, i * UNITS + n + 1)
                        pe.wait_ge(pT_act, i * UNITS + n + 1)
                        pe.wait_ge(pT_dve, i * UNITS + n + 1)
                        if kv == 0:
                            pe.wait_ge(oT_out, i * TURN + u + 1)
                        for h in range(G):
                            for k in range(3):
                                last = nc.tensor.transpose(t_ps[:, (h * 3 + k) * P:(h * 3 + k + 1) * P], sm[:, b, h, k * P:(k + 1) * P], ident[:])
                        last.then_inc(pT_done, 1)
                        pe.wait_ge(pT_act, i * UNITS + n + 2)
                        pe.wait_ge(pT_dve, i * UNITS + n + 2)
                        if kv == 0:
                            pe.wait_ge(o_ready, i * TURN + u + TURN)
                        for h in range(G):
                            head = kv * G + h
                            for k in range(3):
                                last = nc.tensor.matmul(o_ps[:, head * DH:(head + 1) * DH], pT[:, b, (h * 3 + k) * P:(h * 3 + k + 1) * P],
                                                        values[:, bass.ds(i * TURN + u + k, 1), kv * DH:(kv + 1) * DH],
                                                        start=(k == 0), stop=(k == 2))
                        last.then_inc(o_done, 1)

                    def turn_out(u, n):
                        pe.wait_ge(o_ready, i * TURN + u + 1 + TURN)
                        pe.wait_ge(pT_act, i * UNITS + n + 2)
                        pe.wait_ge(pT_dve, i * UNITS + n + 2)
                        for j in range(CT):
                            last = nc.tensor.transpose(t_ps[:, j * P:(j + 1) * P], o[:, u, j * P:(j + 1) * P], ident[:])
                        last.then_inc(oT_done, 1)

                    if at_last is None:
                        return qk(0)
                    for n in range(UNITS):
                        if n < UNITS - 1 or not at_last:
                            qk(n + 1)
                        if n and n % WIN_KV == 0:
                            turn_out(n // WIN_KV - 1, n - 1)
                        pv(n)
                    turn_out(TURN - 1, UNITS - 1)

                turns(pe.Fori(0, CT - 1), turn)

            @block.vector
            def _(v):
                s = Steps(v, dve)
                v.wait_ge(loaded, 64)
                v.sem_inc(masked, 1)
                v.sem_inc(pT_dve, 1)
                v.sem_inc(o_ready, TURN)
                def turn(i, at_last):

                    def convolve(n, part):
                        lo, hi = TAPS * n // UNITS, TAPS * (n + 1) // UNITS
                        mid = lo + SOONER
                        for at in range(lo, mid) if part == 0 else range(mid, hi):
                            for j, part in enumerate(BY_VECTOR):
                                if at:
                                    v.wait_ge(tapped, i * (2 * TAPS) + (2 * at + j - 1))
                                one, step = bass.ds(i, 1), order[at] - MID
                                lo, hi = reach(part, step)
                                weight = taps[:, one, order[at]:order[at] + 1]
                                if at == 0:
                                    last = nc.vector.tensor_scalar(conv[:, one, lo:hi], glu[:, one, lo:hi], weight, conv_b[:, one], ALU.mult, ALU.add)
                                else:
                                    last = nc.vector.scalar_tensor_tensor(conv[:, one, lo:hi], glu[:, one, lo + step:hi + step], weight,
                                                                          conv[:, one, lo:hi], ALU.mult, ALU.add)
                                last.then_inc(tapped, 1)


                    def soft(n):
                        u, kv, b = unit(n)
                        v.wait_ge(scores, i * UNITS + n + 1)
                        v.wait_ge(pT_done, i * UNITS + n + 1)
                        if kv == 0:
                            v.wait_ge(q_in[u % TURN], i * 32 + (u // TURN * 32 + 32))
                        nc.vector.memset(still[:], 0.0)
                        for h in range(G):
                            nc.vector.tensor_tensor_reduce(out=sm[:, b, h, :], in0=s_ps[:, h * HALF:h * HALF + NK], in1=mask[:, u % TURN, :],
                                                           scale=SCALE, scalar=MASKED, op0=ALU.add, op1=ALU.max,
                                                           accum_out=mx[:, b, 0, h:h + 1]).then_inc(masked, 1)
                        v.wait_ge(masked, (i * UNITS + n) * G + G + 1)
                        snk = sink[:, 0, kv * G:(kv + 1) * G]
                        s.link(nc.vector.tensor_tensor(mx[:, b, 1, :], mx[:, b, 0, :], snk, ALU.max))
                        s.add(nc.vector.tensor_scalar(mx[:, b, 2, :], mx[:, b, 1, :], -1.0, None, ALU.mult))
                        nc.vector.tensor_tensor(mx[:, b, 3, :], snk, mx[:, b, 1, :], ALU.subtract).then_inc(bias, 1)

                    def after(n):
                        u, kv, b = unit(n)
                        v.wait_ge(expd, i * UNITS + n + 1)
                        s.link(nc.vector.tensor_tensor(mx[:, b, 4, :], mx[:, b, 4, :], mx[:, b, 5, :], ALU.add))
                        s.link(nc.vector.reciprocal(sink[:, 1, kv * G:(kv + 1) * G], mx[:, b, 4, :]))
                        v.wait_ge(pT_done, i * UNITS + n + 3)
                        nc.vector.tensor_copy(pT[:, b, CUT:G * NK], t_ps[:, CUT:G * NK]).then_inc(pT_dve, 1)

                    def out(u):
                        v.wait_ge(o_done, i * UNITS + u * WIN_KV + 2)
                        v.wait_ge(oT_done, i * TURN + u + 1)
                        nc.vector.tensor_tensor(o[:, u, :].rearrange("p (h d) -> p h d", d=DH), o_ps[:].rearrange("p (h d) -> p h d", d=DH),
                                                sink[:, 1, :].rearrange("p (h o) -> p h o", o=1).to_broadcast([P, WIN_H, DH]),
                                                ALU.mult).then_inc(o_ready, 1)

                    if at_last is None:
                        return soft(0)
                    for n in range(UNITS):
                        after(n)
                        if n < UNITS - 1 or not at_last:
                            soft(n + 1)
                        convolve(n, 0)
                        if n % WIN_KV == 1:
                            out(n // WIN_KV)
                        convolve(n, 1)

                turns(s.loop(CT - 1, UNITS * 4), turn)

            @block.scalar
            def _(act):
                act.wait_ge(loaded, 64)
                act.sem_inc(pT_done, 2)
                act.sem_inc(oT_done, TURN)
                act.sem_inc(pT_act, 1)
                act.sem_inc(oT_out, 1)
                def turn(i, at_last):

                    def scale(n):
                        for at in range(TAPS * n // UNITS, TAPS * (n + 1) // UNITS):
                            one = bass.ds(i, 1)
                            weight = taps[:, one, order[at]:order[at] + 1]
                            if at == 0:
                                nc.scalar.activation(conv[:, one, 0:CUT_TOKENS], glu[:, one, 0:CUT_TOKENS], ACT.Identity,
                                                     bias=conv_b[:, one], scale=weight).then_inc(scaled, 1)
                            else:
                                act.wait_ge(summed, i * (2 * TAPS - 2) + 2 * at)
                                nc.scalar.activation(product[:, at % RING:at % RING + 1, :], glu[:, one, 0:CUT_TOKENS + MID], ACT.Copy,
                                                     scale=weight).then_inc(scaled, 1)

                    def exps(n):
                        u, kv, b = unit(n)
                        act.wait_ge(bias, i * UNITS + n + 1)
                        for h in range(G):
                            nc.scalar.activation(sm[:, b, h, :], sm[:, b, h, :], ACT.Exp, bias=mx[:, b, 2, h:h + 1],
                                                 accum_out=mx[:, b, 4, h:h + 1])
                        nc.scalar.activation(mx[:, b, 5, :], mx[:, b, 3, :], ACT.Exp).then_inc(expd, 1)

                    def after(n):
                        u, kv, b = unit(n)
                        act.wait_ge(pT_done, i * UNITS + n + 3)
                        nc.scalar.activation(pT[:, b, 0:CUT], t_ps[:, 0:CUT], ACT.Copy).then_inc(pT_act, 1)

                    def out(u):
                        act.wait_ge(oT_done, i * TURN + u + 1 + TURN)
                        nc.scalar.activation(cat[:, CT:2 * CT, bass.ds((i * TURN + u) * P, P)],
                                             t_ps[:, 0:WIN_Q].rearrange("p (c n) -> p c n", c=CT), ACT.Copy).then_inc(oT_out, 1)

                    if at_last is None:
                        return exps(0)
                    for n in range(UNITS):
                        if n and n % WIN_KV == 0:
                            out(n // WIN_KV - 1)
                        after(n)
                        if n < UNITS - 1 or not at_last:
                            exps(n + 1)
                        scale(n)
                    out(TURN - 1)

                turns(act.Fori(0, CT - 1), turn)


def norm_channels(c, m, acc, cat):
    nc = c.nc
    with c.stage():
        par = c.sb("conv_par", [P, 2, CT])
        ones = c.sb("ones", [P, P])
        eps = c.sb("eps", [P, 1])
        sq = c.sb("sq", [P, 2, CT, HALF])
        rstd = c.sb("rstd", [P, TOK // HALF, HALF])
        mean_ps, var_ps = c.ps("mean_ps", TOK), c.ps("var_ps", HALF)
        loaded, dve, const = c.sem("loaded"), c.sem("dve"), c.sem("const")
        mean_done, centred, squared, var_done, rooted, normed, cat_done = (
            c.sem(n) for n in ("mean_done", "centred", "squared", "var_done", "rooted", "normed", "cat_done"))
        chunks = TOK // HALF
        with c.block() as block:

            @block.sync
            def _(sp):
                for n, name in enumerate(("conv_g", "conv_beta")):
                    sp.dma_start(par[:, n, :], m[name]).then_inc(loaded, 16)

            @block.gpsimd
            def _(pool):
                pool.memset(ones[:], 1.0 / CONV).then_inc(const, 1)
                pool.memset(eps[:], LN_EPS).then_inc(const, 1)

            @block.vector
            def _(v):
                s = Steps(v, dve)
                v.wait_ge(loaded, 32)
                for n in range(chunks):
                    part = acc[:, :, n * HALF:(n + 1) * HALF]
                    v.wait_ge(mean_done, n + 1)
                    for ct in range(CT):
                        nc.vector.tensor_tensor(part[:, ct, :], part[:, ct, :], mean_ps[:, n * HALF:(n + 1) * HALF], ALU.subtract).then_inc(centred, 1)
                for n in range(chunks):
                    part = acc[:, :, n * HALF:(n + 1) * HALF]
                    v.wait_ge(rooted, n + 1)
                    s.link(nc.vector.reciprocal(rstd[:, n, :], rstd[:, n, :]))
                    v.wait_ge(centred, CT * (n + 1))
                    for ct in range(CT):
                        nc.vector.tensor_tensor(part[:, ct, :], part[:, ct, :], rstd[:, n, :], ALU.mult).then_inc(normed, 1)

            @block.tensor
            def _(pe):
                def mean(n):
                    for ct in range(CT):
                        last = nc.tensor.matmul(mean_ps[:, n * HALF:(n + 1) * HALF], ones[:], acc[:, ct, n * HALF:(n + 1) * HALF],
                                                start=(ct == 0), stop=(ct == CT - 1))
                    last.then_inc(mean_done, 1)

                def variance(n):
                    pe.wait_ge(squared, n + 1)
                    if n:
                        pe.wait_ge(rooted, n)
                    for ct in range(CT):
                        last = nc.tensor.matmul(var_ps[:], ones[:], sq[:, n % 2, ct, :], start=(ct == 0), stop=(ct == CT - 1))
                    last.then_inc(var_done, 1)

                pe.wait_ge(const, 1)
                mean(0)
                for n in range(chunks):
                    if n + 1 < chunks:
                        mean(n + 1)
                    variance(n)

            @block.scalar
            def _(act):
                act.wait_ge(const, 2)
                act.wait_ge(loaded, 32)
                for n in range(chunks):
                    part = acc[:, :, n * HALF:(n + 1) * HALF]
                    act.wait_ge(centred, CT * (n + 1))
                    if n >= 2:
                        act.wait_ge(var_done, n - 1)
                    nc.scalar.activation(sq[:, n % 2], part, ACT.Square).then_inc(squared, 1)
                    act.wait_ge(var_done, n + 1)
                    nc.scalar.activation(rstd[:, n, :], var_ps[:], ACT.Sqrt, bias=eps[:]).then_inc(rooted, 1)
                for n in range(chunks):
                    part = acc[:, :, n * HALF:(n + 1) * HALF]
                    act.wait_ge(normed, CT * (n + 1))
                    for ct in range(CT):
                        nc.scalar.activation(cat[:, ct, n * HALF:(n + 1) * HALF], part[:, ct, :], ACT.Silu,
                                             bias=par[:, 1, ct:ct + 1], scale=par[:, 0, ct:ct + 1]).then_inc(cat_done, 1)


def project_out(c, m, layer, w_out, x_src, cat, affinity, spare):
    nc = c.nc
    with c.stage():
        raw = c.sb("w_raw", [P, 2, D])
        wh = c.sb("w_high", [P, KD, D], F32R)
        wl = spare[:, 0:KD * D].rearrange("p (k n) -> p k n", k=KD)
        wr = c.sb("router", [P, KD, EXPERTS])
        ident = c.sb("ident", [P, P])
        gain, shift = c.sb("gain", [P, D]), c.sb("shift", [P, D])
        ah, al = (spare[:, (KD + 2 * n) * D:(KD + 2 * n + 2) * D].rearrange("p (u k n) -> p u k n", u=2, k=KD) for n in range(2))
        x = c.sb("x", [P, 2, D])
        row = c.sb("row", [P, D])
        stats, mv = c.sb("stats", [P, 12]), c.sb("mv", [P, 4])
        half = c.sb("minus_half", [P, 1])
        x1, ax1 = c.sb("x1", [P, 2, D]), c.sb("ax1", [P, 2, D])
        xT = c.sb("xT", [P, D])
        prob, pr = c.sb("prob", [P, EXPERTS]), c.sb("prob_stats", [P, 4])
        y_ps, t_ps = [c.ps("y_ps0", D), c.ps("y_ps1", D)], c.ps("t_ps", D)
        r_ps, rT_ps = c.ps("r_ps", HALF), c.ps("rT_ps", HALF)
        tables_in, w_in, a_in = c.sem("tables_in"), [c.sem("w_in0"), c.sem("w_in1")], [c.sem("a_in0"), c.sem("a_in1")]
        w_high, w_low, a_high, a_low = c.sem("w_high"), c.sem("w_low"), c.sem("a_high"), c.sem("a_low")
        y_done, res_done, var_ready, rstd_ready, x1_ready, ax_ready, xT_done, xT_ready, r_done, neg_ready, exp_done, prob_ready, rT_done, aff_ready, dve, const = (
            c.sem(n) for n in ("y_done", "res_done", "var_ready", "rstd_ready", "x1_ready", "ax_ready", "xT_done", "xT_ready", "r_done",
                               "neg_ready", "exp_done", "prob_ready", "rT_done", "aff_ready", "dve", "const"))
        x1_out = [c.sem("x1_out0"), c.sem("x1_out1")]
        with c.block() as block:

            @block.sync
            def _(sp):
                def load(a):
                    sp.dma_start(x[:, a.slot, :], x_src[bass.ds(a.t * P, P), :]).then_inc(a_in[a.slot], 16)

                for k in range(KD):
                    if k >= 2:
                        sp.wait_ge(w_low, k - 1)
                    for side in range(2):
                        head = 2 * k + side if layer == 0 else k // 4 * 8 + side * 4 + k % 4
                        sp.dma_start(raw[DH * side:DH * (side + 1), k % 2, :], w_out[head * DH:(head + 1) * DH, :]).then_inc(w_in[k % 2], 16)
                    if k == 1:
                        sp.dma_start(wr[:], m["moe_router"][layer].rearrange("(k p) n -> p k n", p=P)).then_inc(tables_in, 16)
                        sp.dma_start(ident[:], m["ident"]).then_inc(tables_in, 16)
                        sp.dma_start(gain[:], row_broadcast(m["ln1_g"][layer])).then_inc(tables_in, 16)
                        sp.dma_start(shift[:], row_broadcast(m["ln1_b"][layer])).then_inc(tables_in, 16)
                        load(Tile(0, 0))
                        load(Tile(0, 1))
                with sp.Fori(0, TILES // 2 - 1) as i:
                    for n in range(2):
                        at = Tile(i, 2 + n)
                        sp.wait_ge(res_done, at.t + 1)
                        load(at)

            @block.gpsimd
            def _(pool):
                pool.memset(half[:], -0.5).then_inc(const, 1)
                pool.wait_ge(const, 1)
                with pool.Fori(0, TILES // 2) as i:
                    for u in range(2):
                        t = i * 2 + u
                        pool.wait_ge(var_ready, t + 1)
                        pool.tensor_tensor(mv[:, 3:4], mv[:, 2:3], half[:], ALU.pow).then_inc(rstd_ready, 1)

            @block.tensor
            def _(pe):
                def products(at, h, arriving):
                    if h == 0:
                        pe.wait_ge(a_low, at.t + 1)
                        pe.wait_ge(res_done, at.t + 1)
                    cols = slice(h * HALF, (h + 1) * HALF)
                    for k in range(KD):
                        if arriving:
                            pe.wait_ge(w_low, k + 1)
                        for n, (one, other) in enumerate(((ah, wh), (ah, wl), (al, wh))):
                            last = nc.tensor.matmul(y_ps[at.slot][:, cols], one[:, at.slot, k, :], other[:, k, cols],
                                                    start=(k == 0 and n == 0), stop=(k == KD - 1 and n == 2))
                    if h == 1:
                        last.then_inc(y_done, 1)

                def step(at, product, following, normed, routed):
                    before, old = at.next(-1), at.next(-2)
                    if product:
                        products(at, 0, not normed)
                    if routed:
                        pe.wait_ge(xT_ready, old.t + 1)
                        pe.wait_ge(prob_ready, old.t + 1)
                        for k in range(KD):
                            last = nc.tensor.matmul(r_ps[:, 0:EXPERTS], xT[:, k * P:(k + 1) * P], wr[:, k, :],
                                                    start=(k == 0), stop=(k == KD - 1))
                        last.then_inc(r_done, 1)
                    if product:
                        products(at, 1, False)
                    if normed:
                        pe.wait_ge(tables_in, 64)
                        pe.wait_ge(x1_ready, before.t + 1)
                        for k in range(KD):
                            last = nc.tensor.transpose(t_ps[:, k * P:(k + 1) * P], x1[:, before.slot, k * P:(k + 1) * P], ident[:])
                        last.then_inc(xT_done, 1)
                    if routed:
                        pe.wait_ge(prob_ready, old.t + 2)
                        pe.wait_ge(aff_ready, old.t + 1)
                        nc.tensor.transpose(rT_ps[0:EXPERTS, 0:P], prob[:], ident[:]).then_inc(rT_done, 1)

                tile_steps(pe.Fori(0, TILES // 2 - 2), step)

            @block.vector
            def _(v):
                s = Steps(v, dve)

                def low(a):
                    v.wait_ge(a_high, a.t + 1)
                    nc.vector.tensor_tensor(al[:, a.slot, :, :], cat[:, :, bass.ds(a.t * P, P)], ah[:, a.slot, :, :].bitcast(F32), ALU.subtract).then_inc(a_low, 1)

                def step(at, product, following, normed, routed):
                    new, old = at.next(-1), at.next(-2)
                    if normed:
                        v.wait_ge(y_done, new.t + 3)
                        v.wait_ge(a_in[new.slot], new.pair * 16 + 16)
                        nc.vector.scalar_tensor_tensor(row[:], x[:, new.slot, :], ALPHA, y_ps[new.slot][:], ALU.mult, ALU.add).then_inc(res_done, 1)
                        v.wait_ge(res_done, new.t + 3)
                        v.wait_ge(x1_out[new.slot], new.pair * 32 + 32)
                        v.wait_ge(xT_done, new.t + 1)
                        v.wait_ge(ax_ready, new.t + 1)
                        layer_norm_rows(nc, s, row[:], x1[:, new.slot, :], stats, mv, gain[:], shift[:], var_ready, rstd_ready, new.t).then_inc(x1_ready, 1)
                    if following:
                        low(at.next())
                    if routed:
                        v.wait_ge(r_done, old.t + 1)
                        nc.vector.tensor_reduce(pr[:, 0:1], r_ps[:, 0:EXPERTS], AX.X, ALU.max, negate=True).then_inc(neg_ready, 1)
                        v.wait_ge(exp_done, old.t + 1)
                        s.link(nc.vector.reciprocal(pr[:, 2:3], pr[:, 1:2]))
                        nc.vector.tensor_scalar(prob[:], prob[:], pr[:, 2:3], None, ALU.mult).then_inc(prob_ready, 1)

                v.sem_inc(res_done, 2)
                v.sem_inc(prob_ready, 1)
                for k in range(KD):
                    v.wait_ge(w_high, k + 1)
                    nc.vector.tensor_tensor(wl[:, k, :], raw[:, k % 2, :], wh[:, k, :].bitcast(F32), ALU.subtract).then_inc(w_low, 1)
                    if k == 0:
                        low(Tile(0, 0))
                v.wait_ge(tables_in, 64)
                tile_steps(s.loop(TILES // 2 - 2, 2 * (5 + 1)), step)

            @block.scalar
            def _(act):
                def high(a):
                    act.wait_ge(y_done, a.t + 1)
                    nc.scalar.activation(ah[:, a.slot, :, :], cat[:, :, bass.ds(a.t * P, P)], ACT.Copy).then_inc(a_high, 1)

                def step(at, product, following, normed, routed):
                    new, old = at.next(-1), at.next(-2)
                    if following:
                        high(at.next())
                    if normed:
                        act.wait_ge(x1_ready, new.t + 1)
                        act.wait_ge(x1_out[new.slot], new.pair * 32 + 32)
                        nc.scalar.activation(ax1[:, new.slot, :], x1[:, new.slot, :], ACT.Copy, scale=ALPHA).then_inc(ax_ready, 1)
                        act.dma_start(m["x1"][bass.ds(new.t * P, P), :], x1[:, new.slot, :]).then_inc(x1_out[new.slot], 16)
                        act.wait_ge(ax_ready, new.t + 3)
                        act.dma_start(m["acc"][bass.ds(new.t * P, P), :], ax1[:, new.slot, :]).then_inc(x1_out[new.slot], 16)
                    if routed:
                        act.wait_ge(neg_ready, old.t + 1)
                        act.wait_ge(rT_done, old.t + 1)
                        nc.scalar.activation(prob[:], r_ps[:, 0:EXPERTS], ACT.Exp, bias=pr[:, 0:1], accum_out=pr[:, 1:2]).then_inc(exp_done, 1)
                    if normed:
                        act.wait_ge(xT_done, new.t + 3)
                        nc.scalar.activation(xT[:], t_ps[:], ACT.Copy).then_inc(xT_ready, 1)
                    if routed:
                        act.wait_ge(rT_done, old.t + 2)
                        nc.scalar.activation(affinity[:, bass.ds(old.t * P, P)], rT_ps[0:EXPERTS, 0:P], ACT.Copy).then_inc(aff_ready, 1)

                act.sem_inc(xT_done, 2)
                act.sem_inc(y_done, 2)
                act.sem_inc(ax_ready, 2)
                act.sem_inc(aff_ready, 1)
                act.sem_inc(rT_done, 1)
                for u in range(2):
                    act.sem_inc(x1_out[u], 32)
                for k in range(KD):
                    act.wait_ge(w_in[k % 2], k // 2 * 32 + 32)
                    nc.scalar.activation(wh[:, k, :], raw[:, k % 2, :], ACT.Copy).then_inc(w_high, 1)
                    if k == 0:
                        high(Tile(0, 0))
                tile_steps(act.Fori(0, TILES // 2 - 2), step)
                for u in range(2):
                    act.wait_ge(x1_out[u], 32 * (TILES // 2) + 32)


def experts(c, m, layer, affinity):
    nc = c.nc
    R = PROMPT_ROW + EXPERTS
    N = SEQ[1]
    BEST = CAP[1]
    SC, PC = CAP[1], CAP[0]
    CHUNKS, PIECES = 6, 12
    RAW, SPLIT = 4, 4
    GU = KD
    with c.stage():
        ident = c.sb("ident", [P, P])
        gates, rows = c.sb("gates", [P, 2 * PROMPT_ROW]), c.sb("rows", [P, 2 * PROMPT_ROW], U32)
        left = c.sb("left", [R, 2, N])
        best, where, wheref = c.sb("best", [R, BEST]), c.sb("where", [R, BEST], U32), c.sb("wheref", [R, BEST])
        raw = c.sb("raw", [P, RAW, 4 * D])
        high, low = c.sb("high", [P, SPLIT, 2 * D], F32R), c.sb("low", [P, SPLIT, 2 * D], F32R)
        ids = c.sb("ids", [P, 2, 2], U32)
        gsel = c.sb("gsel", [P, 2, 2])
        xs, xp = [c.sb(f"xs{u}", [P, D]) for u in range(2)], [c.sb(f"xp{u}", [PC, D]) for u in range(2)]
        xT = c.sb("xT", [P, KD, 2, SLOTS], F32R)
        gate_up, h = c.sb("gate_up", [P, 2, 2, SLOTS]), c.sb("h", [P, SLOTS])
        hT = c.sb("hT", [P, KD, 2 * SLOTS], F32R)
        ys, yp = c.sb("ys", [P, D]), c.sb("yp", [PC, D])
        h_ps = [c.ps(f"h_ps{b}", 2 * HALF) for b in range(2)]
        y_ps, yp_ps = c.ps("y_ps", D), c.ps("yp_ps", D)
        t_ps = [yp_ps[:, 0:HALF], yp_ps[:, HALF:D]]
        loaded, zeroed, chosen, listed = (c.sem(n) for n in ("loaded", "zeroed", "chosen", "listed"))
        w_in = [c.sem(f"w_in{n}") for n in range(RAW)]
        x_in = [c.sem("x_in0"), c.sem("x_in1")]
        ids_ready, high_ready, low_ready, piece_done, turned, xh_ready, xT_ready, summed, silu_ready, h_ready, ys_ready, yp_ready, added, dve = (
            c.sem(n) for n in ("ids_ready", "high_ready", "low_ready", "piece_done", "turned", "xh_ready", "xT_ready", "summed", "silu_ready",
                               "h_ready", "ys_ready", "yp_ready", "added", "dve"))
        turn_done = c.sem("turn_done")
        still = c.sb("still", [P, 5])
        QUADS = KD // 2
        picks, gate_cols = rows[:].rearrange("p (g e) -> p g e", g=2), gates[:].rearrange("p (g e) -> p g e", g=2)

        def piece_view(n):
            slot = raw[:, n // 2 % RAW, :]
            if n % PIECES < GU:
                at = n % 2 * P
                return slot.rearrange("p (n k f) -> p n k f", n=2, k=KD)[:, :, :, at:at + P]
            return slot.rearrange("p (n k f) -> p n k f", n=2, k=2)[:, n % 2, :, :]

        def split_view(part, n):
            slot = part[:, n % SPLIT, :]
            if n % PIECES < GU:
                return slot.rearrange("p (n k f) -> p n k f", n=2, k=KD)
            return slot.rearrange("p (k f) -> p k f", k=2)

        with c.block() as block:

            @block.sync
            def _(sp):
                sp.dma_start(ident[:], m["ident"]).then_inc(loaded, 16)
                gate_up = [m[n].rearrange("l e (k p) f -> (l e) p k f", p=P) for n in ("moe_w_gate", "moe_w_up")]
                down = m["moe_w_down"].rearrange("l e (h k p) d -> (l e) p h k d", p=P, k=2)
                with sp.Fori(0, EXPERTS // 2) as i:
                    for u in range(2):
                        which = bass.ds(i * 2 + (u + layer * EXPERTS), 1)
                        for chunk in range(CHUNKS):
                            n = u * CHUNKS + chunk
                            sp.wait_ge(low_ready, i * (2 * PIECES) + 2 * n + 2)
                            for part in range(2):
                                if chunk < GU // 2:
                                    to = raw[:, n % RAW, part * 2 * D:(part + 1) * 2 * D].rearrange("p (o k f) -> p o k f", o=1, k=KD)
                                    src = gate_up[part][which, :, :, chunk * 2 * P:(chunk + 1) * 2 * P].rearrange("o p k f -> p o k f")
                                else:
                                    to = raw[:, n % RAW, part * 2 * D:(part + 1) * 2 * D].rearrange("p (o k d) -> p o k d", o=1, k=2)
                                    src = down[which, :, 2 * (chunk - GU // 2) + part, :, :].rearrange("o p k d -> p o k d")
                                sp.dma_start(to, src).then_inc(w_in[n % RAW], 16)

            @block.gpsimd
            def _(pool):
                def hold(at):
                    return pool.tensor_tensor(still[:, at:at + 1], still[:, 0:1], still[:, 0:1], ALU.add)

                def gather(u, e, at):
                    pool.wait_ge(ids_ready, e + 1)
                    pool.wait_ge(turned, e * QUADS + QUADS)
                    pool.wait_ge(turn_done, e + 1)
                    hold(at)
                    pool.indirect_dma_start(out=xs[u][:], out_offset=None, in_=m["x1"],
                                            in_offset=bass.IndirectOffsetOnAxis(ap=ids[:, u, 0:1], axis=0)).then_inc(x_in[u], 16)
                    pool.indirect_dma_start(out=xp[u][:], out_offset=None, in_=m["x1"],
                                            in_offset=bass.IndirectOffsetOnAxis(ap=ids[0:PC, u, 1:2], axis=0)).then_inc(x_in[u], 16)

                pool.sem_inc(turn_done, 2)
                pool.memset(still[:], 0.0).then_inc(zeroed, 1)
                pool.wait_ge(zeroed, 1)
                gather(0, 0, 4)
                with pool.Fori(0, EXPERTS // 2) as i:
                    for u in range(2):
                        e = i * 2 + u
                        gather(1 - u, e + 1, 1)
                        pool.wait_ge(ys_ready, e + 2)
                        pool.wait_ge(yp_ready, e + 2)
                        hold(2)
                        pool.indirect_dma_start(out=m["acc"], out_offset=bass.IndirectOffsetOnAxis(ap=ids[:, u, 0:1], axis=0),
                                                in_=ys[:], in_offset=None, compute_op=ALU.add).then_inc(added, 16)
                        pool.indirect_dma_start(out=m["acc"], out_offset=bass.IndirectOffsetOnAxis(ap=ids[0:PC, u, 1:2], axis=0),
                                                in_=yp[:], in_offset=None, compute_op=ALU.add).then_inc(added, 16)
                        pool.wait_ge(added, e * 32 + 32)
                        hold(3).then_inc(turn_done, 1)

            @block.tensor
            def _(pe):
                def turn(u, e, arrived, first):
                    pe.wait_ge(x_in[u], arrived)
                    pe.wait_ge(yp_ready, e + 1)
                    for q in range(QUADS):
                        bank = t_ps[q % 2]
                        pe.wait_ge(xT_ready, first + q)
                        for j in range(2):
                            k = q * 2 + j
                            nc.tensor.transpose(bank[:, j * SLOTS:j * SLOTS + SC], xs[u][:, k * P:(k + 1) * P], ident[:])
                            last = nc.tensor.transpose(bank[:, j * SLOTS + SC:(j + 1) * SLOTS], xp[u][:, k * P:(k + 1) * P], ident[0:PC, 0:PC])
                        last.then_inc(turned, 1)

                pe.sem_inc(piece_done, SPLIT)
                pe.sem_inc(turned, 2 * QUADS)
                pe.wait_ge(loaded, 16)
                pe.wait_ge(chosen, 1)
                nc.tensor.transpose(y_ps[:, 0:R], best[:], ident[0:R, 0:R])
                nc.tensor.transpose(y_ps[:, 64:64 + R], wheref[:], ident[0:R, 0:R]).then_inc(listed, 1)
                turn(0, 0, 32, 1)
                with pe.Fori(0, EXPERTS // 2) as i:
                    for u in range(2):
                        e = i * 2 + u
                        pe.wait_ge(xT_ready, e * QUADS + QUADS + 2)
                        for f in range(GU):
                            pe.wait_ge(low_ready, e * PIECES + f + 1 + 2 * RAW)
                            pe.wait_ge(summed, e * KD + f + 1)
                            wh, wl = split_view(high, f), split_view(low, f)
                            for n in range(2):
                                ps = h_ps[f % 2][:, n * HALF:n * HALF + 2 * SLOTS]
                                for k in range(KD - 1):
                                    nc.tensor.matmul(ps, wh[:, n, k, :], xT[:, k, :, :].rearrange("p s n -> p (s n)"), start=(k == 0), stop=False)
                                    nc.tensor.matmul(ps[:, 0:SLOTS], wl[:, n, k, :], xT[:, k, 0, :], start=False, stop=False)
                                k = KD - 1
                                nc.tensor.matmul(ps[:, 0:SLOTS], wl[:, n, k, :], xT[:, k, 0, :], start=False, stop=False)
                                last = nc.tensor.matmul(ps, wh[:, n, k, :], xT[:, k, :, :].rearrange("p s n -> p (s n)"), start=False, stop=True)
                            last.then_inc(piece_done, 1)
                        turn(1 - u, e, i * 32 + 32 + 32 * u, e * QUADS + QUADS + 1)
                        pe.wait_ge(ys_ready, e + 1)
                        for n in range(GU, PIECES):
                            pe.wait_ge(low_ready, e * PIECES + n + 1 + 2 * RAW)
                            wh, wl = split_view(high, n), split_view(low, n)
                            for j in range(2):
                                f = (n - GU) * 2 + j
                                pe.wait_ge(h_ready, e * KD + f + 1)
                                first, end = f == 0, f == KD - 1
                                for half in range(2):
                                    cols = slice(half * HALF, (half + 1) * HALF)
                                    nc.tensor.matmul(y_ps[:, cols], hT[:, f, 0:SC], wh[:, j, cols], start=first, stop=False)
                                    nc.tensor.matmul(y_ps[:, cols], hT[:, f, SC + 2 * PC:2 * SLOTS], wh[:, j, cols], start=False, stop=False)
                                    nc.tensor.matmul(y_ps[:, cols], hT[:, f, 0:SC], wl[:, j, cols], start=False, stop=end)

                                def both(half):
                                    cols = slice(half * HALF, (half + 1) * HALF)
                                    return nc.tensor.matmul(yp_ps[:, cols], hT[:, f, SC:SC + 2 * PC], wh[:, j, cols], start=first, stop=end)

                                def rest(half):
                                    cols = slice(half * HALF, (half + 1) * HALF)
                                    return nc.tensor.matmul(yp_ps[0:PC, cols], hT[:, f, SC:SLOTS], wl[:, j, cols], start=False, stop=False)

                                if first:
                                    pe.wait_ge(xT_ready, e * QUADS + 2 * QUADS + 2)
                                for half in range(2):
                                    if end:
                                        rest(half)
                                        last = both(half)
                                    else:
                                        both(half)
                                        last = rest(half)
                            last.then_inc(piece_done, 1)

            @block.scalar
            def _(act):
                def split(e, n):
                    chunk = n // 2
                    if n % 2 == 0:
                        i, u = e
                        at = u * CHUNKS + chunk
                        act.wait_ge(w_in[at % RAW], i * (2 * CHUNKS // RAW * 32) + (at // RAW * 32 + 32))
                    act.wait_ge(piece_done, (e[0] * 2 + e[1]) * PIECES + n + 1)
                    at = e[1] * PIECES + n
                    nc.scalar.activation(split_view(high, at), piece_view(at), ACT.Copy).then_inc(high_ready, 1)

                def turn(first):
                    for q in range(QUADS):
                        act.wait_ge(turned, first + q + 2 * QUADS + 1)
                        nc.scalar.activation(xT[:, 2 * q:2 * q + 2, 0, :], t_ps[q % 2][:, 0:2 * SLOTS].rearrange("p (k n) -> p k n", k=2), ACT.Copy)\
                            .then_inc(xh_ready, 1)

                act.sem_inc(ys_ready, 1)
                for n in range(SPLIT):
                    split((0, 0), n)
                turn(0)
                def pair(i, at_last):
                    for u in range(2):
                        e = i * 2 + u
                        for n in range(PIECES):
                            if n < GU:
                                act.wait_ge(summed, e * KD + n + 3)
                                gate = gate_up[:, n % 2, 0, :]
                                nc.scalar.activation(gate, gate, ACT.Silu).then_inc(silu_ready, 1)
                            if n == GU - 1:
                                turn(e * QUADS + QUADS)
                            if not (at_last and u == 1 and n + SPLIT >= PIECES):
                                split((i, u), n + SPLIT)
                        act.wait_ge(piece_done, e * PIECES + PIECES + SPLIT)
                        act.wait_ge(turn_done, e + 2)
                        nc.scalar.activation(ys[:], y_ps[:], ACT.Copy, scale=gsel[:, u, 0:1]).then_inc(ys_ready, 1)

                with act.Fori(0, EXPERTS // 2 - 1) as i:
                    pair(i, False)
                pair(EXPERTS // 2 - 1, True)

            @block.vector
            def _(v):
                s = Steps(v, dve)

                def pick(u, e):
                    v.wait_ge(turn_done, e + 1)
                    nc.vector.tensor_copy(gsel[:, u, :], gate_cols[:, :, bass.ds(e, 1)].rearrange("p g o -> p (g o)"))
                    nc.vector.tensor_copy(ids[:, u, :], picks[:, :, bass.ds(e, 1)].rearrange("p g o -> p (g o)")).then_inc(ids_ready, 1)

                def split(e, u, n):
                    v.wait_ge(high_ready, e * PIECES + n + 1)
                    at = u * PIECES + n
                    nc.vector.tensor_tensor(split_view(low, at), piece_view(at), split_view(high, at).bitcast(F32), ALU.subtract).then_inc(low_ready, 1)

                def turn(first):
                    for q in range(QUADS):
                        v.wait_ge(xh_ready, first + q + 1)
                        nc.vector.tensor_tensor(xT[:, 2 * q:2 * q + 2, 1, :], t_ps[q % 2][:, 0:2 * SLOTS].rearrange("p (k n) -> p k n", k=2),
                                                xT[:, 2 * q:2 * q + 2, 0, :].bitcast(F32), ALU.subtract).then_inc(xT_ready, 1)

                v.sem_inc(low_ready, 2 * RAW)
                v.sem_inc(xT_ready, 2)
                v.sem_inc(summed, 2)
                v.sem_inc(yp_ready, 1)
                s.add(nc.vector.memset(rows[:], 0))
                s.add(nc.vector.memset(gates[:], 0.0))
                s.link(nc.vector.memset(left[:], -1.0))
                s.add(nc.vector.tensor_copy(left[0:EXPERTS, 0, :], affinity[:, SEQ[0]:TOK]))
                s.link(nc.vector.tensor_copy(left[PROMPT_ROW:R, 0, 0:SEQ[0]], affinity[:, 0:SEQ[0]]))
                for r in range(BEST // 8):
                    now, eight = left[:, r % 2, :], slice(8 * r, 8 * r + 8)
                    s.link(nc.vector.max(out=best[:, eight], in_=now))
                    s.add(nc.vector.max_index(out=where[:, eight], in_max=best[:, eight], in_values=now))
                    if r + 1 < BEST // 8:
                        s.link(nc.vector.match_replace(out=left[:, (r + 1) % 2, :], in_to_replace=best[:, eight], in_values=now, imm_value=-2.0))
                s.settle()
                s.link(nc.vector.tensor_copy(wheref[:], where[:]))
                nc.vector.tensor_scalar(wheref[0:EXPERTS, :], wheref[0:EXPERTS, :], float(SEQ[0]), None, ALU.add).then_inc(chosen, 1)
                v.wait_ge(listed, 1)
                nc.vector.tensor_copy(gates[:, 0:R], y_ps[:, 0:R])
                s.link(nc.vector.tensor_copy(rows[:, 0:R], y_ps[:, 64:64 + R]))
                pick(0, 0)
                for n in range(SPLIT - 1):
                    split(0, 0, n)
                turn(0)
                def pair(i, at_last):
                    for u in range(2):
                        e = i * 2 + u
                        for n in range(PIECES):
                            if n < GU:
                                gate, up = gate_up[:, n % 2, 0, :], gate_up[:, n % 2, 1, :]
                                v.wait_ge(piece_done, e * PIECES + n + 1 + SPLIT)
                                nc.vector.tensor_reduce(gate_up[:, n % 2, :, :], h_ps[n % 2][:].rearrange("p (b n) -> p b n", b=2)[:, :, 0:2 * SLOTS]
                                                        .rearrange("p b (s n) -> p b n s", s=2), AX.X, ALU.add).then_inc(summed, 1)
                            if n == GU - 1:
                                turn(e * QUADS + QUADS)
                            if not (at_last and u == 1 and n + SPLIT - 1 >= PIECES):
                                split(e, u, n + SPLIT - 1)
                            if n < GU:
                                hf = h[:]
                                v.wait_ge(silu_ready, e * KD + n + 1)
                                s.link(nc.vector.tensor_tensor(hf, gate, up, ALU.mult))
                                s.link(nc.vector.tensor_copy(hT[:, n, 0:SLOTS], hf))
                                nc.vector.tensor_tensor(hT[:, n, SLOTS:SLOTS + PC], hf[:, SC:SLOTS], hT[:, n, SC:SLOTS].bitcast(F32), ALU.subtract)
                                nc.vector.tensor_tensor(hT[:, n, SLOTS + PC:2 * SLOTS], hf[:, 0:SC], hT[:, n, 0:SC].bitcast(F32), ALU.subtract).then_inc(h_ready, 1)
                            if n == GU // 2:
                                pick(1 - u, e + 1)
                        v.wait_ge(piece_done, e * PIECES + PIECES + SPLIT)
                        v.wait_ge(turn_done, e + 2)
                        s.link(nc.vector.tensor_copy(yp[:], yp_ps[PC:2 * PC, :]))
                        s.link(nc.vector.tensor_tensor(yp[:], yp[:], yp_ps[0:PC, :], ALU.add))
                        nc.vector.tensor_scalar(yp[:], yp[:], gsel[0:PC, u, 1:2], None, ALU.mult).then_inc(yp_ready, 1)

                with s.loop(EXPERTS // 2 - 1, 2 * (2 * KD + 2)) as i:
                    pair(i, False)
                pair(EXPERTS // 2 - 1, True)


def project_axial(c, m, keys, values):
    nc = c.nc
    QK = AX_Q + AX_KVD
    HEADS = QK // DH
    BATCH = 12
    QW = 2 * AX_Q
    with c.stage():
        w = c.sb("w_in", [P, KD, C_IN])
        ident = c.sb("ident", [P, P])
        gain, shift = c.sb("gain", [P, D]), c.sb("shift", [P, D])
        norm2 = c.sb("norm2", [P, 2, DH])
        r = c.sb("r", [P, 2, D])
        rope = c.sb("rope", [P, TILES, 2 * DH])
        x2 = c.sb("x2", [P, 2, D])
        stats, mv = c.sb("stats", [P, 12]), c.sb("mv", [P, 4])
        half = c.sb("minus_half", [P, HEADS])
        ms = c.sb("ms", [P, 2, HEADS])
        xT = c.sb("xT", [P, D])
        qk = c.sb("qk", [P, QK])
        parts = c.sb("parts", [P, QW + 4 * AX_KVD], F32R)
        ra, rb = c.sb("ra", [P, HEADS, DH]), c.sb("rb", [P, HEADS, DH])
        qT = c.sb("qT", [P, 2, QW], F32R)
        xT_ps, qkv_ps, qkT_ps = c.ps("xT_ps", D), c.ps("qkv_ps", C_IN), c.ps("qkT_ps", BATCH * P)
        tables_in, rope_in, w_in, r_in, x2_out, q_out = c.sem("tables_in"), c.sem("rope_in"), [c.sem(f"w_in{k}") for k in range(KD)], [c.sem("r_in0"), c.sem("r_in1")], [c.sem("x2_out0"), c.sem("x2_out1")], [c.sem("q_out0"), c.sem("q_out1")]
        const, dve, var_ready, rstd_ready, x2_ready, xT_done, xT_ready, qkv_done, copied, squared, ms_ready, rms_ready = (
            c.sem(n) for n in ("const", "dve", "var_ready", "rstd_ready", "x2_ready", "xT_done", "xT_ready", "qkv_done", "copied",
                               "squared", "ms_ready", "rms_ready"))
        rotated, high_ready, parts_ready, qkT_done, qT_ready = (
            c.sem(n) for n in ("rotated", "high_ready", "parts_ready", "qkT_done", "qT_ready"))
        turns = TILES // 2
        LAST = TILES - 1
        q_parts = parts[:, 0:QW].rearrange("p (h s d) -> p h s d", s=2, d=DH)
        k_parts = parts[:, QW:].rearrange("p (h s d) -> p h s d", s=4, d=DH)

        with c.block() as block:

            @block.sync
            def _(sp):
                sp.dma_start(gain[:], row_broadcast(m["ln2_g"][0])).then_inc(tables_in, 16)
                sp.dma_start(shift[:], row_broadcast(m["ln2_b"][0])).then_inc(tables_in, 16)
                sp.dma_start(norm2[:, 0, :], row_broadcast(m["c_q_norm"][0])).then_inc(tables_in, 16)
                sp.dma_start(norm2[:, 1, :], row_broadcast(m["c_k_norm"][0])).then_inc(tables_in, 16)
                sp.dma_start(ident[:], m["ident"]).then_inc(tables_in, 16)

                def load(a):
                    sp.dma_start(r[:, a.slot, :], m["acc"][bass.ds(a.t * P, P), :]).then_inc(r_in[a.slot], 16)

                load(Tile(0, 0))
                load(Tile(0, 1))
                sp.dma_start(rope[:], m["rope_c"].rearrange("(t p) n -> p t n", p=P)).then_inc(rope_in, 16)
                for k in range(KD):
                    sp.dma_start(w[:, k, :], m["c_w_in"][0][k * P:(k + 1) * P, :]).then_inc(w_in[k], 16)
                with sp.Fori(0, turns - 1) as i:
                    for n in range(2):
                        a = Tile(i, 2 + n)
                        sp.wait_ge(x2_ready, a.t + 1)
                        load(a)

            @block.gpsimd
            def _(pool):
                pool.memset(half[:], -0.5).then_inc(const, 1)
                pool.wait_ge(const, 1)

                def layer_norm_root(t):
                    pool.wait_ge(var_ready, t + 1)
                    pool.tensor_tensor(mv[:, 3:4], mv[:, 2:3], half[:, 0:1], ALU.pow).then_inc(rstd_ready, 1)

                def head_norm_root(t):
                    pool.wait_ge(ms_ready, t + 1)
                    pool.tensor_tensor(ms[:, 1, :], ms[:, 0, :], half[:], ALU.pow).then_inc(rms_ready, 1)

                layer_norm_root(0)
                layer_norm_root(1)
                with pool.Fori(0, TILES - 2) as t:
                    layer_norm_root(t + 2)
                    head_norm_root(t)
                head_norm_root(TILES - 2)
                head_norm_root(TILES - 1)

            @block.tensor
            def _(pe):
                def turn_x(a):
                    pe.wait_ge(x2_ready, a.t + 3)
                    for k in range(KD):
                        last = nc.tensor.transpose(xT_ps[:, k * P:(k + 1) * P], x2[:, a.slot, k * P:(k + 1) * P], ident[:])
                    last.then_inc(xT_done, 1)

                def turn_qk(a, batch):
                    if batch == 0:
                        pe.wait_ge(parts_ready, a.t + 2)
                    pe.wait_ge(qT_ready, a.t * 2 + batch + 1)
                    for j in range(BATCH):
                        at = (batch * BATCH + j) * P
                        last = nc.tensor.transpose(qkT_ps[:, j * P:(j + 1) * P], parts[:, at:at + P].bitcast(F32), ident[:])
                    last.then_inc(qkT_done, 1)

                def step(a, products, following, rotary, old):
                    if old:
                        turn_qk(a.next(-2), 0)
                    for n in range(C_IN // HALF):
                        if products:
                            if n == 0:
                                pe.wait_ge(xT_ready, a.t + 1)
                                pe.wait_ge(copied, a.t + 1)
                            for k in range(KD):
                                if not rotary:
                                    pe.wait_ge(w_in[k], 16)
                                last = nc.tensor.matmul(qkv_ps[:, n * HALF:(n + 1) * HALF], xT[:, k * P:(k + 1) * P],
                                                        w[:, k, n * HALF:(n + 1) * HALF], start=(k == 0), stop=(k == KD - 1))
                            if n == C_IN // HALF - 1:
                                last.then_inc(qkv_done, 1)
                        if old and n == 0:
                            turn_qk(a.next(-2), 1)
                    if following:
                        turn_x(a.next())

                pe.wait_ge(tables_in, 80)
                turn_x(Tile(0, 0))
                tile_steps(pe.Fori(0, turns - 2), step)

            @block.scalar
            def _(act):
                def copy_x(a):
                    act.wait_ge(x2_ready, a.t + 3)
                    act.dma_start(m["x2"][bass.ds(a.t * P, P), :], x2[:, a.slot, :]).then_inc(x2_out[a.slot], 16)
                    act.wait_ge(xT_done, a.t + 3)
                    nc.scalar.activation(xT[:], xT_ps[:], ACT.Copy).then_inc(xT_ready, 1)

                def copy_qkv(a):
                    act.wait_ge(qkv_done, a.t + 1)
                    act.wait_ge(parts_ready, a.t + 1)
                    nc.scalar.activation(values[:, bass.ds(a.t, 1), :], qkv_ps[:, QK:C_IN].rearrange("p (o n) -> p o n", o=1), ACT.Copy)
                    nc.scalar.activation(qk[:], qkv_ps[:, 0:QK], ACT.Copy).then_inc(copied, 1)

                def square(a):
                    act.wait_ge(copied, a.t + 2)
                    nc.scalar.activation(ra[:].rearrange("p h d -> p (h d)"), qk[:], ACT.Square).then_inc(squared, 1)

                def high(a):
                    act.wait_ge(rotated, a.t + 1)
                    act.wait_ge(qkT_done, a.t * 2 + 1)
                    heads = qk[:].rearrange("p (h d) -> p h d", d=DH)
                    nc.scalar.activation(q_parts[:, :, 0, :], heads[:, 0:AX_H, :], ACT.Copy)
                    nc.scalar.activation(k_parts[:, :, 0, :], heads[:, AX_H:HEADS, :], ACT.Copy)
                    nc.scalar.activation(k_parts[:, :, 1, :], heads[:, AX_H:HEADS, :], ACT.Copy).then_inc(high_ready, 1)

                def copy_q(a, batch):
                    lo, hi = ((0, BATCH * P), (BATCH * P, QW))[batch]
                    act.wait_ge(qkT_done, a.t * 2 + batch + 2)
                    if batch == 0:
                        act.wait_ge(q_out[a.slot], a.pair * 16 + 16)
                    last = nc.scalar.activation(qT[:, a.slot, lo:hi], qkT_ps[:, 0:hi - lo], ACT.Copy, scale=SCALE)
                    if batch == 1:
                        last = nc.scalar.activation(keys[:, :, bass.ds(a.t * P, P)], qkT_ps[:, hi - lo:].rearrange("p (j n) -> p j n", j=2 * AX_KV), ACT.Copy)
                    last.then_inc(qT_ready, 1)
                    if batch == 1:
                        act.wait_ge(qT_ready, a.t * 2 + 3)
                        act.dma_start(m["qT_parts"][bass.ds(a.t * P, P), :], qT[:, a.slot, :].bitcast(F32)).then_inc(q_out[a.slot], 16)

                def step(a, products, following, rotary, old):
                    if old:
                        copy_q(a.next(-2), 0)
                        copy_q(a.next(-2), 1)
                    if rotary:
                        high(a.next(-1))
                    if products:
                        copy_qkv(a)
                    if following:
                        copy_x(a.next())
                    if products:
                        square(a)

                act.sem_inc(copied, 1)
                act.sem_inc(qT_ready, 1)
                act.sem_inc(qkT_done, 1)
                for u in range(2):
                    act.sem_inc(x2_out[u], 16)
                    act.sem_inc(q_out[u], 16)
                copy_x(Tile(0, 0))
                tile_steps(act.Fori(0, turns - 2), step)
                for u in range(2):
                    act.wait_ge(x2_out[u], 16 * turns + 16)
                    act.wait_ge(q_out[u], 16 * turns + 16)

            @block.vector
            def _(v):
                s = Steps(v, dve)
                heads = qk[:].rearrange("p (h d) -> p h d", d=DH)

                def norm(a):
                    v.wait_ge(r_in[a.slot], a.pair * 16 + 16)
                    v.wait_ge(x2_out[a.slot], a.pair * 16 + 16)
                    v.wait_ge(xT_done, a.t + 1)
                    layer_norm_rows(nc, s, r[:, a.slot, :], x2[:, a.slot, :], stats, mv, gain[:], shift[:], var_ready, rstd_ready, a.t).then_inc(x2_ready, 1)

                def rotate(a):
                    v.wait_ge(squared, a.t + 1)
                    v.wait_ge(rope_in, 16)
                    s.link(nc.vector.tensor_reduce(ms[:, 0, :], ra[:], AX.X, ALU.add))
                    nc.vector.tensor_scalar(ms[:, 0, :], ms[:, 0, :], 1.0 / DH, RMS_EPS, ALU.mult, ALU.add).then_inc(ms_ready, 1)
                    v.wait_ge(rms_ready, a.t + 1)
                    s.link(nc.vector.tensor_tensor(heads, heads, ms[:, 1, :].rearrange("p (h o) -> p h o", o=1).to_broadcast([P, HEADS, DH]), ALU.mult))
                    for n, lo, hi in ((0, 0, AX_H), (1, AX_H, HEADS)):
                        s.add(nc.vector.tensor_tensor(heads[:, lo:hi, :], heads[:, lo:hi, :], norm2[:, n:n + 1, :].to_broadcast([P, hi - lo, DH]), ALU.mult))
                    s.settle()
                    cos = rope[:, bass.ds(a.t, 1), 0:DH].to_broadcast([P, HEADS, DH])
                    s.add(nc.vector.tensor_tensor(ra[:], heads, cos, ALU.mult))
                    for axis in range(2):
                        lo = axis * DH // 2
                        mid, hi = lo + DH // 4, lo + DH // 2
                        for b, e, x, y in ((lo, mid, mid, hi), (mid, hi, lo, mid)):
                            sin = rope[:, bass.ds(a.t, 1), DH + b:DH + e].to_broadcast([P, HEADS, e - b])
                            s.add(nc.vector.tensor_tensor(rb[:, :, b:e], heads[:, :, x:y], sin, ALU.mult))
                    s.settle()
                    nc.vector.tensor_tensor(heads, ra[:], rb[:], ALU.add).then_inc(rotated, 1)
                    v.wait_ge(high_ready, a.t + 1)
                    nc.vector.tensor_tensor(q_parts[:, :, 1, :], heads[:, 0:AX_H, :], q_parts[:, :, 0, :].bitcast(F32), ALU.subtract)
                    for n in range(2):
                        last = nc.vector.tensor_tensor(k_parts[:, :, 2 + n, :], heads[:, AX_H:HEADS, :], k_parts[:, :, 0, :].bitcast(F32), ALU.subtract)
                    last.then_inc(parts_ready, 1)

                def step(a, products, following, rotary, old):
                    if following:
                        norm(a.next())
                    if rotary:
                        rotate(a.next(-1))

                v.wait_ge(tables_in, 80)
                v.sem_inc(x2_ready, 2)
                v.sem_inc(xT_done, 2)
                v.sem_inc(parts_ready, 1)
                norm(Tile(0, 0))
                tile_steps(s.loop(turns - 2, 2 * (5 + 9)), step)


def axial_attention(c, m, keys, values, cat):
    nc = c.nc
    SET = AX_H // 2
    SHARE = SET // 2
    AHEAD = 2
    NB = 4
    with c.stage():
        ident = c.sb("ident", [P, P])
        q = c.sb("q", [P, 2, SET * P], F32R)
        p = c.sb("p", [P, NB, SEQ[1]])
        pT = c.sb("pT", [P, 2, SEQ[1] // P, SET, P])
        col = c.sb("col", [P, NB, 4])
        s_ps, t_ps, o_ps = [c.ps("s_ps0", SEQ[1]), c.ps("s_ps1", SEQ[1])], c.ps("t_ps", SEQ[1]), [c.ps("o_ps0", HALF), c.ps("o_ps1", HALF)]
        loaded, q_in = c.sem("loaded"), [c.sem("q_in0"), c.sem("q_in1")]
        scores, top_ready, expd, inverse, p_ready, pT_done, pT_ready, pv_done, o_out = (
            c.sem(n) for n in ("scores", "top_ready", "expd", "inverse", "p_ready", "pT_done", "pT_ready", "pv_done", "o_out"))

        def schedule(eng, g, run):
            first, tiles = GROUP_FIRST[g], GROUP_TILES[g]
            run(first, 0, 0, False)
            run(first, 1, 1, False)
            with eng.Fori(0, tiles - 2) as i:
                run(i + (first + 1), 0, 2, False)
                run(i + (first + 1), 1, 2, False)
            run(first + tiles - 1, 0, 2, False)
            run(first + tiles - 1, 1, 2, True)

        def set_before(tile, side):
            return (tile, 0) if side == 1 else (tile - 1, 1)

        def number(tile, side, n=0):
            return tile * AX_H + (side * SET + n)

        with c.block() as block:

            @block.sync
            def _(sp):
                sp.dma_start(ident[:], m["ident"]).then_inc(loaded, 16)
                with sp.Fori(0, TILES) as t:
                    for side in range(2):
                        sp.wait_ge(scores, number(t, side, SET))
                        sp.dma_start(q[:, side, :].bitcast(F32), m["qT_parts"][bass.ds(t * P, P), side * SET * P:(side + 1) * SET * P]).then_inc(q_in[side], 16)

            @block.tensor
            def _(pe):
                pe.sem_inc(scores, 2 * SET)
                pe.sem_inc(pT_done, NB)
                pe.sem_inc(pv_done, 2)
                pe.wait_ge(loaded, 16)
                for g in range(len(SEQ)):
                    nk, first = SEQ[g], GROUP_FIRST[g]

                    def qk(tile, side, n):
                        if n >= SET:
                            tile, side, n = (tile, 1, n - SET) if side == 0 else (tile + 1, 0, n - SET)
                        if n == 0:
                            pe.wait_ge(q_in[side], tile * 16 + 16)
                        pe.wait_ge(expd, number(tile, side, n + 1))
                        for b in range(nk // HALF):
                            at = first * P + b * HALF
                            for part in range(2):
                                last = nc.tensor.matmul(s_ps[n % 2][:, b * HALF:(b + 1) * HALF], q[:, side, n * P:(n + 1) * P],
                                                        keys[:, 2 * (2 * side + n // SHARE) + part, at:at + HALF], start=(part == 0), stop=(part == 1))
                        last.then_inc(scores, 1)

                    def turn(tile, side, n):
                        pe.wait_ge(p_ready, number(tile, side, n + 1))
                        pe.wait_ge(pT_ready, number(tile, side, n + 1))
                        for k in range(nk // P):
                            last = nc.tensor.transpose(t_ps[:, k * P:(k + 1) * P], p[:, n % NB, k * P:(k + 1) * P], ident[:])
                        last.then_inc(pT_done, 1)

                    def pv(tile, side, k):
                        if k == 0:
                            pe.wait_ge(o_out, tile * 2 + side + 1)
                        for kv in range(2):
                            last = nc.tensor.matmul(o_ps[side][DH * kv:DH * (kv + 1), :], values[:, first + k, (2 * side + kv) * DH:(2 * side + kv + 1) * DH],
                                                    pT[:, side, k, SHARE * kv:SHARE * (kv + 1), :].rearrange("p h n -> p (h n)"),
                                                    start=(k == 0), stop=(k == nk // P - 1))
                        if k == nk // P - 1:
                            last.then_inc(pv_done, 1)

                    def run(tile, side, before, at_last):
                        for n in range(SET):
                            if not (at_last and n + AHEAD >= SET):
                                qk(tile, side, n + AHEAD)
                            turn(tile, side, n)
                            if before and n < nk // P:
                                pv(*set_before(tile, side), n)

                    for n in range(AHEAD):
                        qk(first, 0, n)
                    schedule(pe, g, run)
                    pe.wait_ge(pT_ready, number(first + GROUP_TILES[g], 0, 1))
                    for k in range(nk // P):
                        pv(first + GROUP_TILES[g] - 1, 1, k)

            @block.vector
            def _(v):
                v.sem_inc(pT_ready, 1)
                for g in range(len(SEQ)):
                    nk, first = SEQ[g], GROUP_FIRST[g]

                    def top(tile, side, n):
                        v.wait_ge(scores, number(tile, side, n + 1 + 2 * SET))
                        nc.vector.tensor_reduce(col[:, n % NB, 0:1], s_ps[n % 2][:, 0:nk], AX.X, ALU.max, negate=True).then_inc(top_ready, 1)

                    def invert(tile, side, n):
                        v.wait_ge(expd, number(tile, side, n + 3))
                        nc.vector.reciprocal(col[:, n % NB, 2:3], col[:, n % NB, 1:2]).then_inc(inverse, 1)

                    def copy(tile, side, n):
                        v.wait_ge(pT_done, number(tile, side, n + 1 + NB))
                        if n == 0:
                            v.wait_ge(pv_done, tile * 2 + side + 1)
                        nc.vector.tensor_copy(pT[:, side, 0:nk // P, n, :], t_ps[:, 0:nk].rearrange("p (k n) -> p k n", k=nk // P)).then_inc(pT_ready, 1)

                    def run(tile, side, before, at_last):
                        for n in range(SET):
                            top(tile, side, n)
                            if n >= AHEAD:
                                copy(tile, side, n - AHEAD)
                            elif before:
                                copy(*set_before(tile, side), n - AHEAD + SET)
                            invert(tile, side, n)
                        if at_last:
                            for n in range(SET - AHEAD, SET):
                                copy(tile, side, n)

                    schedule(v, g, run)

            @block.scalar
            def _(act):
                act.sem_inc(expd, 2)
                act.sem_inc(o_out, 2)
                for g in range(len(SEQ)):
                    nk, first = SEQ[g], GROUP_FIRST[g]

                    def exps(tile, side, n):
                        act.wait_ge(top_ready, number(tile, side, n + 1))
                        act.wait_ge(pT_done, number(tile, side, n + 1))
                        nc.scalar.activation(p[:, n % NB, 0:nk], s_ps[n % 2][:, 0:nk], ACT.Exp, bias=col[:, n % NB, 0:1],
                                             accum_out=col[:, n % NB, 1:2]).then_inc(expd, 1)

                    def norm(tile, side, n):
                        act.wait_ge(inverse, number(tile, side, n + 1))
                        nc.scalar.activation(p[:, n % NB, 0:nk], p[:, n % NB, 0:nk], ACT.Copy, scale=col[:, n % NB, 2:3]).then_inc(p_ready, 1)

                    def out(tile, side):
                        act.wait_ge(pv_done, tile * 2 + side + 3)
                        nc.scalar.activation(cat[:, SHARE * side:SHARE * (side + 1), bass.ds(tile * P, P)],
                                             o_ps[side][:].rearrange("p (j n) -> p j n", j=SHARE), ACT.Copy).then_inc(o_out, 1)

                    def run(tile, side, before, at_last):
                        for n in range(SET):
                            exps(tile, side, n)
                            norm(tile, side, n)
                            if n == AHEAD and before == 2:
                                out(tile - 1, side)

                    schedule(act, g, run)
                    for side in range(2):
                        out(first + GROUP_TILES[g] - 1, side)


def final_norm(c, m):
    nc = c.nc
    RING = 4
    with c.stage():
        gain, shift = c.sb("gain", [P, D]), c.sb("shift", [P, D])
        r, y = c.sb("r", [P, RING, D]), c.sb("y", [P, RING, D])
        stats, mv, half = c.sb("stats", [P, 12]), c.sb("mv", [P, 4]), c.sb("minus_half", [P, 1])
        loaded, r_in, y_out = c.sem("loaded"), [c.sem(f"r_in{u}") for u in range(RING)], [c.sem(f"y_out{u}") for u in range(RING)]
        dve, var_ready, rstd_ready, gained, y_ready, const = (c.sem(n) for n in ("dve", "var_ready", "rstd_ready", "gained", "y_ready", "const"))
        turns = TILES // RING
        with c.block() as block:

            @block.sync
            def _(sp):
                sp.dma_start(gain[:], row_broadcast(m["ln2_g"][1])).then_inc(loaded, 16)
                sp.dma_start(shift[:], row_broadcast(m["ln2_b"][1])).then_inc(loaded, 16)
                sp.sem_inc(gained, RING)
                with sp.Fori(0, turns) as i:
                    for u in range(RING):
                        sp.wait_ge(gained, i * RING + u + 1)
                        sp.dma_start(r[:, u, :], m["acc"][bass.ds((i * RING + u) * P, P), :]).then_inc(r_in[u], 16)

            @block.gpsimd
            def _(pool):
                pool.memset(half[:], -0.5).then_inc(const, 1)
                pool.wait_ge(const, 1)

                def root(t):
                    pool.wait_ge(var_ready, t + 1)
                    pool.tensor_tensor(mv[:, 3:4], mv[:, 2:3], half[:], ALU.pow).then_inc(rstd_ready, 1)

                def add(t, u):
                    pool.wait_ge(gained, t + 1 + RING)
                    pool.tensor_tensor(y[:, u, :], y[:, u, :], shift[:], ALU.add).then_inc(y_ready, 1)

                root(0)
                with pool.Fori(0, turns - 1) as i:
                    for u in range(RING):
                        root(i * RING + (u + 1))
                        add(i * RING + u, u)
                for t in range(TILES - RING, TILES):
                    if t + 1 < TILES:
                        root(t + 1)
                    add(t, t % RING)

            @block.vector
            def _(v):
                s = Steps(v, dve)
                v.wait_ge(loaded, 32)
                with s.loop(turns, RING * 4) as i:
                    for u in range(RING):
                        t = i * RING + u
                        v.wait_ge(r_in[u], i * 16 + 16)
                        v.wait_ge(y_out[u], i * 16 + 16)
                        layer_norm_rows(nc, s, r[:, u, :], y[:, u, :], stats, mv, gain[:], None, var_ready, rstd_ready, t).then_inc(gained, 1)

            @block.scalar
            def _(act):
                for u in range(RING):
                    act.sem_inc(y_out[u], 16)
                with act.Fori(0, turns) as i:
                    for u in range(RING):
                        act.wait_ge(y_ready, i * RING + u + 1)
                        act.dma_start(m["y"][bass.ds((i * RING + u) * P, P), :], y[:, u, :]).then_inc(y_out[u], 16)
                for u in range(RING):
                    act.wait_ge(y_out[u], 16 * turns + 16)


def trunk(nc, m):
    m = dict(m)
    for name in ("x1", "x2", "acc", "qT"):
        m[name] = nc.dram_tensor(f"rows_{name}", (TOK, D), F32).ap()
    m["qT_parts"] = nc.dram_tensor("rows_qT_parts", (TOK, 2 * AX_Q), F32).ap()
    c = Core(nc)
    with c.stage():
        affinity = c.sb("affinity", [EXPERTS, TOK])
        with c.stage():
            cat = c.sb("cat", [P, KD, TOK])
            with c.stage():
                keys, values = c.sb("keys", [P, 2 * WIN_KV, TOK + 2 * P]), c.sb("values", [P, TILES + 2, WIN_KVD])
                glu = c.sb("glu", [P, CT, TOK])
                project_conv_window(c, m, glu, keys, values)
                conv = c.sb("conv", [P, CT, TOK])
                window_and_taps(c, m, keys, values, glu, conv, cat)
                norm_channels(c, m, conv, cat)
            spare = c.sb("spare", [P, (KD + 4) * D], F32R)
            project_out(c, m, 0, m["ab_w_out"][0], m["x"], cat, affinity, spare[:])
        experts(c, m, 0, affinity)
        with c.stage():
            keys, values = c.sb("keys", [P, 2 * AX_KV, TOK], F32R), c.sb("values", [P, TILES, AX_KVD])
            project_axial(c, m, keys, values)
            cat = c.sb("cat", [P, KD, TOK])
            axial_attention(c, m, keys, values, cat)
            project_out(c, m, 1, m["c_w_out"][0], m["x2"], cat, affinity, keys[:].rearrange("p k n -> p (k n)"))
        experts(c, m, 1, affinity)
        final_norm(c, m)


def host_arrays(inputs):
    f32 = np.float32
    a = {n: np.ascontiguousarray(inputs[n]) for n in
         ("ab_w_in", "ab_sink", "ab_w_out", "c_w_in", "c_q_norm", "c_k_norm", "c_w_out", "ln1_g", "ln1_b",
          "moe_router", "moe_w_gate", "moe_w_up", "moe_w_down", "ln2_g", "ln2_b")}
    a["x"] = np.concatenate([np.asarray(inputs["x_prompt"]).reshape(-1, D), np.asarray(inputs["x_sample"]).reshape(-1, D)])
    a["conv_w"] = np.ascontiguousarray(np.asarray(inputs["ab_conv_w"])[0].reshape(TAPS, CT, P).transpose(2, 1, 0))
    for n, name in (("conv_b", "ab_conv_b"), ("conv_g", "ab_conv_ln_g"), ("conv_beta", "ab_conv_ln_b")):
        a[n] = np.ascontiguousarray(np.asarray(inputs[name])[0].reshape(CT, P).T)
    a["ident"] = np.eye(P, dtype=f32)
    pos = np.concatenate([np.arange(n) for n in SEQ])

    def angles(at, dim, theta):
        inv = f32(theta) ** (-np.arange(0, dim, 2, dtype=f32) / f32(dim))
        return at.astype(f32)[:, None] * inv[None, :]

    def table(*ang):
        cos = np.concatenate([np.concatenate([np.cos(x), np.cos(x)], 1) for x in ang], 1)
        sin = np.concatenate([np.concatenate([-np.sin(x), np.sin(x)], 1) for x in ang], 1)
        return np.concatenate([cos, sin], 1).astype(f32)

    a["rope_b"] = table(angles(pos, ROT, 500000.0))
    a["rope_c"] = table(angles(pos // GRID_W, DH // 2, 10000.0), angles(pos % GRID_W, DH // 2, 10000.0))
    mask = np.zeros((TILES, P, 3 * P), f32)
    for g, n in enumerate(SEQ):
        for b in range(n // P):
            qpos = b * P + np.arange(P)[:, None]
            kpos = (b - 1) * P + np.arange(3 * P)[None, :]
            mask[GROUP_FIRST[g] + b] = np.where((np.abs(kpos - qpos) <= P) & (kpos >= 0) & (kpos < n), 0.0, MASKED)
    a["mask"] = mask.reshape(TILES * P, 3 * P)
    return a


def kernel(**inputs):
    import concourse.bacc as bacc
    from concourse.bass_utils import run_bass_kernel_spmd

    nc = bacc.Bacc("TRN2", target_bir_lowering=False, num_devices=1)
    arrays = host_arrays(inputs)
    m = {n: nc.dram_tensor(n, a.shape, mybir.dt.from_np(a.dtype), kind="ExternalInput").ap() for n, a in arrays.items()}
    m["y"] = nc.dram_tensor("y", (TOK, D), F32, kind="ExternalOutput").ap()
    trunk(nc, m)
    y = run_bass_kernel_spmd(nc, [arrays], core_ids=[0]).results[0]["y"]
    return y[:SEQ[0]].reshape(1, SEQ[0], D), y[SEQ[0]:].reshape(1, SEQ[1], D)
```
